# Optimizing a Trainium2 kernel written in Bass

```python
import jax, jax.numpy as jnp
from jax import lax
import numpy as np

D_MODEL = 1024
BATCH = 1
SEQ = 256
DEPTH = 2

CTX_LEN = 256
GRID_W = 64
N_MIX = 2
EPS = 1e-6

MLA_HEADS = 8
MLA_Q_LORA = 256
MLA_KV_LORA = 128
MLA_NOPE = 128
MLA_ROPE = 64
MLA_V = 128
MLA_QK = MLA_NOPE + MLA_ROPE
ROPE_BASE = 10000.0
Q_BLOCK = 128

RG_WIDTH = D_MODEL
RG_BLOCKS = 4
RG_BLOCK = RG_WIDTH // RG_BLOCKS
RG_CONV = 4
RG_CONV_LEFT = 2
RG_C = 8.0

FFN_HIDDEN = 2816
N_EXPERTS = 8
TOP_K = 2
EXPERT_HIDDEN = 3584

kernel_name = 'hybrid_mla_rglru_moe_dit'

def rms_norm(x, g):
    xf = x.astype(jnp.float32)
    y = xf * lax.rsqrt(jnp.mean(xf * xf, axis=-1, keepdims=True) + EPS)
    return (y * g.astype(jnp.float32)).astype(x.dtype)

def modulate(h, shift, scale):
    return h * (1 + scale) + shift

def ada_mod(cvec, w, b):
    return jnp.split(jax.nn.silu(cvec) @ w + b, 6, axis=-1)

def axial_rope(n_tok):
    rows = n_tok // GRID_W
    row = jnp.repeat(jnp.arange(rows, dtype=jnp.float32), GRID_W)
    col = jnp.tile(jnp.arange(GRID_W, dtype=jnp.float32), rows)
    n_freq = MLA_ROPE // 4
    inv = ROPE_BASE ** (-jnp.arange(n_freq, dtype=jnp.float32) / n_freq)
    ang = jnp.concatenate([row[:, None] * inv, col[:, None] * inv], axis=-1)
    return jnp.cos(ang), jnp.sin(ang)

def apply_rope(x, cos, sin):
    half = MLA_ROPE // 2
    c = cos[None, :, None, :].astype(x.dtype)
    s = sin[None, :, None, :].astype(x.dtype)
    x1, x2 = x[..., :half], x[..., half:]
    return jnp.concatenate([x1 * c - x2 * s, x2 * c + x1 * s], axis=-1)

def mla_q(h, w_dq, g_q, w_uq, g_qn, rope):
    b, n, _ = h.shape
    q = (rms_norm(h @ w_dq, g_q) @ w_uq).reshape(b, n, MLA_HEADS, MLA_QK)
    q = rms_norm(q, g_qn)
    if rope is not None:
        q = jnp.concatenate([q[..., :MLA_NOPE], apply_rope(q[..., MLA_NOPE:], *rope)], axis=-1)
    return q

def mla_kv(h, w_dkv, g_kv, w_ukv, g_kn, rope):
    b, n, _ = h.shape
    kv_a = h @ w_dkv
    c_kv = rms_norm(kv_a[..., :MLA_KV_LORA], g_kv)
    k_pe = kv_a[..., MLA_KV_LORA:]
    kv = (c_kv @ w_ukv).reshape(b, n, MLA_HEADS, MLA_NOPE + MLA_V)
    k = jnp.concatenate([kv[..., :MLA_NOPE],
                         jnp.broadcast_to(k_pe[:, :, None, :], (b, n, MLA_HEADS, MLA_ROPE))], axis=-1)
    k = rms_norm(k, g_kn)
    if rope is not None:
        k = jnp.concatenate([k[..., :MLA_NOPE], apply_rope(k[..., MLA_NOPE:], *rope)], axis=-1)
    return k, kv[..., MLA_NOPE:]

def attend(q, k, v):
    s = jnp.einsum('bqhd,bkhd->bhqk', q, k, preferred_element_type=jnp.float32) * (MLA_QK ** -0.5)
    p = jax.nn.softmax(s, axis=-1).astype(v.dtype)
    return jnp.einsum('bhqk,bkhd->bqhd', p, v)

def mla_mixer(hl, hc, w_dq, g_q, w_uq, w_dkv, g_kv, w_ukv, g_qn, g_kn, w_o, need_ctx):
    b, n, _ = hl.shape
    rope = axial_rope(n)
    ql = mla_q(hl, w_dq, g_q, w_uq, g_qn, rope)
    kl, vl = mla_kv(hl, w_dkv, g_kv, w_ukv, g_kn, rope)
    kc, vc = mla_kv(hc, w_dkv, g_kv, w_ukv, g_kn, None)
    k_all = jnp.concatenate([kl, kc], axis=1)
    v_all = jnp.concatenate([vl, vc], axis=1)
    nb = n // Q_BLOCK
    qb = ql.reshape(b, nb, Q_BLOCK, MLA_HEADS, MLA_QK).swapaxes(0, 1)
    ol = lax.map(lambda qi: attend(qi, k_all, v_all), qb)
    ol = ol.swapaxes(0, 1).reshape(b, n, MLA_HEADS * MLA_V) @ w_o
    oc = None
    if need_ctx:
        qc = mla_q(hc, w_dq, g_q, w_uq, g_qn, None)
        oc = attend(qc, kc, vc).reshape(b, hc.shape[1], MLA_HEADS * MLA_V) @ w_o
    return ol, oc

def centred_conv(u, w, b):
    n = u.shape[1]
    up = jnp.pad(u, ((0, 0), (RG_CONV_LEFT, RG_CONV - 1 - RG_CONV_LEFT), (0, 0)))
    out = b
    for k in range(RG_CONV):
        out = out + up[:, k:k + n] * w[k]
    return out

def block_diag(u, w, b):
    ub = u.reshape(u.shape[:-1] + (RG_BLOCKS, RG_BLOCK))
    return jnp.einsum('bnhi,hij->bnhj', ub, w).reshape(u.shape) + b

def rg_coeffs(u, w_a, b_a, w_x, b_x, lam):
    f32 = jnp.float32
    uf = u.astype(f32)
    r = jax.nn.sigmoid(block_diag(uf, w_a.astype(f32), b_a.astype(f32)))
    i = jax.nn.sigmoid(block_diag(uf, w_x.astype(f32), b_x.astype(f32)))
    log_a = -RG_C * r * jax.nn.softplus(-lam.astype(f32))
    return jnp.exp(log_a), jnp.sqrt(-jnp.expm1(2.0 * log_a)) * (i * uf)

def affine_combine(left, right):
    a1, b1 = left
    a2, b2 = right
    return a1 * a2, a2 * b1 + b2

def linear_scan(a, b, h0, reverse):
    if reverse:
        a, b = jnp.flip(a, 1), jnp.flip(b, 1)
    b = b.at[:, 0].add(a[:, 0] * h0)
    _, h = lax.associative_scan(affine_combine, (a, b), axis=1)
    return jnp.flip(h, 1) if reverse else h

def rg_direction(uc, ul, w_a, b_a, w_x, b_x, lam, reverse):
    ac, bc = rg_coeffs(uc, w_a, b_a, w_x, b_x, lam)
    hc = linear_scan(ac, bc, jnp.zeros((uc.shape[0], RG_WIDTH), jnp.float32), reverse)
    h_end = hc[:, 0] if reverse else hc[:, -1]
    al, bl = rg_coeffs(ul, w_a, b_a, w_x, b_x, lam)
    return hc, linear_scan(al, bl, h_end, reverse)

def rglru_mixer(hl, hc, w_in, w_gate, conv_w, conv_b, w_a, b_a, w_x, b_x, lam, w_out, need_ctx):
    ul = centred_conv(hl @ w_in, conv_w, conv_b)
    uc = centred_conv(hc @ w_in, conv_w, conv_b)
    hc_f, hl_f = rg_direction(uc, ul, w_a[0], b_a[0], w_x[0], b_x[0], lam[0], False)
    hc_b, hl_b = rg_direction(uc, ul, w_a[1], b_a[1], w_x[1], b_x[1], lam[1], True)
    ol = ((hl_f + hl_b).astype(hl.dtype) * jax.nn.gelu(hl @ w_gate)) @ w_out
    oc = None
    if need_ctx:
        oc = ((hc_f + hc_b).astype(hc.dtype) * jax.nn.gelu(hc @ w_gate)) @ w_out
    return ol, oc

def swiglu(h, w1, w3, w2):
    return (jax.nn.silu(h @ w1) * (h @ w3)) @ w2

def moe_swiglu(h, w_router, w1, w3, w2):
    logits = jnp.einsum('bnd,de->bne', h, w_router, preferred_element_type=jnp.float32)
    top_val, top_idx = lax.top_k(logits, TOP_K)
    gates = jax.nn.softmax(top_val, axis=-1)
    combine = jnp.einsum('bnk,bnke->bne', gates,
                         jax.nn.one_hot(top_idx, N_EXPERTS, dtype=jnp.float32)).astype(h.dtype)
    out = jnp.zeros_like(h)
    for e in range(N_EXPERTS):
        out = out + combine[..., e:e + 1] * swiglu(h, w1[e], w3[e], w2[e])
    return out

def setup_inputs(seed: int = 0) -> dict:
    key = jax.random.key(seed)
    ks = iter(jax.random.split(key, 40))
    f32 = jnp.float32
    n_a = (DEPTH + 1) // 2
    n_r = DEPTH // 2

    def nrm(shape, fan_in, gain=1.0):
        return gain * fan_in ** -0.5 * jax.random.normal(next(ks), shape, f32)

    def gain_vec(shape):
        return 1.0 + 0.05 * jax.random.normal(next(ks), shape, f32)

    def small(shape):
        return 0.02 * jax.random.normal(next(ks), shape, f32)

    x = jax.random.normal(next(ks), (BATCH, SEQ, D_MODEL), f32)
    c = jax.random.normal(next(ks), (BATCH, D_MODEL), f32)
    ctx = jax.random.normal(next(ks), (BATCH, CTX_LEN, D_MODEL), f32)
    c_ctx = jax.random.normal(next(ks), (D_MODEL,), f32)
    ada_w = nrm((DEPTH, D_MODEL, 6 * D_MODEL), D_MODEL, 0.5)
    ada_b = small((DEPTH, 6 * D_MODEL))
    norm1_g = gain_vec((DEPTH, D_MODEL))
    norm2_g = gain_vec((DEPTH, D_MODEL))
    mla_w_dq = nrm((n_a, D_MODEL, MLA_Q_LORA), D_MODEL)
    mla_g_q = gain_vec((n_a, MLA_Q_LORA))
    mla_w_uq = nrm((n_a, MLA_Q_LORA, MLA_HEADS * MLA_QK), MLA_Q_LORA)
    mla_w_dkv = nrm((n_a, D_MODEL, MLA_KV_LORA + MLA_ROPE), D_MODEL)
    mla_g_kv = gain_vec((n_a, MLA_KV_LORA))
    mla_w_ukv = nrm((n_a, MLA_KV_LORA, MLA_HEADS * (MLA_NOPE + MLA_V)), MLA_KV_LORA)
    mla_g_qn = gain_vec((n_a, MLA_QK))
    mla_g_kn = gain_vec((n_a, MLA_QK))
    mla_w_o = nrm((n_a, MLA_HEADS * MLA_V, D_MODEL), MLA_HEADS * MLA_V)
    rg_w_in = nrm((n_r, D_MODEL, RG_WIDTH), D_MODEL)
    rg_w_gate = nrm((n_r, D_MODEL, RG_WIDTH), D_MODEL)
    rg_conv_w = nrm((n_r, RG_CONV, RG_WIDTH), RG_CONV)
    rg_conv_b = small((n_r, RG_WIDTH))
    rg_w_a = nrm((n_r, 2, RG_BLOCKS, RG_BLOCK, RG_BLOCK), RG_BLOCK)
    rg_b_a = small((n_r, 2, RG_WIDTH))
    rg_w_x = nrm((n_r, 2, RG_BLOCKS, RG_BLOCK, RG_BLOCK), RG_BLOCK)
    rg_b_x = small((n_r, 2, RG_WIDTH))
    a0 = jax.random.uniform(next(ks), (n_r, 2, RG_WIDTH), f32, 0.9, 0.999)
    rg_lam = jnp.log(a0) - jnp.log1p(-a0)
    rg_w_out = nrm((n_r, RG_WIDTH, D_MODEL), RG_WIDTH)
    ffn_w1 = nrm((n_a, D_MODEL, FFN_HIDDEN), D_MODEL)
    ffn_w3 = nrm((n_a, D_MODEL, FFN_HIDDEN), D_MODEL)
    ffn_w2 = nrm((n_a, FFN_HIDDEN, D_MODEL), FFN_HIDDEN)
    moe_w_router = nrm((n_r, D_MODEL, N_EXPERTS), D_MODEL)
    moe_w1 = nrm((n_r, N_EXPERTS, D_MODEL, EXPERT_HIDDEN), D_MODEL)
    moe_w3 = nrm((n_r, N_EXPERTS, D_MODEL, EXPERT_HIDDEN), D_MODEL)
    moe_w2 = nrm((n_r, N_EXPERTS, EXPERT_HIDDEN, D_MODEL), EXPERT_HIDDEN)
    return {'x': x, 'c': c, 'ctx': ctx, 'c_ctx': c_ctx,
            'ada_w': ada_w, 'ada_b': ada_b, 'norm1_g': norm1_g, 'norm2_g': norm2_g,
            'mla_w_dq': mla_w_dq, 'mla_g_q': mla_g_q, 'mla_w_uq': mla_w_uq, 'mla_w_dkv': mla_w_dkv,
            'mla_g_kv': mla_g_kv, 'mla_w_ukv': mla_w_ukv, 'mla_g_qn': mla_g_qn, 'mla_g_kn': mla_g_kn,
            'mla_w_o': mla_w_o,
            'rg_w_in': rg_w_in, 'rg_w_gate': rg_w_gate, 'rg_conv_w': rg_conv_w, 'rg_conv_b': rg_conv_b,
            'rg_w_a': rg_w_a, 'rg_b_a': rg_b_a, 'rg_w_x': rg_w_x, 'rg_b_x': rg_b_x, 'rg_lam': rg_lam,
            'rg_w_out': rg_w_out,
            'ffn_w1': ffn_w1, 'ffn_w3': ffn_w3, 'ffn_w2': ffn_w2,
            'moe_w_router': moe_w_router, 'moe_w1': moe_w1, 'moe_w3': moe_w3, 'moe_w2': moe_w2}

def reference(x, c, ctx, c_ctx, ada_w, ada_b, norm1_g, norm2_g,
              mla_w_dq, mla_g_q, mla_w_uq, mla_w_dkv, mla_g_kv, mla_w_ukv, mla_g_qn, mla_g_kn, mla_w_o,
              rg_w_in, rg_w_gate, rg_conv_w, rg_conv_b, rg_w_a, rg_b_a, rg_w_x, rg_b_x, rg_lam, rg_w_out,
              ffn_w1, ffn_w3, ffn_w2, moe_w_router, moe_w1, moe_w3, moe_w2):
    for i in range(DEPTH):
        need_ctx = i < DEPTH - 1
        j = i // N_MIX
        sh1_l, sc1_l, g1_l, sh2_l, sc2_l, g2_l = [m[:, None, :] for m in ada_mod(c, ada_w[i], ada_b[i])]
        sh1_c, sc1_c, g1_c, sh2_c, sc2_c, g2_c = ada_mod(c_ctx, ada_w[i], ada_b[i])

        hl = modulate(rms_norm(x, norm1_g[i]), sh1_l, sc1_l)
        hc = modulate(rms_norm(ctx, norm1_g[i]), sh1_c, sc1_c)
        if i % N_MIX == 0:
            ol, oc = mla_mixer(hl, hc, mla_w_dq[j], mla_g_q[j], mla_w_uq[j], mla_w_dkv[j], mla_g_kv[j],
                               mla_w_ukv[j], mla_g_qn[j], mla_g_kn[j], mla_w_o[j], need_ctx)
        else:
            ol, oc = rglru_mixer(hl, hc, rg_w_in[j], rg_w_gate[j], rg_conv_w[j], rg_conv_b[j],
                                 rg_w_a[j], rg_b_a[j], rg_w_x[j], rg_b_x[j], rg_lam[j], rg_w_out[j], need_ctx)
        x = x + g1_l * ol

        if i % 2 == 0:
            ffn = lambda h: swiglu(h, ffn_w1[j], ffn_w3[j], ffn_w2[j])
        else:
            ffn = lambda h: moe_swiglu(h, moe_w_router[j], moe_w1[j], moe_w3[j], moe_w2[j])
        x = x + g2_l * ffn(modulate(rms_norm(x, norm2_g[i]), sh2_l, sc2_l))

        if need_ctx:
            ctx = ctx + g1_c * oc
            ctx = ctx + g2_c * ffn(modulate(rms_norm(ctx, norm2_g[i]), sh2_c, sc2_c))
    return x


_drawn_inputs = setup_inputs


def setup_inputs(seed=0):
    import zlib

    import numpy as np

    out = dict(_drawn_inputs(seed))
    spreads = {}
    factors = {'mla_g_q': 7.355,
     'mla_g_kv': 4.204,
     'mla_g_qn': 8.0,
     'mla_g_kn': 8.0,
     'rg_b_a': 63.899,
     'rg_b_x': 37.492,
     'norm2_g': 3.367,
     'rg_conv_b': 4.383}
    for name, (base, spread) in spreads.items():
        noise = np.random.default_rng([zlib.crc32(name.encode()), seed]).standard_normal(out[name].shape)
        drawn = base * np.exp(spread * noise) if base else spread * noise
        out[name] = __import__('jax').numpy.asarray(drawn.astype(out[name].dtype))
    for name, factor in factors.items():
        out[name] = (out[name] * factor).astype(out[name].dtype)
    return out
```

```python
from contextlib import ExitStack

import numpy as np

import concourse.bass as bass
from concourse import mybir

ALU = mybir.AluOpType
ACT = mybir.ActivationFunctionType
AX = mybir.AxisListType
F32 = mybir.dt.float32
F32R = mybir.dt.float32r
I32 = mybir.dt.int32
U32 = mybir.dt.uint32

P = 128
D = 1024
KD = D // P
NC_TOK = 256
NL_TOK = 256
T = NC_TOK + NL_TOK
CTX = slice(0, NC_TOK)
LAT = slice(NC_TOK, T)
EPS = 1e-6
HEADS, Q_LORA, NOPE, ROPE, DV = 8, 256, 128, 64, 128
QK = NOPE + ROPE
KQ = Q_LORA // P
PAIRS = HEADS // 2
GRID_W = 64
ROPE_BASE = 10000.0
FFN = 2816
F_TILES = FFN // P
HALF_F = F_TILES // 2
RG_BLOCKS, RG_CONV, RG_LEFT, RG_C = 4, 4, 2, 8.0
N_EXP, EH = 8, 3584
FB = 512
NJ = EH // FB
SLOTS = P
MAX_OVER = 3
MAX_ROUNDS = N_EXP + MAX_OVER

UW = 2048
TPU = UW // P
RING_IN = 3
RING = 3
RAW_SLOTS = 6
ADA_SLOT = 3
ADA_RING = 2
TMP_SLOT = 5
ADA_GROUPS = 2 * 6 * D // 512
W2_UNIT_TILES = 13
W2_UNITS = -(-KD * HALF_F // W2_UNIT_TILES)
FFN_UNITS = HALF_F + W2_UNITS
U_Q, U_KV, U_V, U_HEADS, U_O, U_FFN = 0, 1, 2, 3, 5, 9
U_RG = U_FFN + 2 * FFN_UNITS
U_RGO = U_RG + 3 * RG_BLOCKS
N_UNITS = U_RGO + KD // 2
EXP_UNITS = NJ * 6

C_ID, C_PERM, C_ONE, C_TRI, C_IOTA, C_COS, C_SIN = 0, P, 2 * P, 3 * P, 4 * P, 5 * P, 5 * P + T
N_CONST = 5 * P + 2 * T
SEL_STEPS = 19
P_C, P_ADAB, P_N1, P_N2 = 0, 16, 112, 128
P_GQ, P_GKV, P_GQN, P_GKN, P_GQR, P_GKR = 144, 146, 147, 148, 149, 150
P_CW, P_CB, P_BA, P_BX, P_LAM, P_RW = 151, 183, 191, 207, 223, 239
N_PAR = P_RW + KD * N_EXP
SH1, SC1, GA1, SH2, SC2, GA2 = range(6)


class Plan:

    def __init__(self):
        self.bank, self.order, self.before, self.n = {}, {}, {}, 0
        last = {}

        def put(name, bank, reader, value):
            self.bank[name], self.order[name], self.before[name] = bank, self.n, last.get(bank)
            last[bank] = (reader, value)
            self.n += 1

        def attend(p, i):
            n = 4 * p + i + 1
            put(("PT0", p, i), 4, "pt_a", n)
            put(("PT1", p, i), 5, "pt_b", n)
            put(("att", p, i), 6, "o_lo", n)

        put(("ss", 0), 6, "root", 1)
        put("qa0", 0, "cq_f", 1)
        put("qa1", 1, "cq_f", 2)
        put("ckv", 2, "cq_f", 3)
        put("pe", 3, "kpe_step", 1)
        put("ss q", 4, "lat_root", 1)
        put("ss kv", 5, "lat_root", 2)
        put("swap k", 6, "kpe_step", 2)
        for i in range(8):
            put(("v", i), i % 4, "v_a" if i % 2 == 0 else "v_b", i // 2 + 1)
        for p in range(PAIRS):
            put(("qn0", p), 0, "q_ready", 4 * p + 1)
            put(("qn1", p), 1, "q_ready", 4 * p + 3)
            put(("qr", p), 2, "qr_step", 4 * p + 1)
            put(("kn0", p), 3, "k_ready", 4 * p + 1)
            put(("kn1", p), 4, "k_ready", 4 * p + 3)
            put(("ss q0", p), 5, "hd_root", 4 * p + 1)
            put(("ss q1", p), 6, "hd_root", 4 * p + 2)
            put(("swap q", p), 5, "qr_step", 4 * p + 2)
            put(("ss k0", p), 5, "hd_root", 4 * p + 3)
            put(("ss k1", p), 6, "hd_root", 4 * p + 4)
            for i in range(4):
                for j in range(2):
                    put((f"score{j}", p, i), 2 * (i % 2) + j, "s_exp", 2 * (4 * p + i) + j + 1)
                if i:
                    attend(p, i - 1)
            attend(p, 3)
        for m in range(KD):
            put(("o", m), m % 4, "x_mid0", 2 * (m + 1))
        put(("ss", 1), 6, "root", 2)
        self.ffn = self.n
        self.n += 2 * len(FFN_MADE)
        last.update({0: ("f_silu", 2 * HALF_F), 1: ("f_mul", 2 * HALF_F + 1), 2: ("f_silu", 2 * HALF_F - 1),
                     3: ("f_mul", 2 * HALF_F), 4: ("f_x", 4 * KD - 1), 5: ("f_x", 4 * KD + 1)})
        put(("ss", 2), 6, "root", 3)
        for b in range(RG_BLOCKS):
            for m in range(2):
                put(("u", b, m), m, "rg_in", 2 * b + m + 1)
            for m in range(2):
                put(("gate", b, m), 2 + m, "rg_gelu", 2 * b + m + 1)
            for d in range(2):
                for m in range(2):
                    put(("a", b, d, m), 4 + m, "rg_sig", 4 * b + 2 * d + m + 1)
                    put(("x", b, d, m), 6 + m, "rg_i", 4 * b + 2 * d + m + 1)
        for m in range(KD):
            put(("rg o", m), m % 4, "x_mid1", m + 1)
        put(("ss", 3), 6, "root", 4)
        put("logits", 0, "lt_ready", 1)
        put("logits T", 1, "rt_step", 1)
        for i in range(4):
            put(("h2", i), 2 + i, "h2_lo", i + 1)
        put("pos", 6, "pos_ready", 1)


def ffn_made():
    done = []
    for i in range(HALF_F):
        done += [("h1", i), ("h3", i)]
    n = KD * HALF_F
    for t in range(n):
        if t % HALF_F == HALF_F - 1:
            done.append(("y", t // HALF_F))
        elif t % W2_UNIT_TILES == W2_UNIT_TILES - 1:
            done.append(("w2 unit", t // W2_UNIT_TILES))
    return {name: i for i, name in enumerate(done)}


FFN_MADE = ffn_made()
M_GATE, M_U0, M_OUT, M_LOOP, J_MADE = 0, 1, 5, 9, 7
M_JU = (M_LOOP, M_LOOP + 1, M_LOOP + 3, M_LOOP + 4, M_LOOP + 5, M_LOOP + 6)
M_JT = M_LOOP + 2
M_TAIL = M_LOOP + J_MADE * (NJ - 1)
M_X, M_GT, M_XT, M_U40, M_U41 = M_TAIL, M_TAIL + 2, M_TAIL + 3, M_TAIL + 5, M_TAIL + 6
ROUND_MADE = M_U41 + 1
PEEL_MADE = 16


def dit_kernel(nc, x_t, consts, params, ada_w, w_units, moe_w, out):
    plan = Plan()
    with ExitStack() as ctx:
        def sb(name, shape, dt=F32, scope=ctx):
            return scope.enter_context(nc.sbuf_tensor(name, shape, dt))

        def sem(name):
            return ctx.enter_context(nc.semaphore(name))

        PS = ctx.enter_context(nc.psum_tensor("PS", [P, 8, 512], F32))

        RAW = sb("RAW", [P, RAW_SLOTS, UW])
        WHI = sb("WHI", [P, RING, UW], F32R)
        WLO = sb("WLO", [P, RING, UW], F32R)
        X = sb("X", [P, KD, T])
        CONST = sb("CONST", [P, N_CONST])
        PAR = sb("PAR", [P, N_PAR])
        CS = sb("CS", [P, KD, 32])
        MC = sb("MC", [P, 2, 48, 2])
        CA = sb("CA", [P, 4, KD, 2])
        GE = sb("GE", [P, 16])
        GQK, EPSC, SPARE = GE[:, 0:1], GE[:, 1:2], GE[:, 8:16]
        RSTD = sb("RSTD", [P, T])
        ROW = sb("ROW", [P, 512])
        HHI = sb("HHI", [P, KD, T], F32R)
        HLO = sb("HLO", [P, KD, T], F32R)
        IDENT = CONST[:, C_ID:C_ID + P]
        PERM = CONST[:, C_PERM:C_PERM + P]
        ONES = CONST[:, C_ONE:C_ONE + P]
        TRI = CONST[:, C_TRI:C_TRI + P]
        IOTA = CONST[:, C_IOTA:C_IOTA + P]
        COS = CONST[:, C_COS:C_COS + T]
        SIN = CONST[:, C_SIN:C_SIN + T]
        TMP = RAW[:, TMP_SLOT, :].rearrange("p (s t) -> p s t", t=T)

        with ExitStack() as mla:
            def mb(name, shape, dt=F32):
                return sb(name, shape, dt, mla)
            CQHI = mb("CQHI", [P, KQ, T], F32R)
            CQLO = mb("CQLO", [P, KQ, T], F32R)
            CKHI = mb("CKHI", [P, T], F32R)
            CKLO = mb("CKLO", [P, T], F32R)
            V = mb("V", [P, 4, HEADS * DV])
            KPE = mb("KPE", [P, T])
            QN = mb("QN", [P, 2, T])
            QR = mb("QR", [P, T])
            KN = mb("KN", [P, 2, T])
            KR = mb("KR", [P, T])
            PR = mb("PR", [P, 2, T])
            PT = mb("PT", [P, 4, 256])
            SMALL = mb("SMALL", [P, 8])
            MX, NM, SM, RI = (SMALL[:, 2 * i:2 * i + 2] for i in range(4))
        with ExitStack() as ffn:
            GHI = sb("GHI", [P, HALF_F, T], F32R, ffn)
            GLO = sb("GLO", [P, HALF_F, T], F32R, ffn)
        with ExitStack() as rg:
            def rb(name, shape, dt=F32):
                return sb(name, shape, dt, rg)
            SEG = NC_TOK + RG_CONV - 1
            UP = rb("UP", [P, 2, 2, SEG])
            UC = rb("UC", [P, 2, T])
            UCHI = rb("UCHI", [P, 2, T], F32R)
            UCLO = rb("UCLO", [P, 2, T], F32R)
            GG = rb("GG", [P, 2, NL_TOK])
            SQ = rb("SQ", [P, 4, T])
            HS = rb("HS", [P, 2, T])
            SPL = rb("SPL", [P, 8, 16])
            YHI = rb("YHI", [P, KD, NL_TOK], F32R)
            YLO = rb("YLO", [P, KD, NL_TOK], F32R)
            RT = RAW[:, ADA_SLOT, :].rearrange("p (n t) -> p n t", t=T)
            IT = RAW[:, ADA_SLOT + 1, :].rearrange("p (n t) -> p n t", t=T)
            TH = TMP
        moe = ctx.enter_context(ExitStack())

        def eb(name, shape, dt=F32):
            return sb(name, shape, dt, moe)
        H2T = eb("H2T", [P, KD, NL_TOK])
        LT = eb("LT", [N_EXP, NL_TOK])
        LG = eb("LG", [P, 2, N_EXP])
        M8 = eb("M8", [P, 2, 8])
        IX = eb("IX", [P, 2, 8], U32)
        IXF = eb("IXF", [P, 2, 8])
        GV = eb("GV", [P, 2, 4])
        MK1 = eb("MK1", [P, 2, N_EXP])
        MK2 = eb("MK2", [P, 2, N_EXP])
        SEL = eb("SEL", [P, 2, N_EXP])
        CMB = eb("CMB", [P, 2, N_EXP])
        POS = eb("POS", [P, 3, N_EXP])
        OVR = eb("OVR", [P, 4, N_EXP])
        RP = eb("RP", [P, 2, 12])
        RG = eb("RG", [P, 2, 12])
        EX = eb("EX", [P, 16])
        EXI = eb("EXI", [P, 16], I32)
        G = eb("G", [P, 2, SLOTS], F32R)
        GTN = eb("GTN", [P, NL_TOK])
        GTR = eb("GTR", [P, NL_TOK], F32R)
        GS = eb("GS", [P, 1])
        XS = eb("XS", [P, D])
        SG = eb("SG", [P, FB])
        GM = eb("GM", [P, FB])
        GTHI = eb("GTHI", [P, 4, SLOTS], F32R)
        GTLO = eb("GTLO", [P, 4, SLOTS], F32R)
        XTHI = HHI[:, 0:2, :].rearrange("p a (b s) -> p (a b) s", s=SLOTS)
        XTLO = HLO[:, 0:2, :].rearrange("p a (b s) -> p (a b) s", s=SLOTS)
        YRHI = HHI[:, 2:4, :]
        YRLO = HLO[:, 2:4, :]
        H2HI = HHI[:, 4:8, :].rearrange("p (t a) b -> p t (a b)", t=2)
        H2LO = HLO[:, 4:8, :].rearrange("p (t a) b -> p t (a b)", t=2)
        YR = eb("YR", [P, 2, 512])
        ACC = eb("ACC", [P, KD, NL_TOK])
        ZERO = eb("ZERO", [P, 512], F32R)

        in_x, in_const, in_par = sem("in_x"), sem("in_const"), sem("in_par")
        raw_in = [sem(f"raw_in{i}") for i in range(RAW_SLOTS)]
        ada_in = [sem(f"ada_in{i}") for i in range(ADA_RING)]
        w_hi, w_lo, made = sem("w_hi"), sem("w_lo"), sem("made")
        e_hi, e_lo, e_made = sem("e_hi"), sem("e_lo"), sem("e_made")
        v_a, v_b = sem("v_a"), sem("v_b")
        rt_step, pos_ready = sem("rt_step"), sem("pos_ready")
        rg_back, rg_sum = sem("rg_back"), sem("rg_sum")
        zeros_ready = sem("zeros_ready")
        cs_zero, cs_ready = sem("cs_zero"), sem("cs_ready")
        eps_ready = sem("eps_ready")
        ada_used, ada_row, ada_rowT, ada_cols = sem("ada_used"), sem("ada_row"), sem("ada_rowT"), sem("ada_cols")
        ada_sum = sem("ada_sum")
        coef = sem("coef")
        gqk_ready = sem("gqk_ready")
        sq_done, sq_used, root, rstd = sem("sq_done"), sem("sq_used"), sem("root"), sem("rstd")
        xr, mod, h_hi, h_lo = sem("xr"), sem("mod"), sem("h_hi"), sem("h_lo")
        lat_sq, lat_root, lat_rstd = sem("lat_sq"), sem("lat_root"), sem("lat_rstd")
        cq_f, cq_hi, cq_lo = sem("cq_f"), sem("cq_hi"), sem("cq_lo")
        kpe_step = sem("kpe_step")
        v_ready = sem("v_ready")
        hd_sq, hd_sum, hd_root, hd_rstd = sem("hd_sq"), sem("hd_sum"), sem("hd_root"), sem("hd_rstd")
        qr_step, q_ready, k_ready = sem("qr_step"), sem("q_ready"), sem("k_ready")
        s_max, s_neg, s_exp, s_rec, s_prob = (sem("s_max"), sem("s_neg"), sem("s_exp"), sem("s_rec"),
                                              sem("s_prob"))
        pt_a, pt_b, o_hi, o_lo = sem("pt_a"), sem("pt_b"), sem("o_hi"), sem("o_lo")
        x_mid = [sem(f"x_mid{i}") for i in range(2)]
        f_silu, f_mul, f_hi, f_lo, f_x = sem("f_silu"), sem("f_mul"), sem("f_hi"), sem("f_lo"), sem("f_x")
        spl = sem("spl")
        rg_pad, rg_in, rg_conv, rg_uhi, rg_ulo = (sem("rg_pad"), sem("rg_in"), sem("rg_conv"), sem("rg_uhi"),
                                                  sem("rg_ulo"))
        rg_gelu, rg_sig, rg_i, rg_exp, rg_tanh = (sem("rg_gelu"), sem("rg_sig"), sem("rg_i"), sem("rg_exp"),
                                                  sem("rg_tanh"))
        rg_iu, rg_sq, rg_w, rg_b, rg_scan = (sem("rg_iu"), sem("rg_sq"), sem("rg_w"), sem("rg_b"),
                                              sem("rg_scan"))
        rg_root, rg_y, rg_yhi, rg_ylo = (sem("rg_root"), sem("rg_y"), sem("rg_yhi"),
                                               sem("rg_ylo"))
        rt, rt_exp, rt_done = sem("rt"), sem("rt_exp"), sem("rt_done")
        lt_ready, h2_hi, h2_lo = sem("lt_ready"), sem("h2_hi"), sem("h2_lo")
        g_ready, gt_ready, gs_ready = sem("g_ready"), sem("gt_ready"), sem("gs_ready")
        gtn_ready = sem("gtn_ready")
        xs_ready, xt_hi, xt_lo = sem("xs_ready"), sem("xt_hi"), sem("xt_lo")
        m_silu, m_mul, m_gthi, m_gtlo = sem("m_silu"), sem("m_mul"), sem("m_gthi"), sem("m_gtlo")
        y_f, y_hi, y_lo, acc = sem("y_f"), sem("y_hi"), sem("y_lo"), sem("acc")
        fin, out_done = sem("fin"), sem("out_done")

        block = ctx.enter_context(nc.Block())

        by_name = {"root": root, "cq_f": cq_f, "kpe_step": kpe_step, "lat_root": lat_root, "v_a": v_a, "v_b": v_b,
                   "q_ready": q_ready, "k_ready": k_ready, "qr_step": qr_step, "hd_root": hd_root,
                   "s_exp": s_exp, "pt_a": pt_a, "pt_b": pt_b, "o_lo": o_lo, "x_mid0": x_mid[0],
                   "x_mid1": x_mid[1], "f_silu": f_silu, "f_mul": f_mul, "f_x": f_x, "rg_in": rg_in,
                   "rg_gelu": rg_gelu, "rg_sig": rg_sig, "rg_i": rg_i, "lt_ready": lt_ready,
                   "rt_step": rt_step, "h2_lo": h2_lo, "pos_ready": pos_ready}

        def bank(name):
            return PS[:, plan.bank[name], :]

        def bank_read(name):
            reader, value = plan.before[name]
            return by_name[reader], value

        def wait_full(eng, name):
            eng.wait_ge(made, plan.order[name] + 1)

        def wait_used(eng, u):
            eng.wait_ge(made, plan.order[LAST_OF_UNIT[u]] + 1)

        LAST_OF_UNIT = {U_Q: "qa1", U_KV: "pe", U_V: ("v", 7), U_HEADS: ("kn1", 1), U_HEADS + 1: ("kn1", 3)}
        for i in range(KD // 2):
            LAST_OF_UNIT[U_O + i] = ("o", 2 * i + 1)
            LAST_OF_UNIT[U_RGO + i] = ("rg o", 2 * i + 1)
        for i in range(RG_BLOCKS):
            LAST_OF_UNIT[U_RG + 3 * i] = ("u", i, 1)
            LAST_OF_UNIT[U_RG + 3 * i + 1] = ("gate", i, 1)
            LAST_OF_UNIT[U_RG + 3 * i + 2] = ("x", i, 1, 1)

        def ffn_at(h, name):
            return plan.ffn + h * len(FFN_MADE) + FFN_MADE[name] + 1

        def ffn_used(h, i):
            i -= RING
            if i < 0:
                h, i = h - 1, i + FFN_UNITS
            if i < HALF_F:
                return ffn_at(h, ("h3", i))
            q = i - HALF_F
            return ffn_at(h, ("y", KD - 1) if q == W2_UNITS - 1 else ("w2 unit", q))

        def round_at(r, n):
            return PEEL_MADE + ROUND_MADE * r + n + 1

        def ada_group(p, i):
            return 4 + 5 * p + i

        def ring(u):
            return u % RING

        def unit_cols(u):
            if u == U_V:
                return HEADS * DV
            if U_FFN <= u < U_RG:
                q = (u - U_FFN) % FFN_UNITS - HALF_F
                if q >= 0:
                    return P * min(W2_UNIT_TILES, KD * HALF_F - W2_UNIT_TILES * q)
            return UW

        def wait_x(eng, n, k):
            if n == 0:
                eng.wait_ge(in_x, 16)
            elif n == 1:
                eng.wait_ge(x_mid[0], 2 * (k + 1))
            elif n == 2:
                eng.wait_ge(f_x, 2 * (KD + k + 1) + 1)
            else:
                eng.wait_ge(x_mid[1], k + 1)

        def toks(n):
            return slice(0, T) if n < 3 else LAT

        @block.sync
        def _(sp):
            sp.dma_start(PAR[:], params).then_inc(in_par, 16)
            sp.dma_start(CONST[:], consts).then_inc(in_const, 16)
            sp.dma_start(X[:], x_t.rearrange("k p t -> p k t")).then_inc(in_x, 16)

            def load(u, slot, cols, at, wait=True):
                if wait:
                    sp.wait_ge(w_hi, at - RING_IN + 1)
                    sp.wait_ge(w_lo, at - RING_IN + 1)
                sp.dma_start(RAW[:, slot, 0:cols], u[:, 0:cols]).then_inc(raw_in[slot], 16)

            for u in range(U_FFN):
                load(w_units[u], u % RING_IN, unit_cols(u), u, u >= RING_IN)
            with sp.Fori(0, 2) as h:
                for i in range(FFN_UNITS):
                    u = U_FFN + h * FFN_UNITS + i
                    load(w_units[bass.ds(u, 1)].rearrange("o p n -> p (o n)"), i % RING_IN,
                         unit_cols(U_FFN + i), u)
            for u in range(U_RG, N_UNITS):
                load(w_units[u], u % RING_IN, unit_cols(u), u, u >= RING_IN)

            def load_expert(e, r, j, c, wait=True):
                if wait:
                    sp.wait_ge(e_hi, r * EXP_UNITS + 6 * j + c - RAW_SLOTS + 1)
                    sp.wait_ge(e_lo, r * EXP_UNITS + 6 * j + c - RAW_SLOTS + 1)
                sp.dma_start(RAW[:, c, :], moe_w[bass.ds(e * EXP_UNITS + 6 * j + c, 1)].rearrange(
                    "o p n -> p (o n)")).then_inc(raw_in[c], 16)

            for c in range(RAW_SLOTS):
                if c == 0:
                    sp.wait_ge(w_hi, N_UNITS)
                    sp.wait_ge(w_lo, N_UNITS)
                if c == ADA_SLOT:
                    sp.wait_ge(rg_y, KD)
                if c == TMP_SLOT:
                    sp.wait_ge(root, 4)
                load_expert(0, 0, 0, c, wait=False)
            with sp.Fori(1, NJ) as j:
                for c in range(RAW_SLOTS):
                    load_expert(0, 0, j, c)
            sp.wait_ge(rt_done, 1)
            rounds = sp.value_load(EXI[0:1, 15:16], min_val=N_EXP, max_val=MAX_ROUNDS)
            with sp.Fori(1, rounds) as r:
                e = sp.value_load(EXI[0:1, bass.ds(r, 1)], min_val=0, max_val=N_EXP - 1)
                with sp.Fori(0, NJ) as j:
                    for c in range(RAW_SLOTS):
                        load_expert(e, r, j, c)
            sp.wait_ge(fin, KD)
            sp.dma_start(out.rearrange("k p t -> p k t"), ACC[:]).then_inc(out_done, 16)
            sp.wait_ge(out_done, 16)

        def norm_scale(pool, n):
            pool.wait_ge(rstd, n + 1)
            for k in range(KD):
                g = n * KD + k
                if 4 <= g < 3 * KD:
                    pool.wait_ge(h_lo, g - 3)
                if n < 3:
                    wait_x(pool, n, k)
                    pool.tensor_tensor(TMP[:, k % 4, :], X[:, k, :], RSTD[:], ALU.mult).then_inc(xr, 1)
                else:
                    wait_x(pool, n, k)
                    pool.tensor_tensor(H2T[:, k, :], X[:, k, LAT], RSTD[:, 0:NL_TOK], ALU.mult).then_inc(xr, 1)

        @block.gpsimd
        def _(pool):
            pool.memset(CS[:], 0.0).then_inc(cs_zero, 1)
            pool.memset(EPSC, EPS).then_inc(eps_ready, 1)
            for i, from_one in enumerate((f_mul, f_x, m_silu, m_mul, m_gtlo, y_lo)):
                pool.memset(SPARE[:, i:i + 1], 0.0).then_inc(from_one, 1)
            def load_ada(n):
                if n < 2 * ADA_GROUPS:
                    if n >= ADA_RING:
                        pool.wait_ge(ada_used, n - ADA_RING + 1)
                    pool.dma_start(RAW[:, ADA_SLOT + n % ADA_RING, :],
                                   ada_w[n]).then_inc(ada_in[n % ADA_RING], 16)

            for n in range(2 * 4 + ADA_RING):
                load_ada(n)
            norm_scale(pool, 0)
            for p in range(PAIRS):
                for kind in range(2):
                    pool.wait_ge(hd_sq, 5 * p + (3 if kind == 0 else 5))
                    rope_sq = TMP[:, 2, :] if kind == 0 else TMP[:, 3, :]
                    for i in range(2):
                        half = slice(64 * i, 64 * i + 64)
                        pool.tensor_tensor(TMP[half, i, :], TMP[half, i, :], rope_sq[half, :],
                                           ALU.add).then_inc(hd_sum, 1)
                    for g in ((0,), (1, 2, 3, 4))[kind]:
                        for n in range(2):
                            load_ada(2 * ada_group(p, g) + ADA_RING + n)
            norm_scale(pool, 1)
            norm_scale(pool, 2)
            for b in range(RG_BLOCKS):
                for n in range(4):
                    e = 4 * b + n + 1
                    pool.wait_ge(rg_i, e)
                    pool.tensor_tensor(IT[:, n, :], IT[:, n, :], UC[:, n % 2, :], ALU.mult).then_inc(rg_iu, 1)
                for n in range(4):
                    e = 4 * b + n + 1
                    pool.wait_ge(rg_exp, e)
                    if b:
                        pool.wait_ge(rg_y, 2 * b)
                    pool.tensor_tensor(SQ[:, n, :], RT[:, n, :], RT[:, n, :], ALU.mult).then_inc(rg_sq, 1)
            norm_scale(pool, 3)
            pool.wait_ge(made, plan.order[("ss", 3)] + 1)
            pool.memset(ZERO[:].bitcast(F32), 0.0).then_inc(zeros_ready, 1)
            pool.memset(ACC[:], 0.0).then_inc(acc, 1)
            pool.memset(GTR[:].bitcast(F32), 0.0).then_inc(gt_ready, 1)
            pool.memset(GS[:], 0.0).then_inc(gs_ready, 1)
            pool.wait_ge(rt_done, 1)
            rounds = pool.value_load(EXI[0:1, 15:16], min_val=N_EXP, max_val=MAX_ROUNDS)

            def out_lo(r):
                for i in range(2):
                    pool.wait_ge(y_hi, 2 * r + i + 1)
                    pool.tensor_tensor(YRLO[:, i, :], YR[:, i, :], YRHI[:, i, :].bitcast(F32),
                                       ALU.subtract).then_inc(y_lo, 1)

            with pool.Fori(0, rounds) as r:
                out_lo(r)
            out_lo(rounds)

        @block.scalar
        def _(act):
            def hi(slot_u, n_in, used):
                s = slot_u % RING
                act.wait_ge(raw_in[s], n_in)
                if used is not None:
                    act.wait_ge(made, used)
                c = unit_cols(slot_u)
                act.activation(WHI[:, s, 0:c], RAW[:, s, 0:c], ACT.Copy).then_inc(w_hi, 1)

            def hi_static(u):
                if u < N_UNITS and not U_FFN <= u < U_RG:
                    hi(u, 16 * (u // RING_IN + 1),
                       None if u < RING else plan.order[LAST_OF_UNIT[u - RING]] + 1 if u != U_RG + 1 and
                       u != U_RG + 2 else ffn_used(2, u - U_RG))

            def squares(n):
                for k in range(KD):
                    g = n * KD + k
                    wait_x(act, n, k)
                    if k >= 2:
                        act.wait_ge(sq_used, n * (KD - 1) + k - 1)
                    N = toks(n)
                    w = N.stop - N.start
                    act.activation(TMP[:, k % 2, 0:w], X[:, k, N], ACT.Square).then_inc(sq_done, 1)
                wait_full(act, ("ss", n))
                act.wait_ge(eps_ready, 1)
                act.activation(RSTD[:, 0:w], bank(("ss", n))[:, 0:w], ACT.Sqrt, bias=EPSC,
                               scale=1.0 / D).then_inc(root, 1)

            def norm_hi(n):
                for k in range(KD):
                    act.wait_ge(mod, 2 * (n * KD + k + 1))
                    act.activation(HHI[:, k, :], TMP[:, k % 4, :], ACT.Copy).then_inc(h_hi, 1)

            def ada_copy(a):
                act.wait_ge(ada_used, 2 * a + 2)
                if a:
                    act.wait_ge(ada_rowT, a)
                act.activation(ROW[:], PS[:, 7, :], ACT.Copy).then_inc(ada_row, 1)

            act.wait_ge(in_par, 16)
            act.wait_ge(cs_zero, 1)
            act.activation(CS[:, :, 0:2], PAR[:, P_C:P_C + 16].rearrange("p (k s) -> p k s", s=2),
                           ACT.Silu).then_inc(cs_ready, 1)
            hi_static(0)
            hi_static(1)
            hi_static(2)
            for a in range(4):
                ada_copy(a)
            squares(0)
            norm_hi(0)
            for i, name in enumerate(("qa0", "qa1", "ckv", "pe")):
                wait_full(act, name)
                act.wait_ge(h_lo, KD)
                act.activation(TMP[:, i, :], bank(name), ACT.Square).then_inc(lat_sq, 1)
            wait_full(act, "ss q")
            act.wait_ge(xr, KD)
            act.activation(RSTD[:], bank("ss q"), ACT.Sqrt, bias=EPSC, scale=1.0 / Q_LORA).then_inc(lat_root, 1)
            for i in range(2):
                act.wait_ge(cq_f, i + 1)
                act.activation(CQHI[:, i, :], TMP[:, i, :], ACT.Copy).then_inc(cq_hi, 1)
            wait_full(act, "ss kv")
            act.activation(RSTD[:], bank("ss kv"), ACT.Sqrt, bias=EPSC, scale=1.0 / P).then_inc(lat_root, 1)
            act.wait_ge(cq_f, 3)
            act.activation(CKHI[:], TMP[:, 2, :], ACT.Copy).then_inc(cq_hi, 1)
            hi_static(3)
            hi_static(4)
            for i in range(0, 8, 2):
                wait_full(act, ("v", i))
                act.activation(V[:, i // 2, 0:512], bank(("v", i)), ACT.Copy).then_inc(v_a, 1)
            hi_static(5)
            for p in range(PAIRS):
                for i, name in enumerate(("qn0", "qn1", "qr")):
                    wait_full(act, (name, p))
                    if i < 2 and p:
                        wait_full(act, (f"ss k{i}", p - 1))
                    if i == 2 and p:
                        act.wait_ge(qr_step, 4 * p)
                    if p == 0:
                        act.wait_ge(cq_lo, 3)
                        act.wait_ge(kpe_step, 4)
                    act.activation(TMP[:, i, :], bank((name, p)), ACT.Square).then_inc(hd_sq, 1)
                ada_copy(ada_group(p, 0))
                for i in range(2):
                    name = (f"ss q{i}", p)
                    wait_full(act, name)
                    if i == 0 and p:
                        act.wait_ge(k_ready, 4 * p)
                    if i == 1:
                        act.wait_ge(q_ready, 4 * p + 2)
                    if p == 0 and i == 0:
                        act.wait_ge(cq_f, 3)
                    act.activation(RSTD[:], bank(name), ACT.Sqrt, bias=EPSC, scale=1.0 / QK).then_inc(hd_root, 1)
                for i in range(2):
                    wait_full(act, (f"kn{i}", p))
                    wait_full(act, (f"ss q{i}", p))
                    act.activation(TMP[:, i, :], bank((f"kn{i}", p)), ACT.Square).then_inc(hd_sq, 1)
                ada_copy(ada_group(p, 1))
                for i in range(2):
                    name = (f"ss k{i}", p)
                    wait_full(act, name)
                    if i == 0:
                        act.wait_ge(q_ready, 4 * p + 4)
                    else:
                        act.wait_ge(k_ready, 4 * p + 2)
                    act.activation(RSTD[:], bank(name), ACT.Sqrt, bias=EPSC, scale=1.0 / QK).then_inc(hd_root, 1)
                ada_copy(ada_group(p, 2))
                for i in range(5):
                    it = 4 * p + i
                    if i < 4:
                        nk = NC_TOK if i % 2 == 0 else T
                        for j in range(2):
                            name = (f"score{j}", p, i)
                            wait_full(act, name)
                            act.wait_ge(s_neg, 2 * it + j + 1)
                            if it:
                                wait_full(act, (f"PT{j}", (it - 1) // 4, (it - 1) % 4))
                            act.activation(PR[:, j, 0:nk], bank(name)[:, 0:nk], ACT.Exp, bias=NM[:, j:j + 1],
                                           scale=QK ** -0.5, accum_out=SM[:, j:j + 1]).then_inc(s_exp, 1)
                    if i in (1, 3):
                        ada_copy(ada_group(p, 3 + i // 2))
                    if i:
                        h, g = 2 * p + (i - 1) // 2, (i - 1) % 2
                        nk = NC_TOK if g == 0 else T
                        name = ("PT0", p, i - 1)
                        wait_full(act, name)
                        if it > 1:
                            wait_full(act, ("att", (it - 2) // 4, (it - 2) % 4))
                        act.activation(PT[:, 0:nk // P, 0:P],
                                       bank(name)[:, 0:nk].rearrange("p (k q) -> p k q", q=P),
                                       ACT.Copy).then_inc(pt_a, 1)
                        name = ("att", p, i - 1)
                        wait_full(act, name)
                        act.activation(HHI[:, h, 256 * g:256 * g + 256], bank(name)[:, 0:256],
                                       ACT.Copy).then_inc(o_hi, 1)
            hi_static(6)
            hi_static(7)
            hi_static(8)

            def ffn_hi(h, i):
                hi(U_FFN + i, 16 * (U_FFN // RING_IN + h * (FFN_UNITS // RING_IN) + i // RING_IN + 1),
                   ffn_used(h, i))

            squares(1)
            ffn_hi(0, 0)
            norm_hi(1)
            with act.Fori(0, 2) as h:
                for i in range(HALF_F):
                    ffn_hi(h, i + 1)
                    b = 2 * (i % 2)
                    g = h * HALF_F + i
                    act.wait_ge(made, ffn_at(h, ("h1", i)))
                    act.wait_ge(f_mul, g + 1)
                    act.activation(TMP[:, 0, :], PS[:, b, :], ACT.Silu).then_inc(f_silu, 1)
                    act.wait_ge(f_mul, g + 2)
                    act.wait_ge(made, plan.ffn + h * len(FFN_MADE))
                    act.activation(GHI[:, i, :], TMP[:, 2 + i % 2, :], ACT.Copy).then_inc(f_hi, 1)
                for i in range(HALF_F + 1, FFN_UNITS):
                    ffn_hi(h, i)
                ffn_hi(h, FFN_UNITS)
            squares(2)
            norm_hi(2)
            act.wait_ge(spl, 2)
            act.activation(SPL[:, 1, :], SPL[:, 0, :], ACT.Exp, scale=-1.0).then_inc(spl, 1)
            act.wait_ge(spl, 4)
            act.activation(SPL[:, 3, :], SPL[:, 2, :], ACT.Ln).then_inc(spl, 1)
            hi_static(U_RG + 1)

            def rg_inputs(b, m):
                wait_full(act, ("u", b, m))
                if b:
                    act.wait_ge(rg_conv, 8 * b)
                act.wait_ge(rg_pad, 1)
                act.activation(UP[:, m, :, RG_LEFT:RG_LEFT + NC_TOK],
                               bank(("u", b, m)).rearrange("p (s t) -> p s t", s=2),
                               ACT.Copy).then_inc(rg_in, 1)

            def conv_hi(b, m):
                act.wait_ge(rg_conv, 8 * b + 4 * m + 4)
                if b:
                    wait_used(act, U_RG + 3 * b - 1)
                act.activation(UCHI[:, m, :], UC[:, m, :], ACT.Copy).then_inc(rg_uhi, 1)

            for m in range(2):
                rg_inputs(0, m)
            hi_static(U_RG + 2)
            for m in range(2):
                conv_hi(0, m)
            for b in range(RG_BLOCKS):
                u = U_RG + 3 * b
                for m in range(2):
                    wait_full(act, ("gate", b, m))
                    if b:
                        act.wait_ge(rg_ylo, 2 * b)
                    act.activation(GG[:, m, :], bank(("gate", b, m))[:, 0:NL_TOK],
                                   ACT.Gelu_apprx_tanh).then_inc(rg_gelu, 1)
                hi_static(u + 3)
                for n in range(4):
                    d, m = divmod(n, 2)
                    e, ch = 4 * b + n, 2 * b + m
                    wait_full(act, ("a", b, d, m))
                    if b:
                        act.wait_ge(rg_scan, e - 3)
                    act.activation(RT[:, n, :], bank(("a", b, d, m)), ACT.Sigmoid,
                                   bias=PAR[:, P_BA + 8 * d + ch:P_BA + 8 * d + ch + 1]).then_inc(rg_sig, 1)
                    wait_full(act, ("x", b, d, m))
                    act.activation(IT[:, n, :], bank(("x", b, d, m)), ACT.Sigmoid,
                                   bias=PAR[:, P_BX + 8 * d + ch:P_BX + 8 * d + ch + 1]).then_inc(rg_i, 1)
                hi_static(u + 4)
                for n in range(4):
                    lam8 = SPL[:, 7, 8 * (n // 2) + 2 * b + n % 2:8 * (n // 2) + 2 * b + n % 2 + 1]
                    act.wait_ge(rg_sig, 4 * b + n + 1)
                    act.activation(TH[:, n, :], RT[:, n, :], ACT.Tanh, scale=lam8).then_inc(rg_tanh, 1)
                    act.activation(RT[:, n, :], RT[:, n, :], ACT.Exp, scale=lam8).then_inc(rg_exp, 1)
                if b < RG_BLOCKS - 1:
                    for m in range(2):
                        rg_inputs(b + 1, m)
                hi_static(u + 5)
                if b < RG_BLOCKS - 1:
                    for m in range(2):
                        conv_hi(b + 1, m)
                for n in range(4):
                    act.wait_ge(rg_w, 4 * b + n + 1)
                    act.activation(TH[:, n, :], TH[:, n, :], ACT.Sqrt, scale=-1.0).then_inc(rg_root, 1)
                for m in range(2):
                    act.wait_ge(rg_y, 2 * b + m + 1)
                    act.activation(YHI[:, 2 * b + m, :], GG[:, m, :], ACT.Copy).then_inc(rg_yhi, 1)
            hi_static(N_UNITS - 1)
            squares(3)
            act.wait_ge(rt, 2)
            act.activation(GV[:, :, 1:2], GV[:, :, 0:1], ACT.Exp).then_inc(rt_exp, 1)
            for i in range(4):
                wait_full(act, ("h2", i))
                act.activation(H2HI[:, i // 2, 512 * (i % 2):512 * (i % 2) + 512], bank(("h2", i)),
                               ACT.Copy).then_inc(h2_hi, 1)
            act.wait_ge(rt_done, 1)
            rounds = act.value_load(EXI[0:1, 15:16], min_val=N_EXP, max_val=MAX_ROUNDS)

            def hi_e(r, j, c, used):
                act.wait_ge(raw_in[c], RAW_BASE[c] + 16 * (r * NJ + j + 1))
                act.wait_ge(e_made, used)
                act.activation(WHI[:, c % RING, :], RAW[:, c, :], ACT.Copy).then_inc(e_hi, 1)

            def gathered(at):
                for i in range(2):
                    act.wait_ge(e_made, at[i])
                    act.activation(XS[:, 512 * i:512 * i + 512], PS[:, 6 + i, :], ACT.Copy).then_inc(xs_ready, 1)

            def transposed(at):
                for i in range(2):
                    act.wait_ge(e_made, at[i])
                    act.activation(XTHI[:, 4 * i:4 * i + 4, :],
                                   PS[:, 5 + i, :].rearrange("p (k s) -> p k s", s=SLOTS),
                                   ACT.Copy).then_inc(xt_hi, 1)

            def out_hi(r):
                act.wait_ge(gs_ready, r + 1)
                act.wait_ge(y_lo, 2 * r + 1)
                act.wait_ge(e_made, round_at(r - 1, M_U41))
                for i in range(2):
                    act.activation(YR[:, i, :], PS[:, 2 + i, :], ACT.Copy, scale=GS[:]).then_inc(y_f, 1)
                for i in range(2):
                    act.wait_ge(y_f, 2 * r + i + 1)
                    act.activation(YRHI[:, i, :], YR[:, i, :], ACT.Copy).then_inc(y_hi, 1)

            wait_full(act, "pos")
            gathered((4, 8))
            transposed((12, 16))
            with act.Fori(0, rounds) as r:
                for c in range(3):
                    hi_e(r, 0, c, round_at(r - 1, (M_JU[5] + J_MADE * (NJ - 2), M_U40, M_U41)[c]))
                out_hi(r)
                for c in range(3, 5):
                    hi_e(r, 0, c, round_at(r, M_U0 + c - 3))

                def silu(j, at):
                    act.wait_ge(e_made, at)
                    act.wait_ge(m_mul, r * NJ + j + 1)
                    act.activation(SG[:], PS[:, 0, :], ACT.Silu).then_inc(m_silu, 1)

                def gt_hi(j, at):
                    act.wait_ge(e_made, at)
                    act.activation(GTHI[:], PS[:, 4, :].rearrange("p (c s) -> p c s", s=SLOTS),
                                   ACT.Copy).then_inc(m_gthi, 1)

                silu(0, round_at(r, M_U0 + 1))
                hi_e(r, 0, 5, round_at(r, M_U0 + 2))
                with act.Fori(0, NJ - 1) as j:
                    used = [round_at(r, n + J_MADE * j) for n in (M_LOOP - 1, *M_JU[:5])]
                    hi_e(r, j + 1, 0, used[0])
                    hi_e(r, j + 1, 1, used[1])
                    gt_hi(j, round_at(r, M_JT + J_MADE * j))
                    hi_e(r, j + 1, 2, used[2])
                    silu(j + 1, round_at(r, M_JU[1] + J_MADE * j))
                    for c in range(3, 6):
                        hi_e(r, j + 1, c, used[c])
                gathered((round_at(r, M_X), round_at(r, M_X + 1)))
                gt_hi(NJ - 1, round_at(r, M_GT))
                transposed((round_at(r, M_XT), round_at(r, M_XT + 1)))
            out_hi(rounds)

        @block.vector
        def _(dve):
            def lo(slot_u, at):
                s = slot_u % RING
                dve.wait_ge(w_hi, at + 1)
                c = unit_cols(slot_u)
                dve.tensor_tensor(WLO[:, s, 0:c], RAW[:, s, 0:c], WHI[:, s, 0:c].bitcast(F32),
                                  ALU.subtract).then_inc(w_lo, 1)

            def lo_static(u):
                if u < N_UNITS and not U_FFN <= u < U_RG:
                    lo(u, u)

            def ada_col(a):
                dve.wait_ge(ada_rowT, a + 1)
                g, layer = a % 12, a // 12
                dst = MC[:, layer, 4 * g:4 * g + 4, :]
                view = PS[:, 7, :].rearrange("p (c j s) -> p c s j", c=4, j=4)[:, :, 0:2, :]
                dve.tensor_reduce(dst, view, AX.X, ALU.add).then_inc(ada_cols, 1)
                dve.wait_ge(ada_cols, a + 1)
                bias = PAR[:, P_ADAB + 48 * layer + 4 * g:P_ADAB + 48 * layer + 4 * g + 4]
                for s in range(2):
                    dve.tensor_tensor(dst[:, :, s], dst[:, :, s], bias, ALU.add).then_inc(ada_sum, 1)

            def coefs(n):
                layer, which = n // 2, SC1 if n % 2 == 0 else SC2
                dve.wait_ge(ada_sum, 8 if n == 0 else 2 * ADA_GROUPS)
                gain = PAR[:, (P_N1 if n % 2 == 0 else P_N2) + 8 * layer:][:, 0:8]
                for s in range(2):
                    dve.scalar_tensor_tensor(CA[:, n, :, s], MC[:, layer, 8 * which:8 * which + 8, s], 1.0, gain,
                                             ALU.add, ALU.mult).then_inc(coef, 1)

            def norm(n):
                layer, sh = n // 2, (SH1 if n % 2 == 0 else SH2)
                dve.wait_ge(root, n + 1)
                w = T if n < 3 else NL_TOK
                dve.reciprocal(RSTD[:, 0:w], RSTD[:, 0:w]).then_inc(rstd, 1)
                dve.wait_ge(coef, 2 * n + 2)
                for k in range(KD):
                    g = n * KD + k
                    dve.wait_ge(xr, g + 1)
                    if n < 3:
                        src = TMP[:, k % 4, :]
                        for s in range(2):
                            cols = slice(256 * s, 256 * s + 256)
                            dve.tensor_scalar(src[:, cols], src[:, cols], CA[:, n, k, s:s + 1],
                                              MC[:, layer, 8 * sh + k, s:s + 1], ALU.mult, ALU.add).then_inc(mod, 1)
                        dve.wait_ge(h_hi, g + 1)
                        dve.wait_ge(mod, 2 * (g + 1))
                        dve.tensor_tensor(HLO[:, k, :], src, HHI[:, k, :].bitcast(F32), ALU.subtract).then_inc(h_lo, 1)
                    else:
                        dve.tensor_scalar(H2T[:, k, :], H2T[:, k, :], CA[:, n, k, 1:2],
                                          MC[:, layer, 8 * sh + k, 1:2], ALU.mult, ALU.add).then_inc(mod, 1)

            dve.wait_ge(in_par, 16)
            dve.wait_ge(in_const, 16)
            lo_static(0)
            lo_static(1)
            lo_static(2)
            for a in range(4):
                ada_col(a)
            coefs(0)
            norm(0)
            dve.wait_ge(lat_root, 1)
            dve.reciprocal(RSTD[:], RSTD[:]).then_inc(lat_rstd, 1)
            dve.wait_ge(lat_rstd, 1)
            for i in range(2):
                name = f"qa{i}"
                dve.wait_ge(lat_sq, i + 1)
                dve.scalar_tensor_tensor(TMP[:, i, :], bank(name), PAR[:, P_GQ + i:P_GQ + i + 1], RSTD[:],
                                         ALU.mult, ALU.mult).then_inc(cq_f, 1)
                dve.wait_ge(cq_f, i + 1)
                dve.wait_ge(cq_hi, i + 1)
                dve.tensor_tensor(CQLO[:, i, :], TMP[:, i, :], CQHI[:, i, :].bitcast(F32),
                                  ALU.subtract).then_inc(cq_lo, 1)
            dve.wait_ge(lat_root, 2)
            dve.reciprocal(RSTD[:], RSTD[:]).then_inc(lat_rstd, 1)
            dve.wait_ge(lat_rstd, 2)
            dve.wait_ge(lat_sq, 3)
            dve.scalar_tensor_tensor(TMP[:, 2, :], bank("ckv"), PAR[:, P_GKV:P_GKV + 1], RSTD[:],
                                     ALU.mult, ALU.mult).then_inc(cq_f, 1)
            dve.wait_ge(cq_f, 3)
            dve.wait_ge(cq_hi, 3)
            dve.tensor_tensor(CKLO[:], TMP[:, 2, :], CKHI[:].bitcast(F32), ALU.subtract).then_inc(cq_lo, 1)
            dve.wait_ge(lat_sq, 4)
            dve.tensor_scalar(KPE[:], bank("pe"), PAR[:, P_GKR:P_GKR + 1], None, ALU.mult).then_inc(kpe_step, 1)
            wait_full(dve, "swap k")
            dve.wait_ge(cq_lo, 3)
            dve.tensor_tensor(TMP[:, 0, :], bank("swap k"), SIN, ALU.mult).then_inc(kpe_step, 1)
            dve.tensor_tensor(KPE[:], KPE[:], COS, ALU.mult).then_inc(kpe_step, 1)
            dve.wait_ge(kpe_step, 3)
            dve.tensor_tensor(KPE[:], KPE[:], TMP[:, 0, :], ALU.add).then_inc(kpe_step, 1)
            dve.tensor_tensor(GQK, PAR[:, P_GQN:P_GQN + 1], PAR[:, P_GKN:P_GKN + 1],
                              ALU.mult).then_inc(gqk_ready, 1)
            lo_static(3)
            lo_static(4)
            for i in range(1, 8, 2):
                wait_full(dve, ("v", i))
                dve.tensor_copy(V[:, i // 2, 512:1024], bank(("v", i))).then_inc(v_b, 1)
            lo_static(5)
            for p in range(PAIRS):
                dve.wait_ge(hd_sq, 5 * p + 3)
                if p:
                    wait_full(dve, ("score1", p - 1, 3))
                dve.tensor_scalar(QR[:], bank(("qr", p)), PAR[:, P_GQR:P_GQR + 1], None,
                                  ALU.mult).then_inc(qr_step, 1)
                ada_col(ada_group(p, 0))
                wait_full(dve, ("swap q", p))
                dve.wait_ge(hd_sum, 4 * p + 2)
                dve.tensor_tensor(TMP[:, 2, :], bank(("swap q", p)), SIN, ALU.mult).then_inc(qr_step, 1)
                dve.tensor_tensor(QR[:], QR[:], COS, ALU.mult).then_inc(qr_step, 1)
                dve.wait_ge(qr_step, 4 * p + 3)
                dve.tensor_tensor(QR[:], QR[:], TMP[:, 2, :], ALU.add).then_inc(qr_step, 1)
                dve.wait_ge(qr_step, 4 * p + 4)
                for i in range(2):
                    half = slice(64 * i, 64 * i + 64)
                    n = 4 * p + i
                    dve.wait_ge(hd_root, n + 1)
                    dve.reciprocal(RSTD[:], RSTD[:]).then_inc(hd_rstd, 1)
                    dve.wait_ge(hd_rstd, n + 1)
                    dve.tensor_tensor(QN[:, i, :], bank((f"qn{i}", p)), RSTD[:], ALU.mult).then_inc(q_ready, 1)
                    dve.tensor_tensor(QR[half, :], QR[half, :], RSTD[half, :], ALU.mult).then_inc(q_ready, 1)
                ada_col(ada_group(p, 1))
                dve.wait_ge(gqk_ready, 1)
                for i in range(2):
                    half = slice(64 * i, 64 * i + 64)
                    n = 4 * p + 2 + i
                    dve.wait_ge(hd_root, n + 1)
                    dve.reciprocal(RSTD[:], RSTD[:]).then_inc(hd_rstd, 1)
                    dve.wait_ge(hd_rstd, n + 1)
                    dve.scalar_tensor_tensor(KN[:, i, :], bank((f"kn{i}", p)), GQK, RSTD[:],
                                             ALU.mult, ALU.mult).then_inc(k_ready, 1)
                    dve.tensor_tensor(KR[half, :], KPE[half, :], RSTD[half, :], ALU.mult).then_inc(k_ready, 1)
                ada_col(ada_group(p, 2))
                for i in range(5):
                    it = 4 * p + i
                    if i < 4:
                        nk = NC_TOK if i % 2 == 0 else T
                        for j in range(2):
                            name = (f"score{j}", p, i)
                            wait_full(dve, name)
                            dve.tensor_reduce(MX[:, j:j + 1], bank(name)[:, 0:nk], AX.X, ALU.max).then_inc(s_max, 1)
                            dve.wait_ge(s_max, 2 * it + j + 1)
                            if it:
                                dve.wait_ge(s_exp, 2 * it - 1 + j)
                            dve.tensor_scalar(NM[:, j:j + 1], MX[:, j:j + 1], -(QK ** -0.5), None,
                                              ALU.mult).then_inc(s_neg, 1)
                        for j in range(2):
                            dve.wait_ge(s_exp, 2 * it + j + 1)
                            dve.reciprocal(RI[:, j:j + 1], SM[:, j:j + 1]).then_inc(s_rec, 1)
                            dve.wait_ge(s_rec, 2 * it + j + 1)
                            dve.tensor_scalar(PR[:, j, 0:nk], PR[:, j, 0:nk], RI[:, j:j + 1], None,
                                              ALU.mult).then_inc(s_prob, 1)
                    if i in (1, 3):
                        ada_col(ada_group(p, 3 + i // 2))
                    if i:
                        h, g = 2 * p + (i - 1) // 2, (i - 1) % 2
                        nk = NC_TOK if g == 0 else T
                        name = ("PT1", p, i - 1)
                        wait_full(dve, name)
                        if it > 1:
                            wait_full(dve, ("att", (it - 2) // 4, (it - 2) % 4))
                        dve.tensor_copy(PT[:, 0:nk // P, P:2 * P],
                                        bank(name)[:, 0:nk].rearrange("p (k q) -> p k q", q=P)).then_inc(pt_b, 1)
                        name = ("att", p, i - 1)
                        dve.wait_ge(o_hi, it)
                        dve.tensor_tensor(HLO[:, h, 256 * g:256 * g + 256], bank(name)[:, 0:256],
                                          HHI[:, h, 256 * g:256 * g + 256].bitcast(F32),
                                          ALU.subtract).then_inc(o_lo, 1)
            lo_static(6)
            lo_static(7)
            for n in range(1, 4):
                coefs(n)

            def residual(name_bank, m, layer, part, streams, then, w=256):
                for s in streams:
                    cols = slice(256 * s, 256 * s + 256)
                    src = name_bank[:, cols] if len(streams) == 2 else name_bank[:, 0:256]
                    dve.scalar_tensor_tensor(X[:, m, cols], src, MC[:, layer, 8 * part + m, s:s + 1],
                                             X[:, m, cols], ALU.mult, ALU.add).then_inc(then, 1)

            for m in range(KD):
                wait_full(dve, ("o", m))
                residual(bank(("o", m)), m, 0, GA1, (0, 1), x_mid[0])
                if m == 1:
                    lo_static(8)
            lo(U_FFN, U_FFN)
            norm(1)
            with dve.Fori(0, 2) as h:
                for i in range(HALF_F):
                    lo(U_FFN + i + 1, U_FFN + h * FFN_UNITS + i + 1)
                    b = 2 * (i % 2)
                    g = h * HALF_F + i
                    dve.wait_ge(f_silu, g + 1)
                    dve.wait_ge(made, ffn_at(h, ("h3", i)))
                    dve.tensor_tensor(TMP[:, 2 + i % 2, :], TMP[:, 0, :], PS[:, b + 1, :],
                                      ALU.mult).then_inc(f_mul, 1)
                    dve.wait_ge(f_mul, g + 2)
                    dve.wait_ge(f_hi, g + 1)
                    dve.tensor_tensor(GLO[:, i, :], TMP[:, 2 + i % 2, :], GHI[:, i, :].bitcast(F32),
                                      ALU.subtract).then_inc(f_lo, 1)
                q = HALF_F + 1
                for m in range(KD):
                    end = HALF_F + ((m + 1) * HALF_F - 1) // W2_UNIT_TILES
                    while q < FFN_UNITS and q <= end + 1:
                        lo(U_FFN + q, U_FFN + h * FFN_UNITS + q)
                        q += 1
                    if m == KD - 1:
                        lo(U_RG, U_FFN + (h + 1) * FFN_UNITS)
                    b = 4 + m % 2
                    dve.wait_ge(made, ffn_at(h, ("y", m)))
                    residual(PS[:, b, :], m, 0, GA2, (0, 1), f_x)
            norm(2)
            LAM = PAR[:, P_LAM:P_LAM + 16]
            dve.tensor_scalar(SPL[:, 5, :], LAM, -1.0, None, ALU.mult).then_inc(spl, 1)
            dve.wait_ge(spl, 1)
            dve.tensor_tensor(SPL[:, 0, :], LAM, SPL[:, 5, :], ALU.max).then_inc(spl, 1)
            dve.wait_ge(spl, 3)
            dve.tensor_scalar(SPL[:, 2, :], SPL[:, 1, :], 1.0, None, ALU.add).then_inc(spl, 1)
            dve.wait_ge(spl, 5)
            dve.tensor_scalar(SPL[:, 4, :], SPL[:, 2, :], -1.0, None, ALU.add).then_inc(spl, 1)
            dve.wait_ge(spl, 6)
            dve.tensor_scalar(SPL[:, 6, :], SPL[:, 4, :], 0.0, None, ALU.is_equal).then_inc(spl, 1)
            dve.wait_ge(spl, 7)
            dve.tensor_tensor(SPL[:, 4, :], SPL[:, 4, :], SPL[:, 6, :], ALU.add).then_inc(spl, 1)
            dve.tensor_tensor(SPL[:, 3, :], SPL[:, 3, :], SPL[:, 6, :], ALU.add).then_inc(spl, 1)
            dve.wait_ge(spl, 9)
            dve.reciprocal(SPL[:, 4, :], SPL[:, 4, :]).then_inc(spl, 1)
            dve.tensor_tensor(SPL[:, 3, :], SPL[:, 3, :], SPL[:, 1, :], ALU.mult).then_inc(spl, 1)
            dve.wait_ge(spl, 11)
            dve.tensor_tensor(SPL[:, 3, :], SPL[:, 3, :], SPL[:, 4, :], ALU.mult).then_inc(spl, 1)
            dve.tensor_scalar(SPL[:, 5, :], SPL[:, 5, :], 0.0, None, ALU.max).then_inc(spl, 1)
            dve.wait_ge(spl, 13)
            dve.tensor_tensor(SPL[:, 3, :], SPL[:, 3, :], SPL[:, 5, :], ALU.add).then_inc(spl, 1)
            dve.wait_ge(spl, 14)
            dve.tensor_scalar(SPL[:, 7, :], SPL[:, 3, :], -RG_C, None, ALU.mult).then_inc(spl, 1)
            dve.wait_ge(spl, 15)
            dve.memset(UP[:], 0.0).then_inc(rg_pad, 1)
            lo_static(U_RG + 1)

            def convolve(b, m):
                ch, n = 2 * b + m, 8 * b + 4 * m
                dve.wait_ge(rg_in, 2 * b + m + 1)
                ucv = UC[:, m, :].rearrange("p (s t) -> p s t", s=2)
                cw = [PAR[:, P_CW + 8 * k + ch:P_CW + 8 * k + ch + 1] for k in range(RG_CONV)]
                if b:
                    dve.wait_ge(rg_iu, 4 * b)
                    dve.wait_ge(rg_uhi, 2 * b)
                dve.tensor_scalar(ucv, UP[:, m, :, 0:NC_TOK], cw[0], PAR[:, P_CB + ch:P_CB + ch + 1],
                                  ALU.mult, ALU.add).then_inc(rg_conv, 1)
                for k in range(1, RG_CONV):
                    dve.wait_ge(rg_conv, n + k)
                    dve.scalar_tensor_tensor(ucv, UP[:, m, :, k:k + NC_TOK], cw[k], ucv,
                                             ALU.mult, ALU.add).then_inc(rg_conv, 1)

            def conv_lo(b, m):
                dve.wait_ge(rg_conv, 8 * b + 4 * m + 4)
                dve.wait_ge(rg_uhi, 2 * b + m + 1)
                dve.tensor_tensor(UCLO[:, m, :], UC[:, m, :], UCHI[:, m, :].bitcast(F32),
                                  ALU.subtract).then_inc(rg_ulo, 1)

            for m in range(2):
                convolve(0, m)
            lo_static(U_RG + 2)
            for m in range(2):
                conv_lo(0, m)
            for b in range(RG_BLOCKS):
                u = U_RG + 3 * b
                lo_static(u + 3)
                lo_static(u + 4)
                if b < RG_BLOCKS - 1:
                    convolve(b + 1, 0)
                for n in range(4):
                    dve.wait_ge(rg_tanh, 4 * b + n + 1)
                    dve.wait_ge(rg_sq, 4 * b + n + 1)
                    dve.scalar_tensor_tensor(TH[:, n, :], SQ[:, n, :], 1.0, TH[:, n, :], ALU.add,
                                             ALU.mult).then_inc(rg_w, 1)
                if b < RG_BLOCKS - 1:
                    convolve(b + 1, 1)
                lo_static(u + 5)
                if b < RG_BLOCKS - 1:
                    for m in range(2):
                        conv_lo(b + 1, m)
                for n in range(4):
                    e, m = 4 * b + n, n % 2
                    dve.wait_ge(rg_root, e + 1)
                    dve.wait_ge(rg_iu, e + 1)
                    dve.tensor_tensor(IT[:, n, :], IT[:, n, :], TH[:, n, :], ALU.mult).then_inc(rg_b, 1)
                for n in range(4):
                    e, m = 4 * b + n, n % 2
                    dve.wait_ge(rg_b, e + 1)
                    dve.wait_ge(rg_w, e + 1)
                    if n < 2:
                        if b:
                            dve.wait_ge(rg_y, 2 * b)
                        dve.tensor_tensor_scan(HS[:, m, :], RT[:, n, :], IT[:, n, :], 0.0, ALU.mult,
                                               ALU.add).then_inc(rg_scan, 1)
                    else:
                        c, l = slice(0, NC_TOK), LAT
                        dve.tensor_tensor_scan(SQ[:, n, c][:, ::-1], RT[:, n, c][:, ::-1], IT[:, n, c][:, ::-1],
                                               0.0, ALU.mult, ALU.add).then_inc(rg_back, 1)
                        dve.wait_ge(rg_back, 2 * b + m + 1)
                        dve.tensor_tensor_scan(SQ[:, n, l][:, ::-1], RT[:, n, l][:, ::-1], IT[:, n, l][:, ::-1],
                                               SQ[:, n, 0:1], ALU.mult, ALU.add).then_inc(rg_scan, 1)
                for n in range(2, 4):
                    m = n % 2
                    dve.wait_ge(rg_scan, 4 * b + n + 1)
                    dve.tensor_tensor(SQ[:, n, LAT], SQ[:, n, LAT], HS[:, m, LAT], ALU.add).then_inc(rg_sum, 1)
                for n in range(2, 4):
                    m = n % 2
                    dve.wait_ge(rg_sum, 2 * b + m + 1)
                    dve.wait_ge(rg_gelu, 2 * b + m + 1)
                    dve.tensor_tensor(GG[:, m, :], GG[:, m, :], SQ[:, n, LAT], ALU.mult).then_inc(rg_y, 1)
                for m in range(2):
                    dve.wait_ge(rg_yhi, 2 * b + m + 1)
                    dve.tensor_tensor(YLO[:, 2 * b + m, :], GG[:, m, :], YHI[:, 2 * b + m, :].bitcast(F32),
                                      ALU.subtract).then_inc(rg_ylo, 1)
            for m in range(KD):
                if m == 2:
                    lo_static(N_UNITS - 1)
                wait_full(dve, ("rg o", m))
                residual(bank(("rg o", m)), m, 1, GA1, (1,), x_mid[1])
            norm(3)
            wait_full(dve, "logits")
            dve.tensor_copy(LT[:], bank("logits")[0:N_EXP, 0:NL_TOK]).then_inc(lt_ready, 1)
            wait_full(dve, "logits T")
            c = [0]

            def step(ins):
                c[0] += 1
                ins.then_inc(rt_step, 1)
                dve.wait_ge(rt_step, c[0])

            step(dve.tensor_copy(LG[:], bank("logits T")[:, 0:2 * N_EXP].rearrange("p (t e) -> p t e", t=2)))
            for t in range(2):
                step(dve.max(M8[:, t, :], LG[:, t, :]))
                step(dve.max_index(IX[:, t, :], M8[:, t, :], LG[:, t, :]))
                dve.tensor_tensor(GV[:, t, 0:1], M8[:, t, 1:2], M8[:, t, 0:1], ALU.subtract).then_inc(rt, 1)
            step(dve.tensor_copy(IXF[:], IX[:]))
            dve.wait_ge(rt_exp, 1)
            step(dve.tensor_scalar(GV[:, :, 2:3], GV[:, :, 1:2], 1.0, None, ALU.add))
            step(dve.reciprocal(GV[:, :, 2:3], GV[:, :, 2:3]))
            step(dve.tensor_tensor(GV[:, :, 3:4], GV[:, :, 1:2], GV[:, :, 2:3], ALU.mult))
            IOTA8 = IOTA[:, 0:N_EXP]
            for t in range(2):
                step(dve.tensor_scalar(MK1[:, t, :], IOTA8, IXF[:, t, 0:1], None, ALU.is_equal))
                step(dve.tensor_scalar(MK2[:, t, :], IOTA8, IXF[:, t, 1:2], None, ALU.is_equal))
                step(dve.tensor_tensor(SEL[:, t, :], MK1[:, t, :], MK2[:, t, :], ALU.add))
                step(dve.tensor_scalar(MK1[:, t, :], MK1[:, t, :], GV[:, t, 2:3], None, ALU.mult))
                step(dve.scalar_tensor_tensor(CMB[:, t, :], MK2[:, t, :], GV[:, t, 3:4], MK1[:, t, :],
                                              ALU.mult, ALU.add))
            assert c[0] == SEL_STEPS
            step(dve.memset(RP[:], -1.0))
            step(dve.memset(RG[:], 0.0))
            wait_full(dve, "pos")
            dve.tensor_copy(POS[:], bank("pos")[:, 0:24].rearrange("p (a e) -> p a e", a=3)).then_inc(pos_ready, 1)
            dve.wait_ge(pos_ready, 1)
            FAR = 8192.0
            for t in range(2):
                step(dve.scalar_tensor_tensor(POS[:, t, :], POS[:, t, :], FAR, SEL[:, t, :], ALU.add, ALU.mult))
                step(dve.tensor_scalar(POS[:, t, :], POS[:, t, :], -FAR, None, ALU.add))
                step(dve.tensor_copy(RP[:, t, 0:N_EXP], POS[:, t, :]))
                step(dve.tensor_copy(RG[:, t, 0:N_EXP], CMB[:, t, :]))
            step(dve.memset(EX[:], 0.0))
            step(dve.tensor_copy(EX[:, 0:N_EXP], IOTA8))
            step(dve.tensor_scalar(OVR[:, 0, :], POS[:, 2, :], float(SLOTS), None, ALU.is_gt))
            step(dve.tensor_tensor_scan(OVR[:, 1, :], ONES[:, 0:N_EXP], OVR[:, 0, :], 0.0, ALU.mult, ALU.add))
            step(dve.tensor_scalar(EX[:, 15:16], OVR[:, 1, N_EXP - 1:N_EXP], float(N_EXP), None, ALU.add))
            step(dve.tensor_tensor(OVR[:, 1, :], OVR[:, 1, :], OVR[:, 0, :], ALU.subtract))
            for n in range(MAX_OVER):
                step(dve.scalar_tensor_tensor(OVR[:, 2, :], OVR[:, 1, :], float(n), OVR[:, 0, :],
                                              ALU.is_equal, ALU.mult))
                col = N_EXP + n
                for src, dst in ((POS[:, 0, :], RP[:, 0, col:col + 1]), (POS[:, 1, :], RP[:, 1, col:col + 1]),
                                 (CMB[:, 0, :], RG[:, 0, col:col + 1]), (CMB[:, 1, :], RG[:, 1, col:col + 1]),
                                 (IOTA8, EX[:, col:col + 1])):
                    step(dve.tensor_tensor(OVR[:, 3, :], OVR[:, 2, :], src, ALU.mult))
                    step(dve.tensor_reduce(dst, OVR[:, 3, :], AX.X, ALU.add))
            step(dve.tensor_scalar(RP[:, :, N_EXP:N_EXP + MAX_OVER], RP[:, :, N_EXP:N_EXP + MAX_OVER],
                                   -float(SLOTS), None, ALU.add))
            dve.tensor_copy(EXI[:], EX[:]).then_inc(rt_done, 1)
            for i in range(4):
                dve.wait_ge(h2_hi, i + 1)
                cols = slice(512 * (i % 2), 512 * (i % 2) + 512)
                dve.tensor_tensor(H2LO[:, i // 2, cols], bank(("h2", i)), H2HI[:, i // 2, cols].bitcast(F32),
                                  ALU.subtract).then_inc(h2_lo, 1)
            dve.wait_ge(rt_done, 1)
            rounds = dve.value_load(EXI[0:1, 15:16], min_val=N_EXP, max_val=MAX_ROUNDS)

            def lo_e(r, j, c):
                dve.wait_ge(e_hi, r * EXP_UNITS + 6 * j + c + 1)
                dve.tensor_tensor(WLO[:, c % RING, :], RAW[:, c, :], WHI[:, c % RING, :].bitcast(F32),
                                  ALU.subtract).then_inc(e_lo, 1)

            def pick(cols):
                for t in range(2):
                    dve.tensor_scalar(G[:, t, :], IOTA, RP[:, t, cols], None, ALU.is_equal).then_inc(g_ready, 1)

            def transposed_lo(n):
                for i in range(2):
                    dve.wait_ge(xt_hi, 2 * n + i + 1)
                    dve.tensor_tensor(XTLO[:, 4 * i:4 * i + 4, :],
                                      PS[:, 5 + i, :].rearrange("p (k s) -> p k s", s=SLOTS),
                                      XTHI[:, 4 * i:4 * i + 4, :].bitcast(F32), ALU.subtract).then_inc(xt_lo, 1)

            wait_full(dve, "pos")
            pick(slice(0, 1))
            transposed_lo(0)
            dve.wait_ge(acc, 1)

            def add_out(r, first):
                for i, b in enumerate((6, 7, 5, 4)):
                    dve.wait_ge(e_made, round_at(r, first + i))
                    if i == 0:
                        dve.wait_ge(acc, 4 * r + 1)
                    part = ACC[:, 2 * i:2 * i + 2, :]
                    dve.tensor_tensor(part, part, PS[:, b, :].rearrange("p (k t) -> p k t", k=2),
                                      ALU.add).then_inc(acc, 1)

            with dve.Fori(0, rounds) as r:
                for c in range(3):
                    lo_e(r, 0, c)
                dve.wait_ge(e_made, round_at(r, M_GATE))
                dve.wait_ge(gt_ready, r + 1)
                dve.tensor_copy(GTN[:], PS[:, 7, 0:NL_TOK]).then_inc(gtn_ready, 1)
                dve.wait_ge(y_f, 2 * r + 2)
                dve.tensor_copy(GS[:], PS[:, 7, NL_TOK:NL_TOK + 1]).then_inc(gs_ready, 1)
                for c in range(3, 6):
                    lo_e(r, 0, c)

                def mul(j, at):
                    dve.wait_ge(m_silu, r * NJ + j + 2)
                    dve.wait_ge(e_made, at)
                    dve.tensor_tensor(GM[:], SG[:], PS[:, 1, :], ALU.mult).then_inc(m_mul, 1)

                def gt_lo(j):
                    dve.wait_ge(m_gthi, r * NJ + j + 1)
                    dve.tensor_tensor(GTLO[:], PS[:, 4, :].rearrange("p (c s) -> p c s", s=SLOTS),
                                      GTHI[:].bitcast(F32), ALU.subtract).then_inc(m_gtlo, 1)

                mul(0, round_at(r, M_U0 + 3))
                pick(bass.ds(r + 1, 1))
                add_out(r, M_OUT)
                dve.wait_ge(gtn_ready, r + 1)
                dve.tensor_copy(GTR[:], GTN[:]).then_inc(gt_ready, 1)
                with dve.Fori(0, NJ - 1) as j:
                    lo_e(r, j + 1, 0)
                    lo_e(r, j + 1, 1)
                    gt_lo(j)
                    for c in range(2, 5):
                        lo_e(r, j + 1, c)
                    mul(j + 1, round_at(r, M_JU[3] + J_MADE * j))
                    lo_e(r, j + 1, 5)
                gt_lo(NJ - 1)
                transposed_lo(r + 1)
            add_out(rounds, 0)
            dve.wait_ge(acc, 4 * rounds + 5)
            for m in range(KD):
                dve.scalar_tensor_tensor(ACC[:, m, :], ACC[:, m, :], MC[:, 1, 8 * GA2 + m, 1:2],
                                         X[:, m, LAT], ALU.mult, ALU.add).then_inc(fin, 1)

        @block.tensor
        def _(pe):
            def three(out, whi, wlo, mhi, mlo, first, last):
                pe.matmul(out, whi, mhi, start=first, stop=False)
                pe.matmul(out, whi, mlo, start=False, stop=False)
                return pe.matmul(out, wlo, mhi, start=False, stop=last)

            def tile(u, i):
                s = u % RING
                return WHI[:, s, P * i:P * i + P], WLO[:, s, P * i:P * i + P]

            def wait_unit(u):
                pe.wait_ge(w_lo, u + 1)

            at = [0]

            def start(name):
                assert plan.order[name] == at[0], name
                at[0] += 1
                if plan.before[name]:
                    pe.wait_ge(*bank_read(name))

            def ada(a):
                if a:
                    pe.wait_ge(ada_cols, a)
                pe.wait_ge(cs_ready, 1)
                for part in range(2):
                    n = 2 * a + part
                    pe.wait_ge(ada_in[n % ADA_RING], 16 * (n // ADA_RING + 1))
                    for j in range(4):
                        ins = pe.matmul(PS[32 * j:32 * j + 32, 7, :], CS[:, 4 * part + j, :],
                                        RAW[:, ADA_SLOT + n % ADA_RING, 512 * j:512 * j + 512],
                                        start=part == 0, stop=part == 1, skip_group_check=True)
                    ins.then_inc(ada_used, 1)

            def ada_turn(a):
                pe.wait_ge(ada_row, a + 1)
                for c in range(4):
                    ins = pe.transpose(PS[:, 7, P * c:P * c + P], ROW[:, P * c:P * c + P], IDENT)
                ins.then_inc(ada_rowT, 1)

            def sums(n):
                w = toks(n).stop - toks(n).start
                start(("ss", n))
                for k in range(KD):
                    pe.wait_ge(sq_done, n * KD + k + 1)
                    ins = pe.matmul(bank(("ss", n))[:, 0:w], ONES, TMP[:, k % 2, 0:w], start=k == 0,
                                    stop=k == KD - 1)
                    ins.then_inc(sq_used if k < KD - 1 else made, 1)

            def project(name, u, first_tile, mhi, mlo, n_k, cols=slice(0, T), chunk_ready=None):
                start(name)
                w = cols.stop - cols.start
                for k in range(n_k):
                    if chunk_ready:
                        pe.wait_ge(chunk_ready[0], chunk_ready[1] + k + 1)
                    hi_t, lo_t = tile(u, first_tile + k)
                    ins = three(bank(name)[:, 0:w], hi_t, lo_t, mhi[:, k, cols], mlo[:, k, cols], k == 0,
                                k == n_k - 1)
                ins.then_inc(made, 1)

            def one(name, out, lhsT, rhs):
                start(name)
                pe.matmul(out, lhsT, rhs, start=True, stop=True).then_inc(made, 1)

            pe.wait_ge(in_par, 16)
            pe.wait_ge(in_const, 16)
            for a in range(4):
                ada(a)
                ada_turn(a)
            sums(0)
            wait_unit(U_Q)
            for m in range(2):
                project(f"qa{m}", U_Q, KD * m, HHI, HLO, KD, chunk_ready=(h_lo, 0))
            wait_unit(U_KV)
            for m, name in enumerate(("ckv", "pe")):
                project(name, U_KV, KD * m, HHI, HLO, KD)
            start("ss q")
            for i in range(2):
                pe.wait_ge(lat_sq, i + 1)
                ins = pe.matmul(bank("ss q"), ONES, TMP[:, i, :], start=i == 0, stop=i == 1)
            ins.then_inc(made, 1)
            pe.wait_ge(lat_sq, 3)
            one("ss kv", bank("ss kv"), ONES, TMP[:, 2, :])
            pe.wait_ge(kpe_step, 1)
            one("swap k", bank("swap k"), PERM, KPE[:])
            wait_unit(U_V)
            pe.wait_ge(cq_lo, 3)
            for i in range(8):
                start(("v", i))
                toks_i = slice(P * (i // 2), P * (i // 2) + P)
                w = slice(512 * (i % 2), 512 * (i % 2) + 512)
                s = ring(U_V)
                three(bank(("v", i)), CKHI[:, toks_i], CKLO[:, toks_i], WHI[:, s, w], WLO[:, s, w], True,
                      True).then_inc(made, 1)
            for p in range(PAIRS):
                u, t0 = U_HEADS + p // 2, 8 * (p % 2)
                wait_unit(u)
                if p:
                    pe.wait_ge(s_prob, 8 * p)
                project(("qn0", p), u, t0, CQHI, CQLO, KQ)
                project(("qn1", p), u, t0 + 2, CQHI, CQLO, KQ)
                project(("qr", p), u, t0 + 4, CQHI, CQLO, KQ)
                for i in range(2):
                    name = (f"kn{i}", p)
                    start(name)
                    hi_t, lo_t = tile(u, t0 + 6 + i)
                    three(bank(name), hi_t, lo_t, CKHI[:], CKLO[:], True, True).then_inc(made, 1)
                ada(ada_group(p, 0))
                ada_turn(ada_group(p, 0))
                for i in range(2):
                    pe.wait_ge(hd_sum, 4 * p + i + 1)
                    one((f"ss q{i}", p), bank((f"ss q{i}", p)), ONES, TMP[:, i, :])
                pe.wait_ge(qr_step, 4 * p + 1)
                one(("swap q", p), bank(("swap q", p)), PERM, QR[:])
                ada(ada_group(p, 1))
                ada_turn(ada_group(p, 1))
                for i in range(2):
                    pe.wait_ge(hd_sum, 4 * p + 2 + i + 1)
                    one((f"ss k{i}", p), bank((f"ss k{i}", p)), ONES, TMP[:, i, :])
                ada(ada_group(p, 2))
                ada_turn(ada_group(p, 2))
                pe.wait_ge(q_ready, 4 * p + 4)
                pe.wait_ge(k_ready, 4 * p + 4)
                for i in range(5):
                    it = 4 * p + i
                    if i < 4:
                        g, hh = i % 2, i // 2
                        nk = NC_TOK if g == 0 else T
                        half = slice(64 * hh, 64 * hh + 64)
                        for j in range(2):
                            name = (f"score{j}", p, i)
                            start(name)
                            q = slice(256 * g + P * j, 256 * g + P * j + P)
                            pe.matmul(bank(name)[:, 0:nk], QN[:, hh, q], KN[:, hh, 0:nk], start=True, stop=False)
                            pe.matmul(bank(name)[:, 0:nk], QR[half, q], KR[half, 0:nk], start=False,
                                      stop=True).then_inc(made, 1)
                    if i:
                        it -= 1
                        g, h = (i - 1) % 2, 2 * p + (i - 1) // 2
                        nk = NC_TOK if g == 0 else T
                        for j in range(2):
                            name = (f"PT{j}", p, i - 1)
                            start(name)
                            pe.wait_ge(s_prob, 2 * it + j + 1)
                            for k in range(nk // P):
                                ins = pe.transpose(bank(name)[:, P * k:P * k + P], PR[:, j, P * k:P * k + P], IDENT)
                            ins.then_inc(made, 1)
                        if i in (1, 3):
                            ada(ada_group(p, 3 + i // 2))
                            ada_turn(ada_group(p, 3 + i // 2))
                        name = ("att", p, i - 1)
                        start(name)
                        pe.wait_ge(pt_a, it + 1)
                        pe.wait_ge(pt_b, it + 1)
                        for k in range(nk // P):
                            ins = pe.matmul(bank(name)[:, 0:256], V[:, k, DV * h:DV * h + DV], PT[:, k, :],
                                            start=k == 0, stop=k == nk // P - 1)
                        ins.then_inc(made, 1)
            for m in range(KD):
                if m % 2 == 0:
                    wait_unit(U_O + m // 2)
                pe.wait_ge(o_lo, 2 * HEADS)
                project(("o", m), U_O + m // 2, KD * (m % 2), HHI, HLO, KD)
            sums(1)
            assert at[0] == plan.ffn
            pe.wait_ge(h_lo, KD + 1)
            with pe.Fori(0, 2) as h:
                for i in range(HALF_F):
                    pe.wait_ge(w_lo, U_FFN + h * FFN_UNITS + i + 1)
                    b = 2 * (i % 2)
                    for o in range(2):
                        ago = h * HALF_F + i - 1
                        if i >= 2:
                            pe.wait_ge((f_silu, f_mul)[o], ago + o)
                        elif i == 0 and o == 0:
                            pe.wait_ge(f_mul, h * HALF_F + 1)
                        for k in range(KD):
                            if i == 0 and o == 0:
                                pe.wait_ge(h_lo, KD + k + 1)
                            hi_t, lo_t = tile(U_FFN + i, KD * o + k)
                            ins = three(PS[:, b + o, :], hi_t, lo_t, HHI[:, k, :], HLO[:, k, :], k == 0,
                                        k == KD - 1)
                        ins.then_inc(made, 1)
                for t in range(KD * HALF_F):
                    m, k = divmod(t, HALF_F)
                    q, c = divmod(t, W2_UNIT_TILES)
                    if c == 0:
                        pe.wait_ge(w_lo, U_FFN + h * FFN_UNITS + HALF_F + q + 1)
                    if m == 0:
                        pe.wait_ge(f_lo, h * HALF_F + k + 1)
                    if k == 0 and m < 2:
                        pe.wait_ge(f_x, 2 * KD * h + 1)
                    elif k == 0:
                        pe.wait_ge(f_x, 2 * KD * h + 2 * (m - 1) + 1)
                    hi_t, lo_t = tile(U_FFN + HALF_F + q, c)
                    ins = three(PS[:, 4 + m % 2, :], hi_t, lo_t, GHI[:, k, :], GLO[:, k, :], k == 0,
                                k == HALF_F - 1)
                    if k == HALF_F - 1 or c == W2_UNIT_TILES - 1:
                        ins.then_inc(made, 1)
            at[0] += 2 * len(FFN_MADE)
            sums(2)
            for b in range(RG_BLOCKS):
                u = U_RG + 3 * b
                wait_unit(u)
                for m in range(2):
                    project(("u", b, m), u, KD * m, HHI, HLO, KD,
                            chunk_ready=(h_lo, 2 * KD) if b == 0 else None)
                wait_unit(u + 1)
                for m in range(2):
                    project(("gate", b, m), u + 1, KD * m, HHI, HLO, KD, cols=LAT)
                wait_unit(u + 2)
                pe.wait_ge(rg_ulo, 2 * b + 2)
                for d in range(2):
                    for m in range(2):
                        for o, name in enumerate("ax"):
                            project((name, b, d, m), u + 2, 2 * (2 * (2 * d + m) + o), UCHI, UCLO, 2)
            pe.wait_ge(rg_ylo, KD)
            for m in range(KD):
                if m % 2 == 0:
                    wait_unit(U_RGO + m // 2)
                project(("rg o", m), U_RGO + m // 2, KD * (m % 2), YHI, YLO, KD, cols=slice(0, NL_TOK))
            sums(3)
            start("logits")
            for k in range(KD):
                pe.wait_ge(mod, 6 * KD + k + 1)
                ins = pe.matmul(bank("logits")[0:N_EXP, 0:NL_TOK], PAR[:, P_RW + N_EXP * k:P_RW + N_EXP * (k + 1)],
                                H2T[:, k, :], start=k == 0, stop=k == KD - 1)
            ins.then_inc(made, 1)
            start("logits T")
            pe.wait_ge(lt_ready, 1)
            for t in range(2):
                ins = pe.transpose(bank("logits T")[:, N_EXP * t:N_EXP * t + N_EXP], LT[:, P * t:P * t + P],
                                   IDENT[0:N_EXP, 0:N_EXP])
            ins.then_inc(made, 1)
            for i in range(4):
                start(("h2", i))
                for k in range(4):
                    ins = pe.transpose(bank(("h2", i))[:, P * k:P * k + P],
                                       H2T[:, 4 * (i % 2) + k, P * (i // 2):P * (i // 2) + P], IDENT)
                ins.then_inc(made, 1)
            start("pos")
            pe.wait_ge(rt_step, SEL_STEPS)
            o = bank("pos")
            pe.matmul(o[:, 0:8], TRI, SEL[:, 0, :], start=True, stop=True)
            pe.matmul(o[:, 8:16], ONES, SEL[:, 0, :], start=True, stop=False)
            pe.matmul(o[:, 8:16], TRI, SEL[:, 1, :], start=False, stop=True)
            pe.matmul(o[:, 16:24], ONES, SEL[:, 0, :], start=True, stop=False)
            pe.matmul(o[:, 16:24], ONES, SEL[:, 1, :], start=False, stop=True).then_inc(made, 1)
            pe.wait_ge(rt_done, 1)
            rounds = pe.value_load(EXI[0:1, 15:16], min_val=N_EXP, max_val=MAX_ROUNDS)

            def gather(n, peel):
                pe.wait_ge(g_ready, 2 * n + 2)
                for i in range(2):
                    cols = slice(512 * i, 512 * i + 512)
                    for t in range(2):
                        for x, part in enumerate((H2HI, H2LO)):
                            last = t == 1 and x == 1
                            ins = pe.matmul(PS[:, 6 + i, :], G[:, t, :], part[:, t, cols],
                                            start=t == 0 and x == 0, stop=last)
                            if last or peel:
                                ins.then_inc(e_made, 1)

            def gather_turn(n, peel):
                for i in range(2):
                    pe.wait_ge(xs_ready, 2 * n + i + 1)
                    for k in range(4):
                        ins = pe.transpose(PS[:, 5 + i, P * k:P * k + P],
                                           XS[:, P * (4 * i + k):P * (4 * i + k) + P], IDENT)
                        if peel:
                            ins.then_inc(e_made, 1)
                    if not peel:
                        ins.then_inc(e_made, 1)

            pe.wait_ge(h2_lo, 4)
            pe.wait_ge(ada_cols, ADA_GROUPS)
            pe.wait_ge(pos_ready, 1)
            pe.wait_ge(zeros_ready, 1)
            def open_sums():
                for i in range(2):
                    pe.matmul(PS[:, 2 + i, :], ZERO[:, 0:P], ZERO[:], start=True, stop=False,
                              skip_group_check=True)

            def scatter(r):
                pe.wait_ge(gt_ready, r + 1)
                pe.wait_ge(y_lo, 2 * r + 3)
                pe.wait_ge(xt_lo, 2 * r + 2)
                for i, b in enumerate((6, 7, 5, 4)):
                    for f in range(2):
                        d = 2 * i + f
                        cols = slice(P * (d % 4), P * (d % 4) + P)
                        pe.matmul(PS[:, b, 256 * f:256 * f + 256], YRHI[:, d // 4, cols], GTR[:], start=True,
                                  stop=False)
                        ins = pe.matmul(PS[:, b, 256 * f:256 * f + 256], YRLO[:, d // 4, cols], GTR[:],
                                        start=False, stop=True)
                    ins.then_inc(e_made, 1)

            open_sums()
            gather(0, True)
            gather_turn(0, True)
            with pe.Fori(0, rounds) as r:
                for t in range(2):
                    pe.transpose(PS[:, 7, P * t:P * t + P], G[:, t, :].bitcast(F32), IDENT)
                for t in range(2):
                    ins = pe.matmul(PS[:, 7, NL_TOK:NL_TOK + 1], G[:, t, :].bitcast(F32), RG[:, t, bass.ds(r, 1)],
                                    start=t == 0, stop=t == 1)
                ins.then_inc(e_made, 1)
                pe.wait_ge(xt_lo, 2 * r + 2)

                def up(j, o, c0):
                    for c in (c0, c0 + 1):
                        pe.wait_ge(e_lo, r * EXP_UNITS + j * 6 + c + 1)
                        if c == c0:
                            pe.wait_ge((m_silu, m_mul)[o], r * NJ + (j if c0 < 4 else j + 1) + 1)
                        s = c % RING
                        for k in range(4):
                            kk = 4 * (c - c0) + k
                            cols = slice(512 * k, 512 * k + 512)
                            ins = three(PS[:, o, :], XTHI[:, kk, :], XTLO[:, kk, :], WHI[:, s, cols],
                                        WLO[:, s, cols], kk == 0, kk == KD - 1)
                        ins.then_inc(e_made, 1)

                def turn(j, waits_gt):
                    pe.wait_ge(m_mul, r * NJ + j + 2)
                    pe.wait_ge(m_gtlo, r * NJ + j + 1)
                    pe.wait_ge(acc, 4 * r + 5)
                    for c in range(4):
                        ins = pe.transpose(PS[:, 4, P * c:P * c + P], GM[:, P * c:P * c + P], IDENT)
                    ins.then_inc(e_made, 1)

                def down(j, j_unit, c0):
                    pe.wait_ge(m_gtlo, r * NJ + j + 2)
                    for c in (c0, c0 + 1):
                        pe.wait_ge(e_lo, r * EXP_UNITS + j_unit * 6 + c + 1)
                        s = c % RING
                        for f in range(2):
                            fc = 2 * (c - c0) + f
                            for i in range(2):
                                cols = slice(1024 * f + 512 * i, 1024 * f + 512 * i + 512)
                                out_i = PS[:, 2 + i, :]
                                hi_g, lo_g = GTHI[:, fc, :], GTLO[:, fc, :]
                                pe.matmul(out_i, hi_g, WHI[:, s, cols], start=False, stop=False,
                                          skip_group_check=True)
                                pe.matmul(out_i, hi_g, WLO[:, s, cols], start=False, stop=False,
                                          skip_group_check=True)
                                ins = pe.matmul(out_i, lo_g, WHI[:, s, cols], start=False, stop=False,
                                                skip_group_check=True)
                        ins.then_inc(e_made, 1)

                up(0, 0, 0)
                up(0, 1, 2)
                pe.wait_ge(gs_ready, r + 2)
                scatter(r)
                pe.wait_ge(y_f, 2 * r + 2)
                open_sums()
                with pe.Fori(0, NJ - 1) as j:
                    up(j, 0, 4)
                    turn(j, True)
                    up(j, 1, 6)
                    down(j, j, 8)
                gather(r + 1, False)
                turn(NJ - 1, True)
                gather_turn(r + 1, False)
                down(NJ - 1, NJ - 1, 4)
            scatter(rounds)


RAW_BASE = [16 * len(range(c, N_UNITS, RING_IN)) if c < RING_IN else 0 for c in range(RAW_SLOTS)]


def tiles(w):
    k, m = w.shape
    return w.reshape(k // P, P, m // P, P).transpose(0, 2, 1, 3)


def unit(ts):
    u = np.zeros((P, UW), np.float32)
    for i, t in enumerate(ts):
        u[:, P * i:P * i + t.shape[1]] = t
    return u


def weight_units(w_dq, w_uq, w_dkv, w_ukv, w_o, f1, f3, f2, g_in, g_gate, w_a, w_x, g_out):
    units = []
    t = tiles(w_dq)
    units.append(unit([t[k, m] for m in range(2) for k in range(KD)]))
    pe2 = np.concatenate([w_dkv, w_dkv[:, P:]], 1)
    t = tiles(pe2)
    units.append(unit([t[k, m] for m in range(2) for k in range(KD)]))
    ukv = w_ukv.reshape(P, HEADS, NOPE + DV)
    units.append(unit(list(ukv[:, :, NOPE:].transpose(1, 0, 2))))
    uq = w_uq.reshape(KQ, P, HEADS, QK)
    heads = []
    for p in range(PAIRS):
        for h in (2 * p, 2 * p + 1):
            heads += [uq[k, :, h, :NOPE] for k in range(KQ)]
        heads += [np.concatenate([uq[k, :, 2 * p, NOPE:], uq[k, :, 2 * p + 1, NOPE:]], 1) for k in range(KQ)]
        heads += [ukv[:, h, :NOPE] for h in (2 * p, 2 * p + 1)]
    units += [unit(heads[:TPU]), unit(heads[TPU:])]
    t = tiles(w_o)
    units += [unit([t[k, m] for m in (i, i + 1) for k in range(KD)]) for i in range(0, KD, 2)]
    t1, t3, t2 = tiles(f1), tiles(f3), tiles(f2)
    for h in range(2):
        fs = range(HALF_F * h, HALF_F * (h + 1))
        units += [unit([t1[k, f] for k in range(KD)] + [t3[k, f] for k in range(KD)]) for f in fs]
        down = [t2[f, m] for m in range(KD) for f in fs]
        units += [unit(down[i:i + W2_UNIT_TILES]) for i in range(0, len(down), W2_UNIT_TILES)]
    ti, tg = tiles(g_in), tiles(g_gate)
    for b in range(RG_BLOCKS):
        units.append(unit([ti[k, m] for m in (2 * b, 2 * b + 1) for k in range(KD)]))
        units.append(unit([tg[k, m] for m in (2 * b, 2 * b + 1) for k in range(KD)]))
        units.append(unit([tiles(w[d, b])[k, m] for d in range(2) for m in range(2) for w in (w_a, w_x)
                           for k in range(2)]))
    t = tiles(g_out)
    units += [unit([t[k, m] for m in (i, i + 1) for k in range(KD)]) for i in range(0, KD, 2)]
    return np.stack(units)


def expert_units(w1, w3, w2):
    def up(w):
        return (w.reshape(N_EXP, 2, 4, P, NJ, FB).transpose(0, 4, 1, 3, 2, 5)).reshape(N_EXP, NJ, 2, P, UW)
    a, b = up(w1), up(w3)
    d = w2.reshape(N_EXP, NJ, 2, 2, P, D).transpose(0, 1, 2, 4, 3, 5).reshape(N_EXP, NJ, 2, P, UW)
    out = np.empty((N_EXP, EXP_UNITS, P, UW), np.float32)
    out[:, 0:2], out[:, 2:4] = a[:, 0], b[:, 0]
    for j in range(1, NJ):
        u = 4 + 6 * (j - 1)
        out[:, u:u + 2], out[:, u + 2:u + 4], out[:, u + 4:u + 6] = a[:, j], b[:, j], d[:, j - 1]
    out[:, EXP_UNITS - 2:] = d[:, NJ - 1]
    return out.reshape(N_EXP * EXP_UNITS, P, UW)


def constants():
    c = np.zeros((P, N_CONST), np.float32)
    i = np.arange(P)
    c[:, C_ID:C_ID + P] = np.eye(P)
    swap = i ^ 32
    c[swap, C_PERM + i] = 1.0
    c[:, C_ONE:C_ONE + P] = 1.0
    c[:, C_TRI:C_TRI + P] = i[:, None] < i[None, :]
    c[:, C_IOTA:C_IOTA + P] = i[None, :]
    n_freq = ROPE // 4
    inv = (np.float32(ROPE_BASE) ** (-np.arange(n_freq, dtype=np.float32) / np.float32(n_freq))).astype(np.float32)
    t = np.arange(NL_TOK)
    row, col = (t // GRID_W).astype(np.float32), (t % GRID_W).astype(np.float32)
    ang = np.concatenate([row[:, None] * inv, col[:, None] * inv], 1).astype(np.float32)
    cos, sin = np.cos(ang).T, np.sin(ang).T
    c[:, C_COS:C_COS + NC_TOK] = 1.0
    c[:, C_COS + NC_TOK:C_COS + T] = np.tile(cos, (4, 1))
    c[:, C_SIN + NC_TOK:C_SIN + T] = np.concatenate([-sin, sin, -sin, sin], 0)
    return c


def columns(v):
    return np.ascontiguousarray(v.reshape(-1, P).T)


def kernel(**inputs):
    import concourse.bacc as bacc
    from concourse.bass_utils import run_bass_kernel_spmd

    a = {k: np.asarray(v) for k, v in inputs.items()}
    xs = np.concatenate([a["ctx"][0], a["x"][0]], 0)
    x_t = np.ascontiguousarray(xs.T.reshape(KD, P, T))
    par = np.concatenate([
        np.stack([columns(a["c_ctx"]), columns(a["c"][0])], -1).reshape(P, 16),
        columns(a["ada_b"]), columns(a["norm1_g"]), columns(a["norm2_g"]),
        columns(a["mla_g_q"][0]), columns(a["mla_g_kv"][0]),
        columns(a["mla_g_qn"][0, :NOPE]), columns(a["mla_g_kn"][0, :NOPE]),
        columns(np.tile(a["mla_g_qn"][0, NOPE:], 2)), columns(np.tile(a["mla_g_kn"][0, NOPE:], 2)),
        columns(a["rg_conv_w"][0]), columns(a["rg_conv_b"][0]), columns(a["rg_b_a"][0]), columns(a["rg_b_x"][0]),
        columns(a["rg_lam"][0]),
        a["moe_w_router"][0].reshape(KD, P, N_EXP).transpose(1, 0, 2).reshape(P, KD * N_EXP)], 1)
    ada_w = np.ascontiguousarray(a["ada_w"].reshape(2, 2, 4, P, 12, 512).transpose(0, 4, 1, 3, 2, 5)).reshape(
        2 * ADA_GROUPS, P, UW)
    w_units = weight_units(a["mla_w_dq"][0], a["mla_w_uq"][0], a["mla_w_dkv"][0], a["mla_w_ukv"][0],
                           a["mla_w_o"][0], a["ffn_w1"][0], a["ffn_w3"][0], a["ffn_w2"][0], a["rg_w_in"][0],
                           a["rg_w_gate"][0], a["rg_w_a"][0], a["rg_w_x"][0], a["rg_w_out"][0])
    moe_w = expert_units(a["moe_w1"][0], a["moe_w3"][0], a["moe_w2"][0])
    arrays = {"x_t": x_t, "consts": constants(), "params": np.ascontiguousarray(par), "ada_w": ada_w,
              "w_units": w_units, "moe_w": moe_w}
    nc = bacc.Bacc("TRN2", target_bir_lowering=False, num_devices=1)
    aps = {k: nc.dram_tensor(k, v.shape, mybir.dt.from_np(v.dtype), kind="ExternalInput").ap()
           for k, v in arrays.items()}
    out = nc.dram_tensor("out", [KD, P, NL_TOK], F32, kind="ExternalOutput").ap()
    dit_kernel(nc, *(aps[k] for k in ("x_t", "consts", "params", "ada_w", "w_units", "moe_w")), out)
    r = run_bass_kernel_spmd(nc, [arrays], core_ids=[0])
    got = r.results[0]["out"]
    return np.ascontiguousarray(got.transpose(2, 0, 1).reshape(1, NL_TOK, D))
```

```python
from contextlib import ExitStack

import numpy as np

import concourse.bass as bass
from concourse import mybir

ALU = mybir.AluOpType
ACT = mybir.ActivationFunctionType
AX = mybir.AxisListType
F32 = mybir.dt.float32
F32R = mybir.dt.float32r
I32 = mybir.dt.int32
U32 = mybir.dt.uint32

P = 128
D = 1024
KD = D // P
NC_TOK = 256
NL_TOK = 256
T = NC_TOK + NL_TOK
CTX = slice(0, NC_TOK)
LAT = slice(NC_TOK, T)
EPS = 1e-6
HEADS, Q_LORA, NOPE, ROPE, DV = 8, 256, 128, 64, 128
QK = NOPE + ROPE
KQ = Q_LORA // P
PAIRS = HEADS // 2
GRID_W = 64
ROPE_BASE = 10000.0
FFN = 2816
F_TILES = FFN // P
HALF_F = F_TILES // 2
RG_BLOCKS, RG_CONV, RG_LEFT, RG_C = 4, 4, 2, 8.0
N_EXP, EH = 8, 3584
FB = 512
NJ = EH // FB
SLOTS = P
MAX_OVER = 3
MAX_ROUNDS = N_EXP + MAX_OVER

UW = 2048
TPU = UW // P
RING_IN = 3
RING = 3
RAW_SLOTS = 6
ADA_SLOT = 3
ADA_RING = 2
TMP_SLOT = 5
ADA_GROUPS = 2 * 6 * D // 512
W2_UNIT_TILES = 13
W2_UNITS = -(-KD * HALF_F // W2_UNIT_TILES)
FFN_UNITS = HALF_F + W2_UNITS
U_KV, U_Q, U_V, U_HEADS, U_O, U_FFN = 0, 1, 2, 3, 5, 9
U_RG = U_FFN + 2 * FFN_UNITS
U_RGO = U_RG + 3 * RG_BLOCKS
N_UNITS = U_RGO + KD // 2
EXP_UNITS = NJ * 6

C_ID, C_PERM, C_ONE, C_TRI, C_IOTA, C_COS, C_SIN = 0, P, 2 * P, 3 * P, 4 * P, 5 * P, 5 * P + T
N_CONST = 5 * P + 2 * T
SEL_STEPS = 19
P_C, P_ADAB, P_N1, P_N2 = 0, 16, 112, 128
P_GQ, P_GKV, P_GQN, P_GKN, P_GQR, P_GKR = 144, 146, 147, 148, 149, 150
P_CW, P_CB, P_BA, P_BX, P_LAM, P_RW = 151, 183, 191, 207, 223, 239
N_PAR = P_RW + KD * N_EXP
SH1, SC1, GA1, SH2, SC2, GA2 = range(6)


class Plan:

    def __init__(self):
        self.bank, self.order, self.before, self.n = {}, {}, {}, 0
        last = {}

        def put(name, bank, reader, value):
            self.bank[name], self.order[name], self.before[name] = bank, self.n, last.get(bank)
            last[bank] = (reader, value)
            self.n += 1

        def head_products(q, c, part):
            if (c, part) == (0, 0):
                put(("qr", q), 6, "qr_step", 4 * q + 1)
                put(("qn0", q), 4, "q_ready", 4 * q + 1)
            elif (c, part) == (0, 1):
                put(("swap q", q), 5, "qr_step", 4 * q + 2)
            elif (c, part) == (1, 0):
                put(("ss q0", q), 5, "hd_root", 4 * q + 1)
                put(("qn1", q), 6, "q_ready", 4 * q + 3)
            elif (c, part) == (2, 0):
                put(("ss q1", q), 5, "hd_root", 4 * q + 2)
                put(("kn0", q), 4, "k_ready", 4 * q + 1)
            elif (c, part) == (3, 0):
                put(("ss k0", q), 5, "hd_root", 4 * q + 3)
                put(("kn1", q), 6, "k_ready", 4 * q + 3)
            elif (c, part) == (3, 1):
                put(("ss k1", q), 5, "hd_root", 4 * q + 4)

        put(("ss", 0), 6, "root", 1)
        put("ckv", 2, "cq_f", 1)
        put("pe", 3, "kpe_step", 1)
        put("qa0", 0, "cq_f", 2)
        put("ss kv", 5, "lat_root", 1)
        put("qa1", 1, "cq_f", 3)
        put("swap k", 6, "kpe_step", 2)
        put("ss q", 4, "lat_root", 2)
        for i in range(8):
            put(("v", i), (5, 2, 3, 6)[i % 4], "v_ready", i + 1)
        for c in range(4):
            head_products(0, c, 0)
            head_products(0, c, 1)
        for p in range(PAIRS):
            for i in range(4):
                it = 4 * p + i
                for j in range(2):
                    put((f"score{j}", p, i), j, "s_exp", 2 * it + j + 1)
                if p + 1 < PAIRS:
                    head_products(p + 1, i, 0)
                for j in range(2):
                    put((f"PT{j}", p, i), 2 + j, "pt_copy", 2 * it + j + 1)
                if p + 1 < PAIRS:
                    head_products(p + 1, i, 1)
                put(("att", p, i), 2, "o_lo", it + 1)
        for m in range(KD):
            put(("o", m), m % 4, "x_mid0", 2 * (m + 1))
        put(("ss", 1), 6, "root", 2)
        self.ffn = self.n
        self.n += 2 * len(FFN_MADE)
        last.update({0: ("f_silu", 2 * HALF_F), 1: ("f_mul", 2 * HALF_F + 1), 2: ("f_silu", 2 * HALF_F - 1),
                     3: ("f_mul", 2 * HALF_F), 4: ("f_x", 4 * KD - 1), 5: ("f_x", 4 * KD + 1)})
        put(("ss", 2), 6, "root", 3)
        for b in range(RG_BLOCKS):
            at = 12 * b
            for m in range(2):
                put(("u", b, m), (at + m) % 8, "rg_in", 2 * b + m + 1)
            for m in range(2):
                put(("gate", b, m), (at + 2 + m) % 8, "rg_gelu", 2 * b + m + 1)
            for n in range(4):
                d, m = divmod(n, 2)
                put(("a", b, d, m), (at + 4 + 2 * n) % 8, "rg_sig", 4 * b + n + 1)
                put(("x", b, d, m), (at + 5 + 2 * n) % 8, "rg_i", 4 * b + n + 1)
        for m in range(KD):
            put(("rg o", m), m, "x_mid1", m + 1)
        put(("ss", 3), 6, "root", 4)
        put("logits", 0, "lt_ready", 1)
        put("logits T", 1, "rt_step", 1)
        for i in range(4):
            put(("h2", i), 2 + i, "h2_lo", i + 1)
        put("pos", 6, "pos_ready", 1)


def ffn_made():
    done = []
    for i in range(HALF_F):
        done += [("h1", i), ("h3", i)]
    n = KD * HALF_F
    for t in range(n):
        if t % HALF_F == HALF_F - 1:
            done.append(("y", t // HALF_F))
        elif t % W2_UNIT_TILES == W2_UNIT_TILES - 1:
            done.append(("w2 unit", t // W2_UNIT_TILES))
    return {name: i for i, name in enumerate(done)}


FFN_MADE = ffn_made()
M_GATE, M_U0, M_OUT, M_LOOP, J_MADE = 0, 1, 5, 9, 7
M_JU = (M_LOOP, M_LOOP + 1, M_LOOP + 3, M_LOOP + 4, M_LOOP + 5, M_LOOP + 6)
M_JT = M_LOOP + 2
M_TAIL = M_LOOP + J_MADE * (NJ - 1)
M_X, M_GT, M_XT, M_U40, M_U41 = M_TAIL, M_TAIL + 2, M_TAIL + 3, M_TAIL + 5, M_TAIL + 6
ROUND_MADE = M_U41 + 1
PEEL_MADE = 16


def dit_kernel(nc, x_t, consts, params, ada_w, w_units, moe_w, out):
    plan = Plan()
    with ExitStack() as ctx:
        def sb(name, shape, dt=F32, scope=ctx):
            return scope.enter_context(nc.sbuf_tensor(name, shape, dt))

        def sem(name):
            return ctx.enter_context(nc.semaphore(name))

        PS = ctx.enter_context(nc.psum_tensor("PS", [P, 8, 512], F32))

        RAW = sb("RAW", [P, RAW_SLOTS, UW])
        WHI = sb("WHI", [P, RING, UW], F32R)
        WLO = sb("WLO", [P, RING, UW], F32R)
        X = sb("X", [P, KD, T])
        CONST = sb("CONST", [P, N_CONST])
        PAR = sb("PAR", [P, N_PAR])
        CS = sb("CS", [P, KD, 32])
        MC = sb("MC", [P, 2, 48, 2])
        CA = sb("CA", [P, 4, KD, 2])
        LAM8 = sb("LAM8", [P, 16])
        GE = sb("GE", [P, 16])
        GQK, EPSC, SPARE = GE[:, 0:1], GE[:, 1:2], GE[:, 8:16]
        RSTD = sb("RSTD", [P, T])
        ROW = sb("ROW", [P, 512])
        HHI = sb("HHI", [P, KD, T], F32R)
        HLO = sb("HLO", [P, KD, T], F32R)
        IDENT = CONST[:, C_ID:C_ID + P]
        PERM = CONST[:, C_PERM:C_PERM + P]
        ONES = CONST[:, C_ONE:C_ONE + P]
        TRI = CONST[:, C_TRI:C_TRI + P]
        IOTA = CONST[:, C_IOTA:C_IOTA + P]
        COS = CONST[:, C_COS:C_COS + T]
        SIN = CONST[:, C_SIN:C_SIN + T]
        TMP = RAW[:, TMP_SLOT, :].rearrange("p (s t) -> p s t", t=T)

        with ExitStack() as mla:
            def mb(name, shape, dt=F32):
                return sb(name, shape, dt, mla)
            CQHI = mb("CQHI", [P, KQ, T], F32R)
            CQLO = mb("CQLO", [P, KQ, T], F32R)
            CKHI = mb("CKHI", [P, T], F32R)
            CKLO = mb("CKLO", [P, T], F32R)
            V = mb("V", [P, 4, HEADS * DV])
            SPL = V[:, 0, 0:P].rearrange("p (i c) -> p i c", c=16)
            KPE = mb("KPE", [P, T])
            QN = mb("QN", [P, 2, T])
            QR = mb("QR", [P, T])
            KN = mb("KN", [P, 2, T])
            KR = mb("KR", [P, T])
            PR = mb("PR", [P, 2, T])
            PT = mb("PT", [P, 4, 256])
            SMALL = mb("SMALL", [P, 8])
            HEAD_SETS = ((RAW[:, 2, 0:2 * T].rearrange("p (i t) -> p i t", i=2), RAW[:, 0, 0:T],
                          RAW[:, 2, 2 * T:4 * T].rearrange("p (i t) -> p i t", i=2), RAW[:, 0, T:2 * T]),
                         (QN[:], QR[:], KN[:], KR[:]))
            MX, NM, SM, RI = (SMALL[:, 2 * i:2 * i + 2] for i in range(4))
        with ExitStack() as ffn:
            GHI = sb("GHI", [P, HALF_F, T], F32R, ffn)
            GLO = sb("GLO", [P, HALF_F, T], F32R, ffn)
        with ExitStack() as rg:
            def rb(name, shape, dt=F32):
                return sb(name, shape, dt, rg)
            SEG = NC_TOK + RG_CONV - 1
            UP = rb("UP", [P, 2, 2, SEG])
            UC = rb("UC", [P, 2, T])
            UCHI = rb("UCHI", [P, 2, T], F32R)
            UCLO = rb("UCLO", [P, 2, T], F32R)
            GG = rb("GG", [P, 2, 2, NL_TOK])
            SQ = rb("SQ", [P, 4, T])
            HS = rb("HS", [P, 2, T])
            YHI = rb("YHI", [P, KD, NL_TOK], F32R)
            YLO = rb("YLO", [P, KD, NL_TOK], F32R)
            RT = RAW[:, ADA_SLOT, :].rearrange("p (n t) -> p n t", t=T)
            IT = RAW[:, ADA_SLOT + 1, :].rearrange("p (n t) -> p n t", t=T)
            TH = TMP
        moe = ctx.enter_context(ExitStack())

        def eb(name, shape, dt=F32):
            return sb(name, shape, dt, moe)
        H2T = eb("H2T", [P, KD, NL_TOK])
        LT = eb("LT", [N_EXP, NL_TOK])
        LG = eb("LG", [P, 2, N_EXP])
        M8 = eb("M8", [P, 2, 8])
        IX = eb("IX", [P, 2, 8], U32)
        IXF = eb("IXF", [P, 2, 8])
        GV = eb("GV", [P, 2, 4])
        MK1 = eb("MK1", [P, 2, N_EXP])
        MK2 = eb("MK2", [P, 2, N_EXP])
        SEL = eb("SEL", [P, 2, N_EXP])
        CMB = eb("CMB", [P, 2, N_EXP])
        POS = eb("POS", [P, 3, N_EXP])
        OVR = eb("OVR", [P, 4, N_EXP])
        RP = eb("RP", [P, 2, 12])
        RG = eb("RG", [P, 2, 12])
        EX = eb("EX", [P, 16])
        EXI = eb("EXI", [P, 16], I32)
        G = eb("G", [P, 2, SLOTS], F32R)
        GTN = eb("GTN", [P, NL_TOK])
        GTR = eb("GTR", [P, NL_TOK], F32R)
        GS = eb("GS", [P, 1])
        XS = eb("XS", [P, D])
        SG = eb("SG", [P, FB])
        GM = eb("GM", [P, FB])
        GTHI = eb("GTHI", [P, 4, SLOTS], F32R)
        GTLO = eb("GTLO", [P, 4, SLOTS], F32R)
        XTHI = HHI[:, 0:2, :].rearrange("p a (b s) -> p (a b) s", s=SLOTS)
        XTLO = HLO[:, 0:2, :].rearrange("p a (b s) -> p (a b) s", s=SLOTS)
        YRHI = HHI[:, 2:4, :]
        YRLO = HLO[:, 2:4, :]
        H2HI = HHI[:, 4:8, :].rearrange("p (t a) b -> p t (a b)", t=2)
        H2LO = HLO[:, 4:8, :].rearrange("p (t a) b -> p t (a b)", t=2)
        YR = eb("YR", [P, 2, 512])
        ACC = eb("ACC", [P, KD, NL_TOK])
        ZERO = eb("ZERO", [P, 512], F32R)

        in_x, in_const, in_par = sem("in_x"), sem("in_const"), sem("in_par")
        raw_in = [sem(f"raw_in{i}") for i in range(RAW_SLOTS)]
        ada_in = [sem(f"ada_in{i}") for i in range(ADA_RING)]
        w_hi, w_lo, made = sem("w_hi"), sem("w_lo"), sem("made")
        e_hi, e_lo, e_made = sem("e_hi"), sem("e_lo"), sem("e_made")
        rt_step, pos_ready = sem("rt_step"), sem("pos_ready")
        rg_back, rg_sum = sem("rg_back"), sem("rg_sum")
        zeros_ready = sem("zeros_ready")
        cs_zero, cs_ready = sem("cs_zero"), sem("cs_ready")
        eps_ready = sem("eps_ready")
        ada_used, ada_row, ada_rowT, ada_cols = sem("ada_used"), sem("ada_row"), sem("ada_rowT"), sem("ada_cols")
        ada_sum = sem("ada_sum")
        coef = sem("coef")
        gqk_ready = sem("gqk_ready")
        sq_done, sq_sum, root, rstd = sem("sq_done"), sem("sq_sum"), sem("root"), sem("rstd")
        xr, mod, h_hi, h_lo = sem("xr"), sem("mod"), sem("h_hi"), sem("h_lo")
        lat_sq, lat_root, lat_rstd = sem("lat_sq"), sem("lat_root"), sem("lat_rstd")
        cq_f, cq_hi, cq_lo = sem("cq_f"), sem("cq_hi"), sem("cq_lo")
        kpe_step = sem("kpe_step")
        v_ready = sem("v_ready")
        hd_sq, hd_sum, hd_root, hd_rstd = sem("hd_sq"), sem("hd_sum"), sem("hd_root"), sem("hd_rstd")
        qr_step, q_ready, k_ready = sem("qr_step"), sem("q_ready"), sem("k_ready")
        s_max, s_neg, s_exp, s_rec, s_prob = (sem("s_max"), sem("s_neg"), sem("s_exp"), sem("s_rec"),
                                              sem("s_prob"))
        pt_copy, o_hi, o_lo = sem("pt_copy"), sem("o_hi"), sem("o_lo")
        x_mid = [sem(f"x_mid{i}") for i in range(2)]
        f_silu, f_mul, f_hi, f_lo, f_x = sem("f_silu"), sem("f_mul"), sem("f_hi"), sem("f_lo"), sem("f_x")
        spl = sem("spl")
        rg_pad, rg_in, rg_conv, rg_uhi, rg_ulo = (sem("rg_pad"), sem("rg_in"), sem("rg_conv"), sem("rg_uhi"),
                                                  sem("rg_ulo"))
        rg_gelu, rg_sig, rg_i, rg_exp, rg_tanh = (sem("rg_gelu"), sem("rg_sig"), sem("rg_i"), sem("rg_exp"),
                                                  sem("rg_tanh"))
        rg_iu, rg_sq, rg_w, rg_b, rg_scan = (sem("rg_iu"), sem("rg_sq"), sem("rg_w"), sem("rg_b"),
                                              sem("rg_scan"))
        rg_root, rg_y, rg_yhi, rg_ylo = (sem("rg_root"), sem("rg_y"), sem("rg_yhi"),
                                               sem("rg_ylo"))
        rt, rt_exp, rounds_ready, rt_done = sem("rt"), sem("rt_exp"), sem("rounds_ready"), sem("rt_done")
        lt_ready, h2_hi, h2_lo = sem("lt_ready"), sem("h2_hi"), sem("h2_lo")
        g_ready, gt_ready, gs_ready = sem("g_ready"), sem("gt_ready"), sem("gs_ready")
        gtn_ready = sem("gtn_ready")
        xs_ready, xt_hi, xt_lo = sem("xs_ready"), sem("xt_hi"), sem("xt_lo")
        m_silu, m_mul, m_gthi, m_gtlo = sem("m_silu"), sem("m_mul"), sem("m_gthi"), sem("m_gtlo")
        y_f, y_hi, y_lo, acc = sem("y_f"), sem("y_hi"), sem("y_lo"), sem("acc")
        fin, out_done = sem("fin"), sem("out_done")

        block = ctx.enter_context(nc.Block())

        reader_sems = {"root": root, "cq_f": cq_f, "kpe_step": kpe_step, "lat_root": lat_root, "v_ready": v_ready,
                       "q_ready": q_ready, "k_ready": k_ready, "qr_step": qr_step, "hd_root": hd_root,
                       "s_exp": s_exp, "pt_copy": pt_copy, "o_lo": o_lo, "x_mid0": x_mid[0],
                       "x_mid1": x_mid[1], "f_silu": f_silu, "f_mul": f_mul, "f_x": f_x, "rg_in": rg_in,
                       "rg_gelu": rg_gelu, "rg_sig": rg_sig, "rg_i": rg_i, "lt_ready": lt_ready,
                       "rt_step": rt_step, "h2_lo": h2_lo, "pos_ready": pos_ready}

        def bank(name):
            return PS[:, plan.bank[name], :]

        def bank_read(name):
            reader, value = plan.before[name]
            return reader_sems[reader], value

        def wait_full(eng, name):
            eng.wait_ge(made, plan.order[name] + 1)

        def wait_used(eng, u):
            eng.wait_ge(made, plan.order[LAST_OF_UNIT[u]] + 1)

        LAST_OF_UNIT = {U_Q: "qa1", U_KV: "pe", U_V: ("v", 7), U_HEADS: ("kn1", 1), U_HEADS + 1: ("kn1", 3)}
        for i in range(KD // 2):
            LAST_OF_UNIT[U_O + i] = ("o", 2 * i + 1)
            LAST_OF_UNIT[U_RGO + i] = ("rg o", 2 * i + 1)
        for i in range(RG_BLOCKS):
            LAST_OF_UNIT[U_RG + 3 * i] = ("u", i, 1)
            LAST_OF_UNIT[U_RG + 3 * i + 1] = ("gate", i, 1)
            LAST_OF_UNIT[U_RG + 3 * i + 2] = ("x", i, 1, 1)

        def ffn_at(h, name):
            return plan.ffn + h * len(FFN_MADE) + FFN_MADE[name] + 1

        def ffn_used(h, i):
            i -= RING
            if i < 0:
                h, i = h - 1, i + FFN_UNITS
            if i < HALF_F:
                return ffn_at(h, ("h3", i))
            q = i - HALF_F
            return ffn_at(h, ("y", KD - 1) if q == W2_UNITS - 1 else ("w2 unit", q))

        def round_at(r, n):
            return PEEL_MADE + ROUND_MADE * r + n + 1

        def ada_group(p, i):
            return 8 + 4 * p + i

        def ring(u):
            return u % RING

        def unit_cols(u):
            if u == U_V:
                return HEADS * DV
            if U_FFN <= u < U_RG:
                q = (u - U_FFN) % FFN_UNITS - HALF_F
                if q >= 0:
                    return P * min(W2_UNIT_TILES, KD * HALF_F - W2_UNIT_TILES * q)
            return UW

        def wait_x(eng, n, k):
            if n == 0:
                eng.wait_ge(in_x, 16)
            elif n == 1:
                eng.wait_ge(x_mid[0], 2 * (k + 1))
            elif n == 2:
                eng.wait_ge(f_x, 2 * (KD + k + 1) + 1)
            else:
                eng.wait_ge(x_mid[1], k + 1)

        def toks(n):
            return slice(0, T) if n < 3 else LAT

        @block.sync
        def _(sp):
            sp.dma_start(PAR[:], params).then_inc(in_par, 16)
            sp.dma_start(CONST[:], consts).then_inc(in_const, 16)

            def load(u, slot, cols, at, wait=True):
                if wait:
                    sp.wait_ge(w_hi, at - RING_IN + 1)
                    sp.wait_ge(w_lo, at - RING_IN + 1)
                sp.dma_start(RAW[:, slot, 0:cols], u[:, 0:cols]).then_inc(raw_in[slot], 16)

            for u in range(U_FFN):
                if u < U_HEADS:
                    sp.wait_ge(ada_used, 2 + 2 * u)
                if u == U_O + 1:
                    sp.wait_ge(made, plan.order[("score1", 2, 3)] + 1)
                load(w_units[u], u % RING_IN, unit_cols(u), u, u >= RING_IN)
            with sp.Fori(0, 2) as h:
                for i in range(FFN_UNITS):
                    u = U_FFN + h * FFN_UNITS + i
                    load(w_units[bass.ds(u, 1)].rearrange("o p n -> p (o n)"), i % RING_IN,
                         unit_cols(U_FFN + i), u)
            for u in range(U_RG, N_UNITS):
                load(w_units[u], u % RING_IN, unit_cols(u), u, u >= RING_IN)

            def load_expert(e, r, j, c, wait=True):
                if wait:
                    sp.wait_ge(e_hi, r * EXP_UNITS + 6 * j + c - RAW_SLOTS + 1)
                    sp.wait_ge(e_lo, r * EXP_UNITS + 6 * j + c - RAW_SLOTS + 1)
                sp.dma_start(RAW[:, c, :], moe_w[bass.ds(e * EXP_UNITS + 6 * j + c, 1)].rearrange(
                    "o p n -> p (o n)")).then_inc(raw_in[c], 16)

            for c in range(RAW_SLOTS):
                if c == 0:
                    sp.wait_ge(w_hi, N_UNITS)
                    sp.wait_ge(w_lo, N_UNITS)
                if c == ADA_SLOT:
                    sp.wait_ge(rg_y, KD)
                if c == TMP_SLOT:
                    sp.wait_ge(root, 4)
                load_expert(0, 0, 0, c, wait=False)
            with sp.Fori(1, NJ) as j:
                for c in range(RAW_SLOTS):
                    load_expert(0, 0, j, c)
            sp.wait_ge(rounds_ready, 1)
            sp.wait_ge(rt_done, 1)
            rounds = sp.value_load(EXI[0:1, 15:16], min_val=N_EXP, max_val=MAX_ROUNDS)
            with sp.Fori(1, rounds) as r:
                e = sp.value_load(EXI[0:1, bass.ds(r, 1)], min_val=0, max_val=N_EXP - 1)
                with sp.Fori(0, NJ) as j:
                    for c in range(RAW_SLOTS):
                        load_expert(e, r, j, c)
            sp.wait_ge(fin, KD)
            sp.dma_start(out.rearrange("k p t -> p k t"), ACC[:]).then_inc(out_done, 16)
            sp.wait_ge(out_done, 16)

        def norm_scale(pool, n):
            pool.wait_ge(rstd, n + 1)
            for k in range(KD):
                g = n * KD + k
                if 4 <= g < 3 * KD:
                    pool.wait_ge(h_lo, g - 3)
                if n < 3:
                    wait_x(pool, n, k)
                    pool.tensor_tensor(TMP[:, k % 4, :], X[:, k, :], RSTD[:], ALU.mult).then_inc(xr, 1)
                else:
                    wait_x(pool, n, k)
                    pool.tensor_tensor(H2T[:, k, :], X[:, k, LAT], RSTD[:, 0:NL_TOK], ALU.mult).then_inc(xr, 1)

        @block.gpsimd
        def _(pool):
            pool.memset(CS[:], 0.0).then_inc(cs_zero, 1)
            pool.memset(EPSC, EPS).then_inc(eps_ready, 1)
            for i, from_one in enumerate((f_mul, f_x, m_silu, m_mul, m_gtlo, y_lo)):
                pool.memset(SPARE[:, i:i + 1], 0.0).then_inc(from_one, 1)
            def load_ada(n):
                if n < 2 * ADA_GROUPS:
                    if n >= ADA_RING:
                        pool.wait_ge(ada_used, n - ADA_RING + 1)
                    pool.dma_start(RAW[:, ADA_SLOT + n % ADA_RING, :],
                                   ada_w[n]).then_inc(ada_in[n % ADA_RING], 16)

            for n in range(2 * 4 + ADA_RING):
                load_ada(n)
                if n == ADA_RING - 1:
                    pool.dma_start(X[:], x_t.rearrange("k p t -> p k t")).then_inc(in_x, 16)
            norm_scale(pool, 0)
            for q in range(PAIRS):
                for n in range(4):
                    i, rope_sq = n % 2, TMP[:, 2 + n // 2, :]
                    half = slice(64 * i, 64 * i + 64)
                    pool.wait_ge(hd_sq, 5 * q + 2 + n)
                    pool.tensor_tensor(TMP[half, i, :], TMP[half, i, :], rope_sq[half, :],
                                       ALU.add).then_inc(hd_sum, 1)
                    for part in range(2):
                        load_ada(2 * ada_group(q - 1, n) + ADA_RING + part)
            for n in range(2 * ada_group(PAIRS - 1, 0) + ADA_RING, 2 * ADA_GROUPS):
                load_ada(n)
            norm_scale(pool, 1)
            norm_scale(pool, 2)
            pool.wait_ge(made, plan.order[("ss", 2)] + 1)
            pool.memset(UP[:], 0.0).then_inc(rg_pad, 1)
            for b in range(RG_BLOCKS):
                for m in range(2):
                    pool.wait_ge(rg_uhi, 2 * b + m + 1)
                    pool.tensor_tensor(UCLO[:, m, :], UC[:, m, :], UCHI[:, m, :].bitcast(F32),
                                       ALU.subtract).then_inc(rg_ulo, 1)
                for n in range(4):
                    e = 4 * b + n + 1
                    pool.wait_ge(rg_i, e)
                    pool.tensor_tensor(IT[:, n, :], IT[:, n, :], UC[:, n % 2, :], ALU.mult).then_inc(rg_iu, 1)
                for n in range(4):
                    e = 4 * b + n + 1
                    pool.wait_ge(rg_exp, e)
                    if b:
                        pool.wait_ge(rg_y, 2 * b)
                    pool.tensor_tensor(SQ[:, n, :], RT[:, n, :], RT[:, n, :], ALU.mult).then_inc(rg_sq, 1)
            norm_scale(pool, 3)
            pool.wait_ge(made, plan.order[("ss", 3)] + 1)
            pool.memset(ZERO[:].bitcast(F32), 0.0).then_inc(zeros_ready, 1)
            pool.memset(ACC[:], 0.0).then_inc(acc, 1)
            pool.memset(GTR[:].bitcast(F32), 0.0).then_inc(gt_ready, 1)
            pool.memset(GS[:], 0.0).then_inc(gs_ready, 1)
            pool.wait_ge(rounds_ready, 1)
            rounds = pool.value_load(EXI[0:1, 15:16], min_val=N_EXP, max_val=MAX_ROUNDS)

            def out_lo(r):
                for i in range(2):
                    pool.wait_ge(y_hi, 2 * r + i + 1)
                    pool.tensor_tensor(YRLO[:, i, :], YR[:, i, :], YRHI[:, i, :].bitcast(F32),
                                       ALU.subtract).then_inc(y_lo, 1)

            with pool.Fori(0, rounds) as r:
                out_lo(r)
            out_lo(rounds)

        @block.scalar
        def _(act):
            def hi(slot_u, n_in, used):
                s = slot_u % RING
                act.wait_ge(raw_in[s], n_in)
                if used is not None:
                    act.wait_ge(made, used)
                c = unit_cols(slot_u)
                act.activation(WHI[:, s, 0:c], RAW[:, s, 0:c], ACT.Copy).then_inc(w_hi, 1)

            def hi_static(u):
                if u < N_UNITS and not U_FFN <= u < U_RG:
                    hi(u, 16 * (u // RING_IN + 1),
                       None if u < RING else plan.order[LAST_OF_UNIT[u - RING]] + 1 if u != U_RG + 1 and
                       u != U_RG + 2 else ffn_used(2, u - U_RG))

            def squares(n):
                N = toks(n)
                w = N.stop - N.start
                for k in range(KD):
                    wait_x(act, n, k)
                    if k >= 3:
                        act.wait_ge(sq_sum, n * (KD - 1) + k - 2)
                    act.activation(TMP[:, k % 2 if k else 2, 0:w], X[:, k, N], ACT.Square).then_inc(sq_done, 1)

            def norm_root(n):
                w = toks(n).stop - toks(n).start
                wait_full(act, ("ss", n))
                act.wait_ge(eps_ready, 1)
                act.activation(RSTD[:, 0:w], bank(("ss", n))[:, 0:w], ACT.Sqrt, bias=EPSC,
                               scale=1.0 / D).then_inc(root, 1)

            def norm_hi(n):
                for k in range(KD):
                    act.wait_ge(mod, 2 * (n * KD + k + 1))
                    act.activation(HHI[:, k, :], TMP[:, k % 4, :], ACT.Copy).then_inc(h_hi, 1)

            def ada_copy(a):
                act.wait_ge(ada_used, 2 * a + 2)
                if a:
                    act.wait_ge(ada_rowT, a)
                act.activation(ROW[:], PS[:, 7, :], ACT.Copy).then_inc(ada_row, 1)

            act.wait_ge(in_par, 16)
            act.wait_ge(cs_zero, 1)
            act.activation(CS[:, :, 0:2], PAR[:, P_C:P_C + 16].rearrange("p (k s) -> p k s", s=2),
                           ACT.Silu).then_inc(cs_ready, 1)
            act.wait_ge(spl, 2)
            act.activation(SPL[:, 1, :], SPL[:, 0, :], ACT.Exp, scale=-1.0).then_inc(spl, 1)
            act.wait_ge(spl, 4)
            act.activation(SPL[:, 3, :], SPL[:, 2, :], ACT.Ln).then_inc(spl, 1)
            ada_copy(0)
            squares(0)
            ada_copy(1)
            norm_root(0)
            for a in range(2, 4):
                ada_copy(a)
            hi_static(0)
            norm_hi(0)
            hi_static(1)
            hi_static(2)

            def latent_squares(name, slot):
                wait_full(act, name)
                act.activation(TMP[:, slot, :], bank(name), ACT.Square).then_inc(lat_sq, 1)

            act.wait_ge(h_lo, KD)
            latent_squares("ckv", 2)
            latent_squares("pe", 3)
            latent_squares("qa0", 0)
            wait_full(act, "ss kv")
            act.wait_ge(xr, KD)
            act.activation(RSTD[:], bank("ss kv"), ACT.Sqrt, bias=EPSC, scale=1.0 / P).then_inc(lat_root, 1)
            hi_static(3)
            latent_squares("qa1", 1)
            act.wait_ge(cq_f, 1)
            act.activation(CKHI[:], TMP[:, 2, :], ACT.Copy).then_inc(cq_hi, 1)
            wait_full(act, "ss q")
            act.activation(RSTD[:], bank("ss q"), ACT.Sqrt, bias=EPSC, scale=1.0 / Q_LORA).then_inc(lat_root, 1)
            for i in range(8):
                wait_full(act, ("v", i))
                act.activation(V[:, i // 2, 512 * (i % 2):512 * (i % 2) + 512], bank(("v", i)),
                               ACT.Copy).then_inc(v_ready, 1)
                if i in (3, 5):
                    c = (3, 5).index(i)
                    act.wait_ge(cq_f, c + 2)
                    act.activation(CQHI[:, c, :], TMP[:, c, :], ACT.Copy).then_inc(cq_hi, 1)

            def head_squares(q, name, slot):
                wait_full(act, (name, q))
                act.activation(TMP[:, slot, :], bank((name, q)), ACT.Square).then_inc(hd_sq, 1)

            def head_root(q, name):
                wait_full(act, (name, q))
                act.activation(RSTD[:], bank((name, q)), ACT.Sqrt, bias=EPSC, scale=1.0 / QK).then_inc(hd_root, 1)

            def head_step(q, c):
                if c == 0:
                    if q == 0:
                        act.wait_ge(cq_lo, 3)
                        act.wait_ge(kpe_step, 4)
                    else:
                        act.wait_ge(hd_sum, 4 * q - 2)
                        wait_full(act, ("ss k0", q - 1))
                    head_squares(q, "qr", 2)
                    head_squares(q, "qn0", 0)
                elif c == 1:
                    if q == 0:
                        act.wait_ge(cq_f, 3)
                    else:
                        act.wait_ge(k_ready, 4 * q)
                    head_root(q, "ss q0")
                    if q:
                        wait_full(act, ("ss k1", q - 1))
                    head_squares(q, "qn1", 1)
                elif c == 2:
                    act.wait_ge(q_ready, 4 * q + 2)
                    head_root(q, "ss q1")
                    wait_full(act, ("ss q0", q))
                    head_squares(q, "kn0", 0)
                else:
                    act.wait_ge(q_ready, 4 * q + 4)
                    head_root(q, "ss k0")
                    wait_full(act, ("ss q1", q))
                    head_squares(q, "kn1", 1)

            def last_root(q):
                act.wait_ge(k_ready, 4 * q + 2)
                head_root(q, "ss k1")

            for c in range(4):
                head_step(0, c)
                ada_copy(ada_group(-1, c))
                if c == 0:
                    hi_static(4)
                    hi_static(5)
            last_root(0)
            for p in range(PAIRS):
                for i in range(4):
                    it, h, g = 4 * p + i, 2 * p + i // 2, i % 2
                    nk = NC_TOK if g == 0 else T
                    for j in range(2):
                        name = (f"score{j}", p, i)
                        wait_full(act, name)
                        act.wait_ge(s_neg, 2 * it + j + 1)
                        if it:
                            act.wait_ge(s_prob, 2 * it - 1 + j)
                        act.activation(PR[:, j, 0:nk], bank(name)[:, 0:nk], ACT.Exp, bias=NM[:, j:j + 1],
                                       scale=QK ** -0.5, accum_out=SM[:, j:j + 1]).then_inc(s_exp, 1)
                    if p + 1 < PAIRS:
                        head_step(p + 1, i)
                    ada_copy(ada_group(p, i))
                    for j in range(2):
                        name = (f"PT{j}", p, i)
                        wait_full(act, name)
                        act.activation(PT[:, 0:nk // P, P * j:P * j + P],
                                       bank(name)[:, 0:nk].rearrange("p (k q) -> p k q", q=P),
                                       ACT.Copy).then_inc(pt_copy, 1)
                    if i == 3 and p + 1 < PAIRS:
                        last_root(p + 1)
                    name = ("att", p, i)
                    wait_full(act, name)
                    act.activation(HHI[:, h, 256 * g:256 * g + 256], bank(name)[:, 0:256],
                                   ACT.Copy).then_inc(o_hi, 1)
            hi_static(6)
            hi_static(7)
            hi_static(8)

            def ffn_hi(h, i):
                hi(U_FFN + i, 16 * (U_FFN // RING_IN + h * (FFN_UNITS // RING_IN) + i // RING_IN + 1),
                   ffn_used(h, i))

            squares(1)
            norm_root(1)
            ffn_hi(0, 0)
            norm_hi(1)
            with act.Fori(0, 2) as h:
                for i in range(HALF_F):
                    ffn_hi(h, i + 1)
                    b = 2 * (i % 2)
                    g = h * HALF_F + i
                    act.wait_ge(made, ffn_at(h, ("h1", i)))
                    act.wait_ge(f_mul, g + 1)
                    act.activation(TMP[:, 0, :], PS[:, b, :], ACT.Silu).then_inc(f_silu, 1)
                    act.wait_ge(f_mul, g + 2)
                    act.wait_ge(made, plan.ffn + h * len(FFN_MADE))
                    act.activation(GHI[:, i, :], TMP[:, 2 + i % 2, :], ACT.Copy).then_inc(f_hi, 1)
                for i in range(HALF_F + 1, FFN_UNITS):
                    ffn_hi(h, i)
                ffn_hi(h, FFN_UNITS)
            squares(2)
            norm_root(2)
            norm_hi(2)
            hi_static(U_RG + 1)

            def rg_inputs(b, m):
                wait_full(act, ("u", b, m))
                if b:
                    act.wait_ge(rg_conv, 8 * b)
                act.wait_ge(rg_pad, 1)
                act.activation(UP[:, m, :, RG_LEFT:RG_LEFT + NC_TOK],
                               bank(("u", b, m)).rearrange("p (s t) -> p s t", s=2),
                               ACT.Copy).then_inc(rg_in, 1)

            def conv_hi(b, m):
                act.wait_ge(rg_conv, 8 * b + 4 * m + 4)
                if b:
                    wait_used(act, U_RG + 3 * b - 1)
                act.activation(UCHI[:, m, :], UC[:, m, :], ACT.Copy).then_inc(rg_uhi, 1)

            for m in range(2):
                rg_inputs(0, m)
            hi_static(U_RG + 2)
            for m in range(2):
                conv_hi(0, m)

            def gelus(b):
                for m in range(2):
                    wait_full(act, ("gate", b, m))
                    if b > 1:
                        act.wait_ge(rg_ylo, 2 * b - 2)
                    act.activation(GG[:, b % 2, m, :], bank(("gate", b, m))[:, 0:NL_TOK],
                                   ACT.Gelu_apprx_tanh).then_inc(rg_gelu, 1)

            def rg_out_hi(b):
                for m in range(2):
                    act.wait_ge(rg_y, 2 * b + m + 1)
                    act.activation(YHI[:, 2 * b + m, :], GG[:, b % 2, m, :], ACT.Copy).then_inc(rg_yhi, 1)

            gelus(0)
            hi_static(U_RG + 3)
            act.wait_ge(spl, 15)
            for b in range(RG_BLOCKS):
                u = U_RG + 3 * b
                for n in range(4):
                    d, m = divmod(n, 2)
                    e, ch = 4 * b + n, 2 * b + m
                    wait_full(act, ("a", b, d, m))
                    if b:
                        act.wait_ge(rg_scan, e - 3)
                    act.activation(RT[:, n, :], bank(("a", b, d, m)), ACT.Sigmoid,
                                   bias=PAR[:, P_BA + 8 * d + ch:P_BA + 8 * d + ch + 1]).then_inc(rg_sig, 1)
                    wait_full(act, ("x", b, d, m))
                    act.activation(IT[:, n, :], bank(("x", b, d, m)), ACT.Sigmoid,
                                   bias=PAR[:, P_BX + 8 * d + ch:P_BX + 8 * d + ch + 1]).then_inc(rg_i, 1)
                if b:
                    rg_out_hi(b - 1)
                for n in range(4):
                    lam8 = LAM8[:, 8 * (n // 2) + 2 * b + n % 2:8 * (n // 2) + 2 * b + n % 2 + 1]
                    act.wait_ge(rg_sig, 4 * b + n + 1)
                    act.activation(TH[:, n, :], RT[:, n, :], ACT.Tanh, scale=lam8).then_inc(rg_tanh, 1)
                    act.activation(RT[:, n, :], RT[:, n, :], ACT.Exp, scale=lam8).then_inc(rg_exp, 1)
                if b < RG_BLOCKS - 1:
                    for m in range(2):
                        rg_inputs(b + 1, m)
                act.wait_ge(w_hi, u + 5)
                hi_static(u + 5)
                if b < RG_BLOCKS - 1:
                    for m in range(2):
                        conv_hi(b + 1, m)
                for n in range(4):
                    act.wait_ge(rg_w, 4 * b + n + 1)
                    act.activation(TH[:, n, :], TH[:, n, :], ACT.Sqrt, scale=-1.0).then_inc(rg_root, 1)
                if b < RG_BLOCKS - 1:
                    gelus(b + 1)
            rg_out_hi(RG_BLOCKS - 1)
            hi_static(N_UNITS - 1)
            squares(3)
            norm_root(3)
            act.wait_ge(rt, 2)
            act.activation(GV[:, :, 1:2], GV[:, :, 0:1], ACT.Exp).then_inc(rt_exp, 1)
            for i in range(4):
                wait_full(act, ("h2", i))
                act.activation(H2HI[:, i // 2, 512 * (i % 2):512 * (i % 2) + 512], bank(("h2", i)),
                               ACT.Copy).then_inc(h2_hi, 1)

            def hi_e(r, j, c, used):
                act.wait_ge(raw_in[c], RAW_BASE[c] + 16 * (r * NJ + j + 1))
                act.wait_ge(e_made, used)
                act.activation(WHI[:, c % RING, :], RAW[:, c, :], ACT.Copy).then_inc(e_hi, 1)

            def gathered(at):
                for i in range(2):
                    act.wait_ge(e_made, at[i])
                    act.activation(XS[:, 512 * i:512 * i + 512], PS[:, 6 + i, :], ACT.Copy).then_inc(xs_ready, 1)

            def transposed(at):
                for i in range(2):
                    act.wait_ge(e_made, at[i])
                    act.activation(XTHI[:, 4 * i:4 * i + 4, :],
                                   PS[:, 5 + i, :].rearrange("p (k s) -> p k s", s=SLOTS),
                                   ACT.Copy).then_inc(xt_hi, 1)

            def out_hi(r):
                act.wait_ge(gs_ready, r + 1)
                act.wait_ge(y_lo, 2 * r + 1)
                act.wait_ge(e_made, round_at(r - 1, M_U41))
                for i in range(2):
                    act.activation(YR[:, i, :], PS[:, 2 + i, :], ACT.Copy, scale=GS[:]).then_inc(y_f, 1)
                for i in range(2):
                    act.wait_ge(y_f, 2 * r + i + 1)
                    act.activation(YRHI[:, i, :], YR[:, i, :], ACT.Copy).then_inc(y_hi, 1)

            wait_full(act, "pos")
            gathered((4, 8))
            transposed((12, 16))
            act.wait_ge(rounds_ready, 1)
            rounds = act.value_load(EXI[0:1, 15:16], min_val=N_EXP, max_val=MAX_ROUNDS)
            with act.Fori(0, rounds) as r:
                for c in range(3):
                    hi_e(r, 0, c, round_at(r - 1, (M_JU[5] + J_MADE * (NJ - 2), M_U40, M_U41)[c]))
                out_hi(r)
                for c in range(3, 5):
                    hi_e(r, 0, c, round_at(r, M_U0 + c - 3))

                def silu(j, at):
                    act.wait_ge(e_made, at)
                    act.wait_ge(m_mul, r * NJ + j + 1)
                    act.activation(SG[:], PS[:, 0, :], ACT.Silu).then_inc(m_silu, 1)

                def gt_hi(j, at):
                    act.wait_ge(e_made, at)
                    act.activation(GTHI[:], PS[:, 4, :].rearrange("p (c s) -> p c s", s=SLOTS),
                                   ACT.Copy).then_inc(m_gthi, 1)

                silu(0, round_at(r, M_U0 + 1))
                hi_e(r, 0, 5, round_at(r, M_U0 + 2))
                with act.Fori(0, NJ - 1) as j:
                    used = [round_at(r, n + J_MADE * j) for n in (M_LOOP - 1, *M_JU[:5])]
                    hi_e(r, j + 1, 0, used[0])
                    hi_e(r, j + 1, 1, used[1])
                    gt_hi(j, round_at(r, M_JT + J_MADE * j))
                    hi_e(r, j + 1, 2, used[2])
                    silu(j + 1, round_at(r, M_JU[1] + J_MADE * j))
                    for c in range(3, 6):
                        hi_e(r, j + 1, c, used[c])
                gathered((round_at(r, M_X), round_at(r, M_X + 1)))
                gt_hi(NJ - 1, round_at(r, M_GT))
                transposed((round_at(r, M_XT), round_at(r, M_XT + 1)))
            out_hi(rounds)

        @block.vector
        def _(dve):
            def lo(slot_u, at):
                s = slot_u % RING
                dve.wait_ge(w_hi, at + 1)
                c = unit_cols(slot_u)
                dve.tensor_tensor(WLO[:, s, 0:c], RAW[:, s, 0:c], WHI[:, s, 0:c].bitcast(F32),
                                  ALU.subtract).then_inc(w_lo, 1)

            def lo_static(u):
                if u < N_UNITS and not U_FFN <= u < U_RG:
                    lo(u, u)

            def split_static(u):
                s, c = u % RING, unit_cols(u)
                dve.wait_ge(w_hi, u)
                dve.wait_ge(raw_in[s], 16 * (u // RING_IN + 1))
                wait_used(dve, u - RING)
                dve.tensor_copy(WHI[:, s, 0:c], RAW[:, s, 0:c]).then_inc(w_hi, 1)
                lo(u, u)

            def ada_col(a):
                dve.wait_ge(ada_rowT, a + 1)
                g, layer = a % 12, a // 12
                dst = MC[:, layer, 4 * g:4 * g + 4, :]
                view = PS[:, 7, :].rearrange("p (c j s) -> p c s j", c=4, j=4)[:, :, 0:2, :]
                dve.tensor_reduce(dst, view, AX.X, ALU.add).then_inc(ada_cols, 1)
                dve.wait_ge(ada_cols, a + 1)
                bias = PAR[:, P_ADAB + 48 * layer + 4 * g:P_ADAB + 48 * layer + 4 * g + 4]
                for s in range(2):
                    dve.tensor_tensor(dst[:, :, s], dst[:, :, s], bias, ALU.add).then_inc(ada_sum, 1)

            def coefs(n):
                layer, which = n // 2, SC1 if n % 2 == 0 else SC2
                dve.wait_ge(ada_sum, 8 if n == 0 else 2 * ADA_GROUPS)
                gain = PAR[:, (P_N1 if n % 2 == 0 else P_N2) + 8 * layer:][:, 0:8]
                for s in range(2):
                    dve.scalar_tensor_tensor(CA[:, n, :, s], MC[:, layer, 8 * which:8 * which + 8, s], 1.0, gain,
                                             ALU.add, ALU.mult).then_inc(coef, 1)

            def add_square(n, k):
                w = toks(n).stop - toks(n).start
                dve.wait_ge(sq_done, n * KD + k + 1)
                if k > 1:
                    dve.wait_ge(sq_sum, n * (KD - 1) + k - 1)
                dve.tensor_tensor(TMP[:, 2, 0:w], TMP[:, 2, 0:w], TMP[:, k % 2, 0:w],
                                  ALU.add).then_inc(sq_sum, 1)

            def inverse(n):
                dve.wait_ge(root, n + 1)
                w = T if n < 3 else NL_TOK
                dve.reciprocal(RSTD[:, 0:w], RSTD[:, 0:w]).then_inc(rstd, 1)

            def norm(n):
                layer, sh = n // 2, (SH1 if n % 2 == 0 else SH2)
                if n:
                    inverse(n)
                if n == 1:
                    lo(U_FFN, U_FFN)
                dve.wait_ge(coef, 2 * n + 2)

                def low(k):
                    g = n * KD + k
                    dve.wait_ge(h_hi, g + 1)
                    dve.wait_ge(mod, 2 * (g + 1))
                    dve.tensor_tensor(HLO[:, k, :], TMP[:, k % 4, :], HHI[:, k, :].bitcast(F32),
                                      ALU.subtract).then_inc(h_lo, 1)

                for k in range(KD):
                    g = n * KD + k
                    dve.wait_ge(xr, g + 1)
                    if n < 3:
                        src = TMP[:, k % 4, :]
                        for s in range(2):
                            cols = slice(256 * s, 256 * s + 256)
                            dve.tensor_scalar(src[:, cols], src[:, cols], CA[:, n, k, s:s + 1],
                                              MC[:, layer, 8 * sh + k, s:s + 1], ALU.mult, ALU.add).then_inc(mod, 1)
                        if k:
                            low(k - 1)
                        if k == KD - 1:
                            low(k)
                    else:
                        dve.tensor_scalar(H2T[:, k, :], H2T[:, k, :], CA[:, n, k, 1:2],
                                          MC[:, layer, 8 * sh + k, 1:2], ALU.mult, ALU.add).then_inc(mod, 1)

            dve.wait_ge(in_par, 16)
            LAM = PAR[:, P_LAM:P_LAM + 16]
            dve.tensor_scalar(SPL[:, 5, :], LAM, -1.0, None, ALU.mult).then_inc(spl, 1)
            dve.wait_ge(spl, 1)
            dve.tensor_tensor(SPL[:, 0, :], LAM, SPL[:, 5, :], ALU.max).then_inc(spl, 1)
            dve.wait_ge(spl, 3)
            dve.tensor_scalar(SPL[:, 2, :], SPL[:, 1, :], 1.0, None, ALU.add).then_inc(spl, 1)
            dve.wait_ge(spl, 5)
            dve.tensor_scalar(SPL[:, 4, :], SPL[:, 2, :], -1.0, None, ALU.add).then_inc(spl, 1)
            dve.wait_ge(spl, 6)
            dve.tensor_scalar(SPL[:, 6, :], SPL[:, 4, :], 0.0, None, ALU.is_equal).then_inc(spl, 1)
            dve.wait_ge(spl, 7)
            dve.tensor_tensor(SPL[:, 4, :], SPL[:, 4, :], SPL[:, 6, :], ALU.add).then_inc(spl, 1)
            dve.tensor_tensor(SPL[:, 3, :], SPL[:, 3, :], SPL[:, 6, :], ALU.add).then_inc(spl, 1)
            dve.wait_ge(spl, 9)
            dve.reciprocal(SPL[:, 4, :], SPL[:, 4, :]).then_inc(spl, 1)
            dve.tensor_tensor(SPL[:, 3, :], SPL[:, 3, :], SPL[:, 1, :], ALU.mult).then_inc(spl, 1)
            dve.wait_ge(spl, 11)
            dve.tensor_tensor(SPL[:, 3, :], SPL[:, 3, :], SPL[:, 4, :], ALU.mult).then_inc(spl, 1)
            dve.tensor_scalar(SPL[:, 5, :], SPL[:, 5, :], 0.0, None, ALU.max).then_inc(spl, 1)
            dve.wait_ge(spl, 13)
            dve.tensor_tensor(SPL[:, 3, :], SPL[:, 3, :], SPL[:, 5, :], ALU.add).then_inc(spl, 1)
            dve.wait_ge(spl, 14)
            dve.tensor_scalar(LAM8[:], SPL[:, 3, :], -RG_C, None, ALU.mult).then_inc(spl, 1)
            dve.wait_ge(in_const, 16)
            ada_col(0)
            for k in range(1, KD):
                add_square(0, k)
            ada_col(1)
            inverse(0)
            for a in range(2, 4):
                ada_col(a)
            coefs(0)
            lo_static(0)
            norm(0)
            lo_static(1)
            lo_static(2)

            def latent(i, name, gain, slot, lo_out, hi_in):
                dve.wait_ge(lat_sq, (3, 4, 1)[slot])
                dve.scalar_tensor_tensor(TMP[:, slot, :], bank(name), PAR[:, gain:gain + 1], RSTD[:],
                                         ALU.mult, ALU.mult).then_inc(cq_f, 1)
                dve.wait_ge(cq_f, i + 1)
                dve.wait_ge(cq_hi, i + 1)
                dve.tensor_tensor(lo_out, TMP[:, slot, :], hi_in.bitcast(F32), ALU.subtract).then_inc(cq_lo, 1)

            def latent_rstd(n):
                dve.wait_ge(lat_root, n)
                dve.reciprocal(RSTD[:], RSTD[:]).then_inc(lat_rstd, 1)
                dve.wait_ge(lat_rstd, n)

            dve.wait_ge(lat_sq, 2)
            dve.tensor_scalar(KPE[:], bank("pe"), PAR[:, P_GKR:P_GKR + 1], None, ALU.mult).then_inc(kpe_step, 1)
            latent_rstd(1)
            lo_static(3)
            latent(0, "ckv", P_GKV, 2, CKLO[:], CKHI[:])
            wait_full(dve, "swap k")
            dve.wait_ge(cq_lo, 1)
            dve.tensor_tensor(TMP[:, 2, :], bank("swap k"), SIN, ALU.mult).then_inc(kpe_step, 1)
            latent_rstd(2)
            latent(1, "qa0", P_GQ, 0, CQLO[:, 0, :], CQHI[:, 0, :])
            latent(2, "qa1", P_GQ + 1, 1, CQLO[:, 1, :], CQHI[:, 1, :])
            dve.tensor_tensor(KPE[:], KPE[:], COS, ALU.mult).then_inc(kpe_step, 1)
            dve.wait_ge(kpe_step, 3)
            dve.tensor_tensor(KPE[:], KPE[:], TMP[:, 2, :], ALU.add).then_inc(kpe_step, 1)
            dve.tensor_tensor(GQK, PAR[:, P_GQN:P_GQN + 1], PAR[:, P_GKN:P_GKN + 1],
                              ALU.mult).then_inc(gqk_ready, 1)
            dve.wait_ge(gqk_ready, 1)

            def query(q, i):
                qn, qr, kn, kr = HEAD_SETS[q % 2]
                half, n = slice(64 * i, 64 * i + 64), 4 * q + i
                dve.wait_ge(hd_root, n + 1)
                dve.reciprocal(RSTD[:], RSTD[:]).then_inc(hd_rstd, 1)
                dve.wait_ge(hd_rstd, n + 1)
                dve.tensor_tensor(qn[:, i, :], bank((f"qn{i}", q)), RSTD[:], ALU.mult).then_inc(q_ready, 1)
                dve.wait_ge(qr_step, 4 * q + 4)
                dve.tensor_tensor(qr[half, :], qr[half, :], RSTD[half, :], ALU.mult).then_inc(q_ready, 1)

            def key(q, i):
                qn, qr, kn, kr = HEAD_SETS[q % 2]
                half, n = slice(64 * i, 64 * i + 64), 4 * q + 2 + i
                dve.wait_ge(hd_root, n + 1)
                dve.reciprocal(RSTD[:], RSTD[:]).then_inc(hd_rstd, 1)
                dve.wait_ge(hd_rstd, n + 1)
                dve.scalar_tensor_tensor(kn[:, i, :], bank((f"kn{i}", q)), GQK, RSTD[:],
                                         ALU.mult, ALU.mult).then_inc(k_ready, 1)
                dve.tensor_tensor(kr[half, :], KPE[half, :], RSTD[half, :], ALU.mult).then_inc(k_ready, 1)

            def head_step(q, c, group):
                if q == PAIRS:
                    ada_col(group)
                elif c == 0:
                    qn, qr, kn, kr = HEAD_SETS[q % 2]
                    dve.wait_ge(hd_sq, 5 * q + 1)
                    if q > 1:
                        wait_full(dve, ("score1", q - 2, 3))
                    dve.tensor_scalar(qr, bank(("qr", q)), PAR[:, P_GQR:P_GQR + 1], None,
                                      ALU.mult).then_inc(qr_step, 1)
                    ada_col(group)
                    wait_full(dve, ("swap q", q))
                    dve.tensor_tensor(kr, bank(("swap q", q)), SIN, ALU.mult).then_inc(qr_step, 1)
                    dve.tensor_tensor(qr, qr, COS, ALU.mult).then_inc(qr_step, 1)
                    dve.wait_ge(qr_step, 4 * q + 3)
                    dve.tensor_tensor(qr, qr, kr, ALU.add).then_inc(qr_step, 1)
                elif c == 1:
                    query(q, 0)
                    ada_col(group)
                elif c == 2:
                    query(q, 1)
                    ada_col(group)
                else:
                    key(q, 0)
                    ada_col(group)
                    key(q, 1)

            for c in range(4):
                head_step(0, c, ada_group(-1, c))
                if c == 0:
                    lo_static(4)
                    lo_static(5)
            for p in range(PAIRS):
                for i in range(4):
                    it, h, g = 4 * p + i, 2 * p + i // 2, i % 2
                    nk = NC_TOK if g == 0 else T
                    for j in range(2):
                        name = (f"score{j}", p, i)
                        wait_full(dve, name)
                        dve.tensor_reduce(MX[:, j:j + 1], bank(name)[:, 0:nk], AX.X, ALU.max).then_inc(s_max, 1)
                        dve.wait_ge(s_max, 2 * it + j + 1)
                        if it:
                            dve.wait_ge(s_exp, 2 * it - 1 + j)
                        dve.tensor_scalar(NM[:, j:j + 1], MX[:, j:j + 1], -(QK ** -0.5), None,
                                          ALU.mult).then_inc(s_neg, 1)
                    for j in range(2):
                        dve.wait_ge(s_exp, 2 * it + j + 1)
                        dve.reciprocal(RI[:, j:j + 1], SM[:, j:j + 1]).then_inc(s_rec, 1)
                        dve.wait_ge(s_rec, 2 * it + j + 1)
                        dve.tensor_scalar(PR[:, j, 0:nk], PR[:, j, 0:nk], RI[:, j:j + 1], None,
                                          ALU.mult).then_inc(s_prob, 1)
                    head_step(p + 1, i, ada_group(p, i))
                    name = ("att", p, i)
                    dve.wait_ge(o_hi, it + 1)
                    dve.tensor_tensor(HLO[:, h, 256 * g:256 * g + 256], bank(name)[:, 0:256],
                                      HHI[:, h, 256 * g:256 * g + 256].bitcast(F32),
                                      ALU.subtract).then_inc(o_lo, 1)
            lo_static(6)
            lo_static(7)
            for n in range(1, 4):
                coefs(n)

            def residual(name_bank, m, layer, part, streams, then, w=256):
                for s in streams:
                    cols = slice(256 * s, 256 * s + 256)
                    src = name_bank[:, cols] if len(streams) == 2 else name_bank[:, 0:256]
                    dve.scalar_tensor_tensor(X[:, m, cols], src, MC[:, layer, 8 * part + m, s:s + 1],
                                             X[:, m, cols], ALU.mult, ALU.add).then_inc(then, 1)

            for m in range(KD):
                wait_full(dve, ("o", m))
                residual(bank(("o", m)), m, 0, GA1, (0, 1), x_mid[0])
                if m > 1:
                    add_square(1, m - 1)
                if m == 1:
                    lo_static(8)
            add_square(1, KD - 1)
            norm(1)
            with dve.Fori(0, 2) as h:
                for i in range(HALF_F):
                    lo(U_FFN + i + 1, U_FFN + h * FFN_UNITS + i + 1)
                    b = 2 * (i % 2)
                    g = h * HALF_F + i
                    dve.wait_ge(f_silu, g + 1)
                    dve.wait_ge(made, ffn_at(h, ("h3", i)))
                    dve.tensor_tensor(TMP[:, 2 + i % 2, :], TMP[:, 0, :], PS[:, b + 1, :],
                                      ALU.mult).then_inc(f_mul, 1)
                    dve.wait_ge(f_mul, g + 2)
                    dve.wait_ge(f_hi, g + 1)
                    dve.tensor_tensor(GLO[:, i, :], TMP[:, 2 + i % 2, :], GHI[:, i, :].bitcast(F32),
                                      ALU.subtract).then_inc(f_lo, 1)
                q = HALF_F + 1
                for m in range(KD):
                    end = HALF_F + ((m + 1) * HALF_F - 1) // W2_UNIT_TILES
                    while q < FFN_UNITS and q <= end + 1:
                        lo(U_FFN + q, U_FFN + h * FFN_UNITS + q)
                        q += 1
                    if m == KD - 1:
                        lo(U_RG, U_FFN + (h + 1) * FFN_UNITS)
                    b = 4 + m % 2
                    dve.wait_ge(made, ffn_at(h, ("y", m)))
                    residual(PS[:, b, :], m, 0, GA2, (0, 1), f_x)
            for k in range(1, KD):
                add_square(2, k)
            norm(2)
            lo_static(U_RG + 1)

            def convolve(b, m):
                ch, n = 2 * b + m, 8 * b + 4 * m
                dve.wait_ge(rg_in, 2 * b + m + 1)
                ucv = UC[:, m, :].rearrange("p (s t) -> p s t", s=2)
                cw = [PAR[:, P_CW + 8 * k + ch:P_CW + 8 * k + ch + 1] for k in range(RG_CONV)]
                if b:
                    dve.wait_ge(rg_iu, 4 * b)
                    dve.wait_ge(rg_ulo, 2 * b)
                dve.tensor_scalar(ucv, UP[:, m, :, 0:NC_TOK], cw[0], PAR[:, P_CB + ch:P_CB + ch + 1],
                                  ALU.mult, ALU.add).then_inc(rg_conv, 1)
                for k in range(1, RG_CONV):
                    dve.wait_ge(rg_conv, n + k)
                    dve.scalar_tensor_tensor(ucv, UP[:, m, :, k:k + NC_TOK], cw[k], ucv,
                                             ALU.mult, ALU.add).then_inc(rg_conv, 1)

            def rg_out_lo(b):
                for m in range(2):
                    dve.wait_ge(rg_yhi, 2 * b + m + 1)
                    dve.tensor_tensor(YLO[:, 2 * b + m, :], GG[:, b % 2, m, :], YHI[:, 2 * b + m, :].bitcast(F32),
                                      ALU.subtract).then_inc(rg_ylo, 1)

            for m in range(2):
                convolve(0, m)
            lo_static(U_RG + 2)
            lo_static(U_RG + 3)
            for b in range(RG_BLOCKS):
                u = U_RG + 3 * b
                split_static(u + 4)
                if b:
                    rg_out_lo(b - 1)
                if b < RG_BLOCKS - 1:
                    convolve(b + 1, 0)
                    convolve(b + 1, 1)
                lo_static(u + 5)
                for n in range(4):
                    dve.wait_ge(rg_tanh, 4 * b + n + 1)
                    dve.wait_ge(rg_sq, 4 * b + n + 1)
                    dve.scalar_tensor_tensor(TH[:, n, :], SQ[:, n, :], 1.0, TH[:, n, :], ALU.add,
                                             ALU.mult).then_inc(rg_w, 1)
                if b < RG_BLOCKS - 1:
                    split_static(u + 6)
                for n in range(4):
                    e, m = 4 * b + n, n % 2
                    dve.wait_ge(rg_root, e + 1)
                    dve.wait_ge(rg_iu, e + 1)
                    dve.tensor_tensor(IT[:, n, :], IT[:, n, :], TH[:, n, :], ALU.mult).then_inc(rg_b, 1)
                for n in range(4):
                    e, m = 4 * b + n, n % 2
                    dve.wait_ge(rg_b, e + 1)
                    dve.wait_ge(rg_w, e + 1)
                    if n < 2:
                        if b:
                            dve.wait_ge(rg_y, 2 * b)
                        dve.tensor_tensor_scan(HS[:, m, :], RT[:, n, :], IT[:, n, :], 0.0, ALU.mult,
                                               ALU.add).then_inc(rg_scan, 1)
                    else:
                        c, l = slice(0, NC_TOK), LAT
                        dve.tensor_tensor_scan(SQ[:, n, c][:, ::-1], RT[:, n, c][:, ::-1], IT[:, n, c][:, ::-1],
                                               0.0, ALU.mult, ALU.add).then_inc(rg_back, 1)
                        dve.wait_ge(rg_back, 2 * b + m + 1)
                        dve.tensor_tensor_scan(SQ[:, n, l][:, ::-1], RT[:, n, l][:, ::-1], IT[:, n, l][:, ::-1],
                                               SQ[:, n, 0:1], ALU.mult, ALU.add).then_inc(rg_scan, 1)
                for n in range(2, 4):
                    m = n % 2
                    dve.wait_ge(rg_scan, 4 * b + n + 1)
                    dve.tensor_tensor(SQ[:, n, LAT], SQ[:, n, LAT], HS[:, m, LAT], ALU.add).then_inc(rg_sum, 1)
                for n in range(2, 4):
                    m = n % 2
                    dve.wait_ge(rg_sum, 2 * b + m + 1)
                    dve.wait_ge(rg_gelu, 2 * b + m + 1)
                    dve.tensor_tensor(GG[:, b % 2, m, :], GG[:, b % 2, m, :], SQ[:, n, LAT],
                                      ALU.mult).then_inc(rg_y, 1)
            rg_out_lo(RG_BLOCKS - 1)
            for m in range(KD):
                if m == 2:
                    lo_static(N_UNITS - 1)
                wait_full(dve, ("rg o", m))
                residual(bank(("rg o", m)), m, 1, GA1, (1,), x_mid[1])
                if m > 1:
                    add_square(3, m - 1)
            add_square(3, KD - 1)
            norm(3)
            wait_full(dve, "logits")
            dve.tensor_copy(LT[:], bank("logits")[0:N_EXP, 0:NL_TOK]).then_inc(lt_ready, 1)
            wait_full(dve, "logits T")
            def pick(cols):
                for t in range(2):
                    dve.tensor_scalar(G[:, t, :], IOTA, RP[:, t, cols], None, ALU.is_equal).then_inc(g_ready, 1)

            c = [0]

            def step(ins):
                c[0] += 1
                ins.then_inc(rt_step, 1)
                dve.wait_ge(rt_step, c[0])

            step(dve.tensor_copy(LG[:], bank("logits T")[:, 0:2 * N_EXP].rearrange("p (t e) -> p t e", t=2)))
            for t in range(2):
                step(dve.max(M8[:, t, :], LG[:, t, :]))
                step(dve.max_index(IX[:, t, :], M8[:, t, :], LG[:, t, :]))
                dve.tensor_tensor(GV[:, t, 0:1], M8[:, t, 1:2], M8[:, t, 0:1], ALU.subtract).then_inc(rt, 1)
            step(dve.tensor_copy(IXF[:], IX[:]))
            dve.wait_ge(rt_exp, 1)
            step(dve.tensor_scalar(GV[:, :, 2:3], GV[:, :, 1:2], 1.0, None, ALU.add))
            step(dve.reciprocal(GV[:, :, 2:3], GV[:, :, 2:3]))
            step(dve.tensor_tensor(GV[:, :, 3:4], GV[:, :, 1:2], GV[:, :, 2:3], ALU.mult))
            IOTA8 = IOTA[:, 0:N_EXP]
            for t in range(2):
                step(dve.tensor_scalar(MK1[:, t, :], IOTA8, IXF[:, t, 0:1], None, ALU.is_equal))
                step(dve.tensor_scalar(MK2[:, t, :], IOTA8, IXF[:, t, 1:2], None, ALU.is_equal))
                step(dve.tensor_tensor(SEL[:, t, :], MK1[:, t, :], MK2[:, t, :], ALU.add))
                step(dve.tensor_scalar(MK1[:, t, :], MK1[:, t, :], GV[:, t, 2:3], None, ALU.mult))
                step(dve.scalar_tensor_tensor(CMB[:, t, :], MK2[:, t, :], GV[:, t, 3:4], MK1[:, t, :],
                                              ALU.mult, ALU.add))
            assert c[0] == SEL_STEPS
            for i in range(4):
                dve.wait_ge(h2_hi, i + 1)
                cols = slice(512 * (i % 2), 512 * (i % 2) + 512)
                dve.tensor_tensor(H2LO[:, i // 2, cols], bank(("h2", i)), H2HI[:, i // 2, cols].bitcast(F32),
                                  ALU.subtract).then_inc(h2_lo, 1)
            step(dve.memset(RP[:], -1.0))
            step(dve.memset(RG[:], 0.0))
            wait_full(dve, "pos")
            dve.tensor_copy(POS[:], bank("pos")[:, 0:24].rearrange("p (a e) -> p a e", a=3)).then_inc(pos_ready, 1)
            dve.wait_ge(pos_ready, 1)
            FAR = 8192.0
            for t in range(2):
                step(dve.scalar_tensor_tensor(POS[:, t, :], POS[:, t, :], FAR, SEL[:, t, :], ALU.add, ALU.mult))
                step(dve.tensor_scalar(POS[:, t, :], POS[:, t, :], -FAR, None, ALU.add))
                step(dve.tensor_copy(RP[:, t, 0:N_EXP], POS[:, t, :]))
                step(dve.tensor_copy(RG[:, t, 0:N_EXP], CMB[:, t, :]))
            pick(slice(0, 1))
            step(dve.memset(EX[:], 0.0))
            step(dve.tensor_copy(EX[:, 0:N_EXP], IOTA8))
            step(dve.tensor_scalar(OVR[:, 0, :], POS[:, 2, :], float(SLOTS), None, ALU.is_gt))
            step(dve.tensor_tensor_scan(OVR[:, 1, :], ONES[:, 0:N_EXP], OVR[:, 0, :], 0.0, ALU.mult, ALU.add))
            step(dve.tensor_scalar(EX[:, 15:16], OVR[:, 1, N_EXP - 1:N_EXP], float(N_EXP), None, ALU.add))
            dve.tensor_copy(EXI[:], EX[:]).then_inc(rounds_ready, 1)
            step(dve.tensor_tensor(OVR[:, 1, :], OVR[:, 1, :], OVR[:, 0, :], ALU.subtract))
            for n in range(MAX_OVER):
                step(dve.scalar_tensor_tensor(OVR[:, 2, :], OVR[:, 1, :], float(n), OVR[:, 0, :],
                                              ALU.is_equal, ALU.mult))
                col = N_EXP + n
                for src, dst in ((POS[:, 0, :], RP[:, 0, col:col + 1]), (POS[:, 1, :], RP[:, 1, col:col + 1]),
                                 (CMB[:, 0, :], RG[:, 0, col:col + 1]), (CMB[:, 1, :], RG[:, 1, col:col + 1]),
                                 (IOTA8, EX[:, col:col + 1])):
                    step(dve.tensor_tensor(OVR[:, 3, :], OVR[:, 2, :], src, ALU.mult))
                    step(dve.tensor_reduce(dst, OVR[:, 3, :], AX.X, ALU.add))
            step(dve.tensor_scalar(RP[:, :, N_EXP:N_EXP + MAX_OVER], RP[:, :, N_EXP:N_EXP + MAX_OVER],
                                   -float(SLOTS), None, ALU.add))
            dve.tensor_copy(EXI[:, N_EXP:N_EXP + MAX_OVER], EX[:, N_EXP:N_EXP + MAX_OVER]).then_inc(rt_done, 1)
            dve.wait_ge(rt_done, 1)
            rounds = dve.value_load(EXI[0:1, 15:16], min_val=N_EXP, max_val=MAX_ROUNDS)

            def lo_e(r, j, c):
                dve.wait_ge(e_hi, r * EXP_UNITS + 6 * j + c + 1)
                dve.tensor_tensor(WLO[:, c % RING, :], RAW[:, c, :], WHI[:, c % RING, :].bitcast(F32),
                                  ALU.subtract).then_inc(e_lo, 1)

            def transposed_lo(n):
                for i in range(2):
                    dve.wait_ge(xt_hi, 2 * n + i + 1)
                    dve.tensor_tensor(XTLO[:, 4 * i:4 * i + 4, :],
                                      PS[:, 5 + i, :].rearrange("p (k s) -> p k s", s=SLOTS),
                                      XTHI[:, 4 * i:4 * i + 4, :].bitcast(F32), ALU.subtract).then_inc(xt_lo, 1)

            transposed_lo(0)
            dve.wait_ge(acc, 1)

            def add_out(r, first):
                for i, b in enumerate((6, 7, 5, 4)):
                    dve.wait_ge(e_made, round_at(r, first + i))
                    if i == 0:
                        dve.wait_ge(acc, 4 * r + 1)
                    part = ACC[:, 2 * i:2 * i + 2, :]
                    dve.tensor_tensor(part, part, PS[:, b, :].rearrange("p (k t) -> p k t", k=2),
                                      ALU.add).then_inc(acc, 1)

            with dve.Fori(0, rounds) as r:
                for c in range(3):
                    lo_e(r, 0, c)
                dve.wait_ge(e_made, round_at(r, M_GATE))
                dve.wait_ge(gt_ready, r + 1)
                dve.tensor_copy(GTN[:], PS[:, 7, 0:NL_TOK]).then_inc(gtn_ready, 1)
                dve.wait_ge(y_f, 2 * r + 2)
                dve.tensor_copy(GS[:], PS[:, 7, NL_TOK:NL_TOK + 1]).then_inc(gs_ready, 1)
                for c in range(3, 6):
                    lo_e(r, 0, c)

                def mul(j, at):
                    dve.wait_ge(m_silu, r * NJ + j + 2)
                    dve.wait_ge(e_made, at)
                    dve.tensor_tensor(GM[:], SG[:], PS[:, 1, :], ALU.mult).then_inc(m_mul, 1)

                def gt_lo(j):
                    dve.wait_ge(m_gthi, r * NJ + j + 1)
                    dve.tensor_tensor(GTLO[:], PS[:, 4, :].rearrange("p (c s) -> p c s", s=SLOTS),
                                      GTHI[:].bitcast(F32), ALU.subtract).then_inc(m_gtlo, 1)

                mul(0, round_at(r, M_U0 + 3))
                pick(bass.ds(r + 1, 1))
                add_out(r, M_OUT)
                dve.wait_ge(gtn_ready, r + 1)
                dve.tensor_copy(GTR[:], GTN[:]).then_inc(gt_ready, 1)
                with dve.Fori(0, NJ - 1) as j:
                    lo_e(r, j + 1, 0)
                    lo_e(r, j + 1, 1)
                    gt_lo(j)
                    for c in range(2, 5):
                        lo_e(r, j + 1, c)
                    mul(j + 1, round_at(r, M_JU[3] + J_MADE * j))
                    lo_e(r, j + 1, 5)
                gt_lo(NJ - 1)
                transposed_lo(r + 1)
            add_out(rounds, 0)
            dve.wait_ge(acc, 4 * rounds + 5)
            for m in range(KD):
                dve.scalar_tensor_tensor(ACC[:, m, :], ACC[:, m, :], MC[:, 1, 8 * GA2 + m, 1:2],
                                         X[:, m, LAT], ALU.mult, ALU.add).then_inc(fin, 1)

        @block.tensor
        def _(pe):
            def three(out, whi, wlo, mhi, mlo, first, last):
                pe.matmul(out, whi, mhi, start=first, stop=False)
                pe.matmul(out, whi, mlo, start=False, stop=False)
                return pe.matmul(out, wlo, mhi, start=False, stop=last)

            def tile(u, i):
                s = u % RING
                return WHI[:, s, P * i:P * i + P], WLO[:, s, P * i:P * i + P]

            def wait_unit(u):
                pe.wait_ge(w_lo, u + 1)

            at = [0]

            def start(name):
                assert plan.order[name] == at[0], name
                at[0] += 1
                if plan.before[name]:
                    pe.wait_ge(*bank_read(name))

            def ada(a):
                if a:
                    pe.wait_ge(ada_cols, a)
                pe.wait_ge(cs_ready, 1)
                for part in range(2):
                    n = 2 * a + part
                    pe.wait_ge(ada_in[n % ADA_RING], 16 * (n // ADA_RING + 1))
                    for j in range(4):
                        ins = pe.matmul(PS[32 * j:32 * j + 32, 7, :], CS[:, 4 * part + j, :],
                                        RAW[:, ADA_SLOT + n % ADA_RING, 512 * j:512 * j + 512],
                                        start=part == 0, stop=part == 1, skip_group_check=True)
                    ins.then_inc(ada_used, 1)

            def ada_turn(a):
                pe.wait_ge(ada_row, a + 1)
                for c in range(4):
                    ins = pe.transpose(PS[:, 7, P * c:P * c + P], ROW[:, P * c:P * c + P], IDENT)
                ins.then_inc(ada_rowT, 1)

            def sums(n):
                w = toks(n).stop - toks(n).start
                start(("ss", n))
                pe.wait_ge(sq_sum, (n + 1) * (KD - 1))
                pe.matmul(bank(("ss", n))[:, 0:w], ONES, TMP[:, 2, 0:w], start=True, stop=True).then_inc(made, 1)

            def project(name, u, first_tile, mhi, mlo, n_k, cols=slice(0, T), first_k=0):
                start(name)
                w = cols.stop - cols.start
                for k in range(first_k, n_k):
                    hi_t, lo_t = tile(u, first_tile + k)
                    ins = three(bank(name)[:, 0:w], hi_t, lo_t, mhi[:, k, cols], mlo[:, k, cols], k == 0,
                                k == n_k - 1)
                ins.then_inc(made, 1)

            def project_two(names, u, ready):
                for name in names:
                    start(name)
                for k in range(KD):
                    pe.wait_ge(h_lo, ready + k + 1)
                    for m, name in enumerate(names):
                        hi_t, lo_t = tile(u, KD * m + k)
                        ins = three(bank(name), hi_t, lo_t, HHI[:, k, :], HLO[:, k, :], k == 0, k == KD - 1)
                        if k == KD - 1:
                            ins.then_inc(made, 1)

            def one(name, out, lhsT, rhs):
                start(name)
                pe.matmul(out, lhsT, rhs, start=True, stop=True).then_inc(made, 1)

            pe.wait_ge(in_par, 16)
            pe.wait_ge(in_const, 16)
            for a in range(4):
                ada(a)
                if a == 1:
                    sums(0)
                ada_turn(a)
            wait_unit(U_KV)
            project_two(("ckv", "pe"), U_KV, 0)
            wait_unit(U_Q)
            project("qa0", U_Q, 0, HHI, HLO, KD)
            pe.wait_ge(lat_sq, 1)
            one("ss kv", bank("ss kv"), ONES, TMP[:, 2, :])
            project("qa1", U_Q, KD, HHI, HLO, KD)
            pe.wait_ge(kpe_step, 1)
            one("swap k", bank("swap k"), PERM, KPE[:])
            start("ss q")
            for i in range(2):
                pe.wait_ge(lat_sq, i + 3)
                ins = pe.matmul(bank("ss q"), ONES, TMP[:, i, :], start=i == 0, stop=i == 1)
            ins.then_inc(made, 1)
            wait_unit(U_V)
            pe.wait_ge(cq_lo, 1)
            for i in range(8):
                start(("v", i))
                toks_i = slice(P * (i // 2), P * (i // 2) + P)
                w = slice(512 * (i % 2), 512 * (i % 2) + 512)
                s = ring(U_V)
                three(bank(("v", i)), CKHI[:, toks_i], CKLO[:, toks_i], WHI[:, s, w], WLO[:, s, w], True,
                      True).then_inc(made, 1)
            def sum_squares(q, name, n):
                pe.wait_ge(hd_sum, 4 * q + n + 1)
                one((name, q), bank((name, q)), ONES, TMP[:, n % 2, :])

            def head_step(q, c, part):
                u, t0 = U_HEADS + q // 2, 8 * (q % 2)

                def key(i):
                    name = (f"kn{i}", q)
                    start(name)
                    hi_t, lo_t = tile(u, t0 + 6 + i)
                    three(bank(name), hi_t, lo_t, CKHI[:], CKLO[:], True, True).then_inc(made, 1)

                if (c, part) == (0, 0):
                    wait_unit(u)
                    pe.wait_ge(cq_lo, 3)
                    project(("qr", q), u, t0 + 4, CQHI, CQLO, KQ)
                    project(("qn0", q), u, t0, CQHI, CQLO, KQ)
                elif (c, part) == (0, 1):
                    pe.wait_ge(qr_step, 4 * q + 1)
                    one(("swap q", q), bank(("swap q", q)), PERM, HEAD_SETS[q % 2][1])
                elif (c, part) == (1, 0):
                    sum_squares(q, "ss q0", 0)
                    project(("qn1", q), u, t0 + 2, CQHI, CQLO, KQ)
                elif (c, part) == (2, 0):
                    sum_squares(q, "ss q1", 1)
                    key(0)
                elif (c, part) == (3, 0):
                    sum_squares(q, "ss k0", 2)
                    key(1)
                elif (c, part) == (3, 1):
                    sum_squares(q, "ss k1", 3)

            for c in range(4):
                head_step(0, c, 0)
                ada(ada_group(-1, c))
                ada_turn(ada_group(-1, c))
                head_step(0, c, 1)
            for p in range(PAIRS):
                qn, qr, kn, kr = HEAD_SETS[p % 2]
                for i in range(4):
                    it, g, hh = 4 * p + i, i % 2, i // 2
                    nk = NC_TOK if g == 0 else T
                    half = slice(64 * hh, 64 * hh + 64)
                    pe.wait_ge(q_ready, 4 * p + 2 * hh + 2)
                    pe.wait_ge(k_ready, 4 * p + 2 * hh + 2)
                    for j in range(2):
                        name = (f"score{j}", p, i)
                        start(name)
                        q = slice(256 * g + P * j, 256 * g + P * j + P)
                        pe.matmul(bank(name)[:, 0:nk], qn[:, hh, q], kn[:, hh, 0:nk], start=True, stop=False)
                        pe.matmul(bank(name)[:, 0:nk], qr[half, q], kr[half, 0:nk], start=False,
                                  stop=True).then_inc(made, 1)
                    if p + 1 < PAIRS:
                        head_step(p + 1, i, 0)
                    ada(ada_group(p, i))
                    ada_turn(ada_group(p, i))
                    for j in range(2):
                        name = (f"PT{j}", p, i)
                        start(name)
                        pe.wait_ge(s_prob, 2 * it + j + 1)
                        for k in range(nk // P):
                            ins = pe.transpose(bank(name)[:, P * k:P * k + P], PR[:, j, P * k:P * k + P], IDENT)
                        ins.then_inc(made, 1)
                    if p + 1 < PAIRS:
                        head_step(p + 1, i, 1)
                    name = ("att", p, i)
                    start(name)
                    pe.wait_ge(pt_copy, 2 * it + 2)
                    for k in range(nk // P):
                        h = 2 * p + hh
                        ins = pe.matmul(bank(name)[:, 0:256], V[:, k, DV * h:DV * h + DV], PT[:, k, :],
                                        start=k == 0, stop=k == nk // P - 1)
                    ins.then_inc(made, 1)
            for m in range(KD):
                if m % 2 == 0:
                    wait_unit(U_O + m // 2)
                pe.wait_ge(o_lo, 2 * HEADS)
                project(("o", m), U_O + m // 2, KD * (m % 2), HHI, HLO, KD)
            sums(1)
            assert at[0] == plan.ffn
            pe.wait_ge(h_lo, KD + 1)
            with pe.Fori(0, 2) as h:
                for i in range(HALF_F):
                    pe.wait_ge(w_lo, U_FFN + h * FFN_UNITS + i + 1)
                    b = 2 * (i % 2)
                    steps = [(o, k) for k in range(KD) for o in range(2)] if i == 0 else [
                        (o, k) for o in range(2) for k in range(KD)]
                    if i == 0:
                        pe.wait_ge(f_mul, h * HALF_F + 1)
                    for o, k in steps:
                        if i >= 2 and k == 0:
                            pe.wait_ge((f_silu, f_mul)[o], h * HALF_F + i - 1 + o)
                        if i == 0 and o == 0:
                            pe.wait_ge(h_lo, KD + k + 1)
                        hi_t, lo_t = tile(U_FFN + i, KD * o + k)
                        ins = three(PS[:, b + o, :], hi_t, lo_t, HHI[:, k, :], HLO[:, k, :], k == 0,
                                    k == KD - 1)
                        if k == KD - 1:
                            ins.then_inc(made, 1)
                for t in range(KD * HALF_F):
                    m, k = divmod(t, HALF_F)
                    q, c = divmod(t, W2_UNIT_TILES)
                    if c == 0:
                        pe.wait_ge(w_lo, U_FFN + h * FFN_UNITS + HALF_F + q + 1)
                    if m == 0:
                        pe.wait_ge(f_lo, h * HALF_F + k + 1)
                    if k == 0 and m < 2:
                        pe.wait_ge(f_x, 2 * KD * h + 1)
                    elif k == 0:
                        pe.wait_ge(f_x, 2 * KD * h + 2 * (m - 1) + 1)
                    hi_t, lo_t = tile(U_FFN + HALF_F + q, c)
                    ins = three(PS[:, 4 + m % 2, :], hi_t, lo_t, GHI[:, k, :], GLO[:, k, :], k == 0,
                                k == HALF_F - 1)
                    if k == HALF_F - 1 or c == W2_UNIT_TILES - 1:
                        ins.then_inc(made, 1)
            at[0] += 2 * len(FFN_MADE)
            sums(2)
            for b in range(RG_BLOCKS):
                u = U_RG + 3 * b
                wait_unit(u)
                if b == 0:
                    project_two((("u", b, 0), ("u", b, 1)), u, 2 * KD)
                else:
                    for m in range(2):
                        project(("u", b, m), u, KD * m, HHI, HLO, KD)
                wait_unit(u + 1)
                for m in range(2):
                    project(("gate", b, m), u + 1, KD * m, HHI, HLO, KD, cols=LAT)
                wait_unit(u + 2)
                pe.wait_ge(rg_ulo, 2 * b + 2)
                for d in range(2):
                    for m in range(2):
                        for o, name in enumerate("ax"):
                            project((name, b, d, m), u + 2, 2 * (2 * (2 * d + m) + o), UCHI, UCLO, 2)
            EARLY_M, EARLY_K = 6, KD - 2
            pe.wait_ge(rg_ylo, EARLY_K)
            for m in range(EARLY_M):
                wait_unit(U_RGO + m // 2)
                pe.wait_ge(*bank_read(("rg o", m)))
                for k in range(EARLY_K):
                    hi_t, lo_t = tile(U_RGO + m // 2, KD * (m % 2) + k)
                    three(bank(("rg o", m))[:, 0:NL_TOK], hi_t, lo_t, YHI[:, k, :], YLO[:, k, :], k == 0, False)
            pe.wait_ge(rg_ylo, KD)
            for m in range(KD):
                wait_unit(U_RGO + m // 2)
                project(("rg o", m), U_RGO + m // 2, KD * (m % 2), YHI, YLO, KD, cols=slice(0, NL_TOK),
                        first_k=EARLY_K if m < EARLY_M else 0)
            sums(3)
            start("logits")
            for k in range(KD):
                pe.wait_ge(mod, 6 * KD + k + 1)
                ins = pe.matmul(bank("logits")[0:N_EXP, 0:NL_TOK], PAR[:, P_RW + N_EXP * k:P_RW + N_EXP * (k + 1)],
                                H2T[:, k, :], start=k == 0, stop=k == KD - 1)
            ins.then_inc(made, 1)
            start("logits T")
            pe.wait_ge(lt_ready, 1)
            for t in range(2):
                ins = pe.transpose(bank("logits T")[:, N_EXP * t:N_EXP * t + N_EXP], LT[:, P * t:P * t + P],
                                   IDENT[0:N_EXP, 0:N_EXP])
            ins.then_inc(made, 1)
            for i in range(4):
                start(("h2", i))
                for k in range(4):
                    ins = pe.transpose(bank(("h2", i))[:, P * k:P * k + P],
                                       H2T[:, 4 * (i % 2) + k, P * (i // 2):P * (i // 2) + P], IDENT)
                ins.then_inc(made, 1)
            start("pos")
            pe.wait_ge(rt_step, SEL_STEPS)
            o = bank("pos")
            pe.matmul(o[:, 0:8], TRI, SEL[:, 0, :], start=True, stop=True)
            pe.matmul(o[:, 8:16], ONES, SEL[:, 0, :], start=True, stop=False)
            pe.matmul(o[:, 8:16], TRI, SEL[:, 1, :], start=False, stop=True)
            pe.matmul(o[:, 16:24], ONES, SEL[:, 0, :], start=True, stop=False)
            pe.matmul(o[:, 16:24], ONES, SEL[:, 1, :], start=False, stop=True).then_inc(made, 1)

            def gather(n, peel):
                pe.wait_ge(g_ready, 2 * n + 2)
                for i in range(2):
                    cols = slice(512 * i, 512 * i + 512)
                    for t in range(2):
                        for x, part in enumerate((H2HI, H2LO)):
                            last = t == 1 and x == 1
                            ins = pe.matmul(PS[:, 6 + i, :], G[:, t, :], part[:, t, cols],
                                            start=t == 0 and x == 0, stop=last)
                            if last or peel:
                                ins.then_inc(e_made, 1)

            def gather_turn(n, peel):
                for i in range(2):
                    pe.wait_ge(xs_ready, 2 * n + i + 1)
                    for k in range(4):
                        ins = pe.transpose(PS[:, 5 + i, P * k:P * k + P],
                                           XS[:, P * (4 * i + k):P * (4 * i + k) + P], IDENT)
                        if peel:
                            ins.then_inc(e_made, 1)
                    if not peel:
                        ins.then_inc(e_made, 1)

            pe.wait_ge(h2_lo, 4)
            pe.wait_ge(ada_cols, ADA_GROUPS)
            pe.wait_ge(pos_ready, 1)
            pe.wait_ge(zeros_ready, 1)
            def open_sums():
                for i in range(2):
                    pe.matmul(PS[:, 2 + i, :], ZERO[:, 0:P], ZERO[:], start=True, stop=False,
                              skip_group_check=True)

            def scatter(r):
                pe.wait_ge(gt_ready, r + 1)
                pe.wait_ge(y_lo, 2 * r + 3)
                pe.wait_ge(xt_lo, 2 * r + 2)
                for i, b in enumerate((6, 7, 5, 4)):
                    for f in range(2):
                        d = 2 * i + f
                        cols = slice(P * (d % 4), P * (d % 4) + P)
                        pe.matmul(PS[:, b, 256 * f:256 * f + 256], YRHI[:, d // 4, cols], GTR[:], start=True,
                                  stop=False)
                        ins = pe.matmul(PS[:, b, 256 * f:256 * f + 256], YRLO[:, d // 4, cols], GTR[:],
                                        start=False, stop=True)
                    ins.then_inc(e_made, 1)

            open_sums()
            gather(0, True)
            gather_turn(0, True)
            pe.wait_ge(rounds_ready, 1)
            rounds = pe.value_load(EXI[0:1, 15:16], min_val=N_EXP, max_val=MAX_ROUNDS)
            with pe.Fori(0, rounds) as r:
                for t in range(2):
                    pe.transpose(PS[:, 7, P * t:P * t + P], G[:, t, :].bitcast(F32), IDENT)
                for t in range(2):
                    ins = pe.matmul(PS[:, 7, NL_TOK:NL_TOK + 1], G[:, t, :].bitcast(F32), RG[:, t, bass.ds(r, 1)],
                                    start=t == 0, stop=t == 1)
                ins.then_inc(e_made, 1)
                pe.wait_ge(xt_lo, 2 * r + 2)

                def up(j, o, c0):
                    for c in (c0, c0 + 1):
                        pe.wait_ge(e_lo, r * EXP_UNITS + j * 6 + c + 1)
                        if c == c0:
                            pe.wait_ge((m_silu, m_mul)[o], r * NJ + (j if c0 < 4 else j + 1) + 1)
                        s = c % RING
                        for k in range(4):
                            kk = 4 * (c - c0) + k
                            cols = slice(512 * k, 512 * k + 512)
                            ins = three(PS[:, o, :], XTHI[:, kk, :], XTLO[:, kk, :], WHI[:, s, cols],
                                        WLO[:, s, cols], kk == 0, kk == KD - 1)
                        ins.then_inc(e_made, 1)

                def turn(j, waits_gt):
                    pe.wait_ge(m_mul, r * NJ + j + 2)
                    pe.wait_ge(m_gtlo, r * NJ + j + 1)
                    pe.wait_ge(acc, 4 * r + 5)
                    for c in range(4):
                        ins = pe.transpose(PS[:, 4, P * c:P * c + P], GM[:, P * c:P * c + P], IDENT)
                    ins.then_inc(e_made, 1)

                def down(j, j_unit, c0):
                    pe.wait_ge(m_gtlo, r * NJ + j + 2)
                    for c in (c0, c0 + 1):
                        pe.wait_ge(e_lo, r * EXP_UNITS + j_unit * 6 + c + 1)
                        s = c % RING
                        for f in range(2):
                            fc = 2 * (c - c0) + f
                            for i in range(2):
                                cols = slice(1024 * f + 512 * i, 1024 * f + 512 * i + 512)
                                out_i = PS[:, 2 + i, :]
                                hi_g, lo_g = GTHI[:, fc, :], GTLO[:, fc, :]
                                pe.matmul(out_i, hi_g, WHI[:, s, cols], start=False, stop=False,
                                          skip_group_check=True)
                                pe.matmul(out_i, hi_g, WLO[:, s, cols], start=False, stop=False,
                                          skip_group_check=True)
                                ins = pe.matmul(out_i, lo_g, WHI[:, s, cols], start=False, stop=False,
                                                skip_group_check=True)
                        ins.then_inc(e_made, 1)

                up(0, 0, 0)
                up(0, 1, 2)
                pe.wait_ge(gs_ready, r + 2)
                scatter(r)
                pe.wait_ge(y_f, 2 * r + 2)
                open_sums()
                with pe.Fori(0, NJ - 1) as j:
                    up(j, 0, 4)
                    turn(j, True)
                    up(j, 1, 6)
                    down(j, j, 8)
                gather(r + 1, False)
                turn(NJ - 1, True)
                gather_turn(r + 1, False)
                down(NJ - 1, NJ - 1, 4)
            scatter(rounds)


RAW_BASE = [16 * len(range(c, N_UNITS, RING_IN)) if c < RING_IN else 0 for c in range(RAW_SLOTS)]


def tiles(w):
    k, m = w.shape
    return w.reshape(k // P, P, m // P, P).transpose(0, 2, 1, 3)


def unit(ts):
    u = np.zeros((P, UW), np.float32)
    for i, t in enumerate(ts):
        u[:, P * i:P * i + t.shape[1]] = t
    return u


def weight_units(w_dq, w_uq, w_dkv, w_ukv, w_o, f1, f3, f2, g_in, g_gate, w_a, w_x, g_out):
    units = []
    pe2 = np.concatenate([w_dkv, w_dkv[:, P:]], 1)
    for t in (tiles(pe2), tiles(w_dq)):
        units.append(unit([t[k, m] for m in range(2) for k in range(KD)]))
    ukv = w_ukv.reshape(P, HEADS, NOPE + DV)
    units.append(unit(list(ukv[:, :, NOPE:].transpose(1, 0, 2))))
    uq = w_uq.reshape(KQ, P, HEADS, QK)
    heads = []
    for p in range(PAIRS):
        for h in (2 * p, 2 * p + 1):
            heads += [uq[k, :, h, :NOPE] for k in range(KQ)]
        heads += [np.concatenate([uq[k, :, 2 * p, NOPE:], uq[k, :, 2 * p + 1, NOPE:]], 1) for k in range(KQ)]
        heads += [ukv[:, h, :NOPE] for h in (2 * p, 2 * p + 1)]
    units += [unit(heads[:TPU]), unit(heads[TPU:])]
    t = tiles(w_o)
    units += [unit([t[k, m] for m in (i, i + 1) for k in range(KD)]) for i in range(0, KD, 2)]
    t1, t3, t2 = tiles(f1), tiles(f3), tiles(f2)
    for h in range(2):
        fs = range(HALF_F * h, HALF_F * (h + 1))
        units += [unit([t1[k, f] for k in range(KD)] + [t3[k, f] for k in range(KD)]) for f in fs]
        down = [t2[f, m] for m in range(KD) for f in fs]
        units += [unit(down[i:i + W2_UNIT_TILES]) for i in range(0, len(down), W2_UNIT_TILES)]
    ti, tg = tiles(g_in), tiles(g_gate)
    for b in range(RG_BLOCKS):
        units.append(unit([ti[k, m] for m in (2 * b, 2 * b + 1) for k in range(KD)]))
        units.append(unit([tg[k, m] for m in (2 * b, 2 * b + 1) for k in range(KD)]))
        units.append(unit([tiles(w[d, b])[k, m] for d in range(2) for m in range(2) for w in (w_a, w_x)
                           for k in range(2)]))
    t = tiles(g_out)
    units += [unit([t[k, m] for m in (i, i + 1) for k in range(KD)]) for i in range(0, KD, 2)]
    return np.stack(units)


def expert_units(w1, w3, w2):
    def up(w):
        return (w.reshape(N_EXP, 2, 4, P, NJ, FB).transpose(0, 4, 1, 3, 2, 5)).reshape(N_EXP, NJ, 2, P, UW)
    a, b = up(w1), up(w3)
    d = w2.reshape(N_EXP, NJ, 2, 2, P, D).transpose(0, 1, 2, 4, 3, 5).reshape(N_EXP, NJ, 2, P, UW)
    out = np.empty((N_EXP, EXP_UNITS, P, UW), np.float32)
    out[:, 0:2], out[:, 2:4] = a[:, 0], b[:, 0]
    for j in range(1, NJ):
        u = 4 + 6 * (j - 1)
        out[:, u:u + 2], out[:, u + 2:u + 4], out[:, u + 4:u + 6] = a[:, j], b[:, j], d[:, j - 1]
    out[:, EXP_UNITS - 2:] = d[:, NJ - 1]
    return out.reshape(N_EXP * EXP_UNITS, P, UW)


def constants():
    c = np.zeros((P, N_CONST), np.float32)
    i = np.arange(P)
    c[:, C_ID:C_ID + P] = np.eye(P)
    swap = i ^ 32
    c[swap, C_PERM + i] = 1.0
    c[:, C_ONE:C_ONE + P] = 1.0
    c[:, C_TRI:C_TRI + P] = i[:, None] < i[None, :]
    c[:, C_IOTA:C_IOTA + P] = i[None, :]
    n_freq = ROPE // 4
    inv = (np.float32(ROPE_BASE) ** (-np.arange(n_freq, dtype=np.float32) / np.float32(n_freq))).astype(np.float32)
    t = np.arange(NL_TOK)
    row, col = (t // GRID_W).astype(np.float32), (t % GRID_W).astype(np.float32)
    ang = np.concatenate([row[:, None] * inv, col[:, None] * inv], 1).astype(np.float32)
    cos, sin = np.cos(ang).T, np.sin(ang).T
    c[:, C_COS:C_COS + NC_TOK] = 1.0
    c[:, C_COS + NC_TOK:C_COS + T] = np.tile(cos, (4, 1))
    c[:, C_SIN + NC_TOK:C_SIN + T] = np.concatenate([-sin, sin, -sin, sin], 0)
    return c


def columns(v):
    return np.ascontiguousarray(v.reshape(-1, P).T)


def kernel(**inputs):
    import concourse.bacc as bacc
    from concourse.bass_utils import run_bass_kernel_spmd

    a = {k: np.asarray(v) for k, v in inputs.items()}
    xs = np.concatenate([a["ctx"][0], a["x"][0]], 0)
    x_t = np.ascontiguousarray(xs.T.reshape(KD, P, T))
    par = np.concatenate([
        np.stack([columns(a["c_ctx"]), columns(a["c"][0])], -1).reshape(P, 16),
        columns(a["ada_b"]), columns(a["norm1_g"]), columns(a["norm2_g"]),
        columns(a["mla_g_q"][0]), columns(a["mla_g_kv"][0]),
        columns(a["mla_g_qn"][0, :NOPE]), columns(a["mla_g_kn"][0, :NOPE]),
        columns(np.tile(a["mla_g_qn"][0, NOPE:], 2)), columns(np.tile(a["mla_g_kn"][0, NOPE:], 2)),
        columns(a["rg_conv_w"][0]), columns(a["rg_conv_b"][0]), columns(a["rg_b_a"][0]), columns(a["rg_b_x"][0]),
        columns(a["rg_lam"][0]),
        a["moe_w_router"][0].reshape(KD, P, N_EXP).transpose(1, 0, 2).reshape(P, KD * N_EXP)], 1)
    ada_w = np.ascontiguousarray(a["ada_w"].reshape(2, 2, 4, P, 12, 512).transpose(0, 4, 1, 3, 2, 5)).reshape(
        2 * ADA_GROUPS, P, UW)
    w_units = weight_units(a["mla_w_dq"][0], a["mla_w_uq"][0], a["mla_w_dkv"][0], a["mla_w_ukv"][0],
                           a["mla_w_o"][0], a["ffn_w1"][0], a["ffn_w3"][0], a["ffn_w2"][0], a["rg_w_in"][0],
                           a["rg_w_gate"][0], a["rg_w_a"][0], a["rg_w_x"][0], a["rg_w_out"][0])
    moe_w = expert_units(a["moe_w1"][0], a["moe_w3"][0], a["moe_w2"][0])
    arrays = {"x_t": x_t, "consts": constants(), "params": np.ascontiguousarray(par), "ada_w": ada_w,
              "w_units": w_units, "moe_w": moe_w}
    nc = bacc.Bacc("TRN2", target_bir_lowering=False, num_devices=1)
    aps = {k: nc.dram_tensor(k, v.shape, mybir.dt.from_np(v.dtype), kind="ExternalInput").ap()
           for k, v in arrays.items()}
    out = nc.dram_tensor("out", [KD, P, NL_TOK], F32, kind="ExternalOutput").ap()
    dit_kernel(nc, *(aps[k] for k in ("x_t", "consts", "params", "ada_w", "w_units", "moe_w")), out)
    r = run_bass_kernel_spmd(nc, [arrays], core_ids=[0])
    got = r.results[0]["out"]
    return np.ascontiguousarray(got.transpose(2, 0, 1).reshape(1, NL_TOK, D))
```
